# Optimizing a Trainium2 kernel written in Bass

```python
import math
import jax, jax.numpy as jnp
from jax import lax
import numpy as np

D_MODEL = 1024
BATCH = 1
SEQ = 256
DEPTH = 4

CHUNK = 64
N_MIXERS = 3
NORM_EPS = 1e-6
N_SUBLAYER_NORMS = 6

HG_EXPAND = 128
HG_HEADS = D_MODEL // HG_EXPAND
HG_F_DIM = HG_HEADS * HG_EXPAND
HG_V_DIM = D_MODEL // HG_HEADS
HG_BLOCK = 16
HG_MID = HG_BLOCK // 2

DA_HEAD_DIM = 64
DA_HEADS = D_MODEL // (2 * DA_HEAD_DIM)
DA_Q_BLOCK = 128

POOL_WINDOWS = (2, 4, 8, 16)
POOL_GROUPS = len(POOL_WINDOWS)
POOL_GROUP_DIM = D_MODEL // POOL_GROUPS

D_FF = 2816

N_A = (DEPTH + 2) // 3
N_B = (DEPTH + 1) // 3
N_C = DEPTH // 3


def rmsnorm(x, w):
    xf = x.astype(jnp.float32)
    y = xf * lax.rsqrt(jnp.mean(xf * xf, axis=-1, keepdims=True) + NORM_EPS)
    return (y * w.astype(jnp.float32)).astype(x.dtype)

def swiglu(x, w_in, w_out):
    g, u = jnp.split(x @ w_in, 2, axis=-1)
    return (jax.nn.silu(g) * u) @ w_out

def alibi_slopes(n_heads):
    return jnp.exp2(-8.0 * jnp.arange(1, n_heads + 1, dtype=jnp.float32) / n_heads)

def hgrn_lower_bound(lb_raw, layer):
    p = jax.nn.softmax(lb_raw.astype(jnp.float32), axis=0)
    return jnp.cumsum(p, axis=0)[layer] - p[0]

def hgrn2_mixer(x, w_in, gnorm_w, w_out, lb):
    f32 = jnp.float32
    B, S, _ = x.shape
    nb = S // HG_BLOCK
    q, f_pre, i_in, g = jnp.split(
        x @ w_in, [HG_F_DIM, 2 * HG_F_DIM, 2 * HG_F_DIM + D_MODEL], axis=-1)
    f = lb + (1.0 - lb) * jax.nn.sigmoid(f_pre.astype(f32))
    k = 1.0 - f
    log_f = jnp.log(f)

    def heads(t, dim):
        return t.reshape(B, nb, HG_BLOCK, HG_HEADS, dim).transpose(0, 3, 1, 2, 4)

    qh = heads(q.astype(f32), HG_EXPAND)
    kh = heads(k, HG_EXPAND)
    vh = heads(i_in.astype(f32), HG_V_DIM)
    b = jnp.cumsum(heads(log_f, HG_EXPAND), axis=3)
    b_last = b[:, :, :, -1:, :]
    b_mid = b[:, :, :, HG_MID:HG_MID + 1, :]

    q_r = qh * jnp.exp(b - b_mid)
    k_r = kh * jnp.exp(b_mid - b)
    causal = jnp.tril(jnp.ones((HG_BLOCK, HG_BLOCK), dtype=bool))
    a = jnp.where(causal, jnp.einsum('bhntk,bhnsk->bhnts', q_r, k_r), 0.0)
    o_intra = jnp.einsum('bhnts,bhnsv->bhntv', a, vh)

    q_inter = qh * jnp.exp(b)
    k_state = kh * jnp.exp(b_last - b)
    decay = jnp.exp(b_last[:, :, :, 0, :])

    def step(state, xs):
        qi, ks, vs, dec = xs
        o = jnp.einsum('bhtk,bhkv->bhtv', qi, state)
        state = state * dec[..., None] + jnp.einsum('bhtk,bhtv->bhkv', ks, vs)
        return state, o

    xs = (jnp.moveaxis(q_inter, 2, 0), jnp.moveaxis(k_state, 2, 0),
          jnp.moveaxis(vh, 2, 0), jnp.moveaxis(decay, 2, 0))
    s0 = jnp.zeros((B, HG_HEADS, HG_EXPAND, HG_V_DIM), f32)
    _, o_inter = lax.scan(step, s0, xs)

    o = o_intra + jnp.moveaxis(o_inter, 0, 2)
    o = o.transpose(0, 2, 3, 1, 4).reshape(B, S, HG_HEADS, HG_V_DIM)
    gate = jax.nn.silu(g.astype(f32).reshape(B, S, HG_HEADS, HG_V_DIM))
    o = rmsnorm(o, gnorm_w) * gate
    return o.reshape(B, S, D_MODEL).astype(x.dtype) @ w_out

def diff_attention(x, w_in, lam, subln_w, w_out, layer):
    f32 = jnp.float32
    B, S, _ = x.shape
    H, dh = DA_HEADS, DA_HEAD_DIM
    q, k, v = jnp.split(x @ w_in, 3, axis=-1)
    q = q.reshape(B, S, H, 2, dh).transpose(0, 2, 3, 1, 4)
    k = k.reshape(B, S, H, 2, dh).transpose(0, 2, 3, 1, 4)
    v = v.reshape(B, S, H, 2 * dh).transpose(0, 2, 1, 3)

    lam_init = 0.8 - 0.6 * math.exp(-0.3 * layer)
    lam_f = lam.astype(f32)
    lam_full = (jnp.exp(jnp.sum(lam_f[0] * lam_f[1]))
                - jnp.exp(jnp.sum(lam_f[2] * lam_f[3])) + lam_init)
    slopes = alibi_slopes(H)
    scale = dh ** -0.5
    n_qb = S // DA_Q_BLOCK
    q_blocks = q.reshape(B, H, 2, n_qb, DA_Q_BLOCK, dh).transpose(3, 0, 1, 2, 4, 5)
    key_pos = jnp.arange(S)

    def block(args):
        qb, start = args
        q_pos = start + jnp.arange(DA_Q_BLOCK)
        s = jnp.einsum('bhgqd,bhgkd->bhgqk', qb, k).astype(f32) * scale
        dist = jnp.abs(q_pos[:, None] - key_pos[None, :]).astype(f32)
        allowed = (key_pos[None, :] // CHUNK) <= (q_pos[:, None] // CHUNK)
        s = s - slopes[None, :, None, None, None] * dist
        p = jax.nn.softmax(jnp.where(allowed, s, -jnp.inf), axis=-1)
        w = p[:, :, 0] - lam_full * p[:, :, 1]
        return jnp.einsum('bhqk,bhkv->bhqv', w.astype(v.dtype), v)

    starts = jnp.arange(n_qb, dtype=jnp.int32) * DA_Q_BLOCK
    o = lax.map(block, (q_blocks, starts))
    o = o.transpose(1, 0, 3, 2, 4).reshape(B, S, H, 2 * dh)
    o = rmsnorm(o, subln_w) * (1.0 - lam_init)
    return o.reshape(B, S, D_MODEL) @ w_out

def pool_mixer(x, w_in, w_group, scale, w_out):
    f32 = jnp.float32
    B, S, _ = x.shape
    u = (x @ w_in).astype(f32).reshape(B, S, POOL_GROUPS, POOL_GROUP_DIM)
    csum = jnp.cumsum(u, axis=1)
    count_pos = jnp.arange(S)
    outs = []
    for g_idx, w in enumerate(POOL_WINDOWS):
        cs = csum[:, :, g_idx]
        lag = jnp.pad(cs[:, :S - w], ((0, 0), (w, 0), (0, 0)))
        count = jnp.minimum(count_pos + 1, w).astype(f32)
        mean = (cs - lag) / count[None, :, None]
        outs.append(mean - u[:, :, g_idx])
    p = jnp.stack(outs, axis=2)
    y = jnp.einsum('bsgc,gcd->bsgd', p, w_group.astype(f32))
    y = y * scale.astype(f32).reshape(POOL_GROUPS, POOL_GROUP_DIM)
    return y.reshape(B, S, D_MODEL).astype(x.dtype) @ w_out

def first_inputs(seed: int = 0) -> dict:
    key = jax.random.key(seed)
    ks = jax.random.split(key, 18)
    f32 = jnp.float32

    def dense(k, shape, fan_in):
        return jax.random.normal(k, shape, f32) * fan_in ** -0.5

    def gain(k, shape, s=0.05):
        return 1.0 + s * jax.random.normal(k, shape, f32)

    G, C = POOL_GROUPS, POOL_GROUP_DIM
    return {
        "x": jax.random.normal(ks[0], (BATCH, SEQ, D_MODEL), f32),
        "norm_gains": gain(ks[1], (DEPTH, N_SUBLAYER_NORMS, D_MODEL)),
        "ffn1_w_in": dense(ks[2], (DEPTH, D_MODEL, 2 * D_FF), D_MODEL),
        "ffn1_w_out": dense(ks[3], (DEPTH, D_FF, D_MODEL), D_FF),
        "ffn2_w_in": dense(ks[4], (DEPTH, D_MODEL, 2 * D_FF), D_MODEL),
        "ffn2_w_out": dense(ks[5], (DEPTH, D_FF, D_MODEL), D_FF),
        "hgrn_w_in": dense(ks[6], (N_A, D_MODEL, 2 * HG_F_DIM + 2 * D_MODEL), D_MODEL),
        "hgrn_gnorm": gain(ks[7], (N_A, HG_V_DIM)),
        "hgrn_w_out": dense(ks[8], (N_A, D_MODEL, D_MODEL), D_MODEL),
        "hgrn_lb_raw": 0.5 * jax.random.normal(ks[9], (DEPTH, HG_F_DIM), f32),
        "diff_w_in": dense(ks[10], (N_B, D_MODEL, 3 * D_MODEL), D_MODEL),
        "diff_lambda": 0.1 * jax.random.normal(ks[11], (N_B, 4, DA_HEAD_DIM), f32),
        "diff_subln": gain(ks[12], (N_B, 2 * DA_HEAD_DIM)),
        "diff_w_out": dense(ks[13], (N_B, D_MODEL, D_MODEL), D_MODEL),
        "pool_w_in": dense(ks[14], (N_C, D_MODEL, D_MODEL), D_MODEL),
        "pool_w_group": dense(ks[15], (N_C, G, C, C), C),
        "pool_scale": gain(ks[16], (N_C, D_MODEL), 0.1),
        "pool_w_out": dense(ks[17], (N_C, D_MODEL, D_MODEL), D_MODEL),
    }

def first_block(x, norm_gains, ffn1_w_in, ffn1_w_out, ffn2_w_in, ffn2_w_out,
              hgrn_w_in, hgrn_gnorm, hgrn_w_out, hgrn_lb_raw,
              diff_w_in, diff_lambda, diff_subln, diff_w_out,
              pool_w_in, pool_w_group, pool_scale, pool_w_out):
    h = x
    for i in range(DEPTH):
        kind, j = i % N_MIXERS, i // N_MIXERS
        gn = norm_gains[i]
        h = h + 0.5 * rmsnorm(swiglu(rmsnorm(h, gn[0]), ffn1_w_in[i], ffn1_w_out[i]), gn[1])
        hn = rmsnorm(h, gn[2])
        if kind == 0:
            lb = hgrn_lower_bound(hgrn_lb_raw, i)
            m = hgrn2_mixer(hn, hgrn_w_in[j], hgrn_gnorm[j], hgrn_w_out[j], lb)
        elif kind == 1:
            m = diff_attention(hn, diff_w_in[j], diff_lambda[j], diff_subln[j], diff_w_out[j], i)
        else:
            m = pool_mixer(hn, pool_w_in[j], pool_w_group[j], pool_scale[j], pool_w_out[j])
        h = h + rmsnorm(m, gn[3])
        h = h + 0.5 * rmsnorm(swiglu(rmsnorm(h, gn[4]), ffn2_w_in[i], ffn2_w_out[i]), gn[5])
    return h


DEPTH_2 = 2

N_HYB = (DEPTH_2 + 1) // 2
N_REC = DEPTH_2 // 2
CONV_K = 4
D_SSM = D_MODEL
SSM_HEAD_DIM = 64
SSM_HEADS = D_SSM // SSM_HEAD_DIM
SSM_GROUPS = 2
SSM_STATE = 128
SSM_CONV_DIM = D_SSM + 2 * SSM_GROUPS * SSM_STATE
SSD_CHUNK = 128
FOX_HEAD_DIM = 128
FOX_HEADS = 8
D_FOX = FOX_HEADS * FOX_HEAD_DIM
Q_BLOCK = 128
HYB_IN = D_SSM + SSM_CONV_DIM + SSM_HEADS + 3 * D_FOX + FOX_HEADS
D_RNN = D_MODEL
RNN_BLOCKS = 8
RNN_BLOCK = D_RNN // RNN_BLOCKS
RG_LRU_C = 8.0


def rms_norm(x, g):
    xf = x.astype(jnp.float32)
    y = xf * lax.rsqrt(jnp.mean(xf * xf, axis=-1, keepdims=True) + NORM_EPS)
    return (y * g.astype(jnp.float32)).astype(x.dtype)

def swiglu_2(x, w_in, w_out):
    gate, up = jnp.split(x @ w_in, 2, axis=-1)
    return (jax.nn.silu(gate) * up) @ w_out

def causal_conv(x, w, bias):
    s = x.shape[1]
    kw = w.shape[0]
    xp = jnp.pad(x, ((0, 0), (kw - 1, 0), (0, 0)))
    y = xp[:, 0:s] * w[0]
    for k in range(1, kw):
        y = y + xp[:, k:k + s] * w[k]
    return y + bias

def ssd_chunked(xh, dt, a, bm, cm):
    b, s, nh, p = xh.shape
    g, n = bm.shape[-2:]
    kh = nh // g
    c = s // SSD_CHUNK
    X = (xh.astype(jnp.float32) * dt[..., None]).reshape(b, c, SSD_CHUNK, g, kh, p)
    Bc = bm.astype(jnp.float32).reshape(b, c, SSD_CHUNK, g, n)
    Cc = cm.astype(jnp.float32).reshape(b, c, SSD_CHUNK, g, n)
    dA = (dt * a).reshape(b, c, SSD_CHUNK, g, kh).transpose(0, 3, 4, 1, 2)
    a_cs = jnp.cumsum(dA, axis=-1)
    causal = jnp.tril(jnp.ones((SSD_CHUNK, SSD_CHUNK), dtype=bool))
    seg = a_cs[..., :, None] - a_cs[..., None, :]
    L = jnp.exp(jnp.where(causal, seg, -jnp.inf))
    cb = jnp.einsum("bclgn,bcsgn->bgcls", Cc, Bc)
    y_diag = jnp.einsum("bgkcls,bcsgkp->bclgkp", L * cb[:, :, None], X)
    decay_states = jnp.exp(a_cs[..., -1:] - a_cs)
    states = jnp.einsum("bclgn,bgkcl,bclgkp->bcgkpn", Bc, decay_states, X)
    chunk_tot = a_cs[..., -1]
    chunk_cs = jnp.cumsum(chunk_tot, axis=-1)
    cs_prev = chunk_cs - chunk_tot
    seg_c = cs_prev[..., :, None] - chunk_cs[..., None, :]
    strict = jnp.tril(jnp.ones((c, c), dtype=bool), k=-1)
    decay_chunk = jnp.exp(jnp.where(strict, seg_c, -jnp.inf))
    init_states = jnp.einsum("bgkzc,bcgkpn->bzgkpn", decay_chunk, states)
    state_decay_out = jnp.exp(a_cs)
    y_off = jnp.einsum("bclgn,bcgkpn,bgkcl->bclgkp", Cc, init_states, state_decay_out)
    return (y_diag + y_off).reshape(b, s, nh, p)

def forgetting_attention(q, k, v, log_f):
    b, s, h, d = q.shape
    nblk = s // Q_BLOCK
    cum = jnp.cumsum(log_f, axis=1).transpose(0, 2, 1)
    qb = q.reshape(b, nblk, Q_BLOCK, h, d).transpose(1, 0, 2, 3, 4)
    cqb = cum.reshape(b, h, nblk, Q_BLOCK).transpose(2, 0, 1, 3)
    kpos = jnp.arange(s)
    scale = d ** -0.5

    def block(args):
        qi, ci, i = args
        logits = jnp.einsum("bqhd,bkhd->bhqk", qi, k).astype(jnp.float32) * scale
        logits = logits + ci[..., :, None] - cum[:, :, None, :]
        qpos = i * Q_BLOCK + jnp.arange(Q_BLOCK)
        mask = kpos[None, :] <= qpos[:, None]
        probs = jax.nn.softmax(jnp.where(mask, logits, -jnp.inf), axis=-1)
        return jnp.einsum("bhqk,bkhd->bqhd", probs.astype(v.dtype), v)

    out = lax.map(block, (qb, cqb, jnp.arange(nblk)))
    return out.transpose(1, 0, 2, 3, 4).reshape(b, s, h, d)

def hybrid_mixer(h, w_in, conv_w, conv_b, dt_bias, a_log, d_skip, ssm_norm_g, fox_b_f, w_out):
    b, s, _ = h.shape
    sizes = (D_SSM, SSM_CONV_DIM, SSM_HEADS, D_FOX, D_FOX, D_FOX)
    offs = np.cumsum(sizes).tolist()
    z, xbc, dt_raw, q, k, v, f_raw = jnp.split(h @ w_in, offs, axis=-1)
    xbc = jax.nn.silu(causal_conv(xbc, conv_w, conv_b))
    xs, bm, cm = jnp.split(xbc, [D_SSM, D_SSM + SSM_GROUPS * SSM_STATE], axis=-1)
    xh = xs.reshape(b, s, SSM_HEADS, SSM_HEAD_DIM)
    dt = jax.nn.softplus(dt_raw.astype(jnp.float32) + dt_bias.astype(jnp.float32))
    a = -jnp.exp(a_log.astype(jnp.float32))
    y = ssd_chunked(xh, dt, a,
                    bm.reshape(b, s, SSM_GROUPS, SSM_STATE),
                    cm.reshape(b, s, SSM_GROUPS, SSM_STATE))
    y = y + d_skip.astype(jnp.float32)[:, None] * xh.astype(jnp.float32)
    y = y.reshape(b, s, D_SSM) * jax.nn.silu(z.astype(jnp.float32))
    yg = y.reshape(b, s, SSM_GROUPS, D_SSM // SSM_GROUPS)
    yg = yg * lax.rsqrt(jnp.mean(yg * yg, axis=-1, keepdims=True) + NORM_EPS)
    y_ssm = (yg.reshape(b, s, D_SSM) * ssm_norm_g.astype(jnp.float32)).astype(h.dtype)
    log_f = jax.nn.log_sigmoid(f_raw.astype(jnp.float32) + fox_b_f.astype(jnp.float32))
    o = forgetting_attention(q.reshape(b, s, FOX_HEADS, FOX_HEAD_DIM),
                             k.reshape(b, s, FOX_HEADS, FOX_HEAD_DIM),
                             v.reshape(b, s, FOX_HEADS, FOX_HEAD_DIM), log_f)
    o = o.reshape(b, s, D_FOX).astype(h.dtype)
    return jnp.concatenate([y_ssm, o], axis=-1) @ w_out

def rg_lru(x, w_a, b_a, w_x, b_x, lam):
    b, s, d = x.shape
    xb = x.reshape(b, s, RNN_BLOCKS, RNN_BLOCK)
    r = jax.nn.sigmoid((jnp.einsum("bsnj,njk->bsnk", xb, w_a).reshape(b, s, d) + b_a).astype(jnp.float32))
    i = jax.nn.sigmoid((jnp.einsum("bsnj,njk->bsnk", xb, w_x).reshape(b, s, d) + b_x).astype(jnp.float32))
    log_a = RG_LRU_C * r * jax.nn.log_sigmoid(lam.astype(jnp.float32))
    a = jnp.exp(log_a)
    u = jnp.sqrt(-jnp.expm1(2.0 * log_a)) * (i * x.astype(jnp.float32))

    def combine(left, right):
        a1, b1 = left
        a2, b2 = right
        return a1 * a2, a2 * b1 + b2

    _, hs = lax.associative_scan(combine, (a, u), axis=1)
    return hs.astype(x.dtype)

def recurrent_mixer(h, w_in, conv_w, conv_b, w_a, b_a, w_x, b_x, lam, w_out):
    gate, xr = jnp.split(h @ w_in, 2, axis=-1)
    gate = jax.nn.gelu(gate, approximate=True)
    xr = causal_conv(xr, conv_w, conv_b)
    return (rg_lru(xr, w_a, b_a, w_x, b_x, lam) * gate) @ w_out

def second_inputs(seed: int = 0) -> dict:
    key = jax.random.key(seed)
    ks = jax.random.split(key, 24)
    f32 = jnp.float32

    def nrm(k, shape, scale):
        return jax.random.normal(k, shape, f32) * scale

    def unif(k, shape, lo, hi):
        return jax.random.uniform(k, shape, f32, lo, hi)

    x = nrm(ks[0], (BATCH, SEQ, D_MODEL), 1.0)
    norm_g = 1.0 + nrm(ks[1], (DEPTH_2, 6, D_MODEL), 0.05)
    ffn_w_in = nrm(ks[2], (DEPTH_2, 2, D_MODEL, 2 * D_FF), D_MODEL ** -0.5)
    ffn_w_out = nrm(ks[3], (DEPTH_2, 2, D_FF, D_MODEL), D_FF ** -0.5)
    hyb_w_in = nrm(ks[4], (N_HYB, D_MODEL, HYB_IN), D_MODEL ** -0.5)
    ssm_conv_w = nrm(ks[5], (N_HYB, CONV_K, SSM_CONV_DIM), CONV_K ** -0.5)
    ssm_conv_b = nrm(ks[6], (N_HYB, SSM_CONV_DIM), 0.02)
    dt0 = jnp.exp(unif(ks[7], (N_HYB, SSM_HEADS), math.log(1e-3), math.log(1e-1)))
    ssm_dt_bias = dt0 + jnp.log(-jnp.expm1(-dt0))
    ssm_a_log = jnp.log(unif(ks[8], (N_HYB, SSM_HEADS), 1.0, 16.0))
    ssm_d = 1.0 + nrm(ks[9], (N_HYB, SSM_HEADS), 0.1)
    ssm_norm_g = 1.0 + nrm(ks[10], (N_HYB, D_SSM), 0.05)
    fox_b_f = unif(ks[11], (N_HYB, FOX_HEADS), 1.0, 4.0)
    hyb_w_out = nrm(ks[12], (N_HYB, D_SSM + D_FOX, D_MODEL), (D_SSM + D_FOX) ** -0.5)
    rec_w_in = nrm(ks[13], (N_REC, D_MODEL, 2 * D_RNN), D_MODEL ** -0.5)
    rec_conv_w = nrm(ks[14], (N_REC, CONV_K, D_RNN), CONV_K ** -0.5)
    rec_conv_b = nrm(ks[15], (N_REC, D_RNN), 0.02)
    rec_w_a = nrm(ks[16], (N_REC, RNN_BLOCKS, RNN_BLOCK, RNN_BLOCK), RNN_BLOCK ** -0.5)
    rec_b_a = nrm(ks[17], (N_REC, D_RNN), 0.02)
    rec_w_x = nrm(ks[18], (N_REC, RNN_BLOCKS, RNN_BLOCK, RNN_BLOCK), RNN_BLOCK ** -0.5)
    rec_b_x = nrm(ks[19], (N_REC, D_RNN), 0.02)
    a0 = unif(ks[20], (N_REC, D_RNN), 0.9, 0.999)
    s0 = a0 ** (1.0 / RG_LRU_C)
    rec_lambda = jnp.log(s0) - jnp.log1p(-s0)
    rec_w_out = nrm(ks[21], (N_REC, D_RNN, D_MODEL), D_RNN ** -0.5)
    return {"x": x, "norm_g": norm_g, "ffn_w_in": ffn_w_in, "ffn_w_out": ffn_w_out,
            "hyb_w_in": hyb_w_in, "ssm_conv_w": ssm_conv_w, "ssm_conv_b": ssm_conv_b,
            "ssm_dt_bias": ssm_dt_bias, "ssm_a_log": ssm_a_log, "ssm_d": ssm_d,
            "ssm_norm_g": ssm_norm_g, "fox_b_f": fox_b_f, "hyb_w_out": hyb_w_out,
            "rec_w_in": rec_w_in, "rec_conv_w": rec_conv_w, "rec_conv_b": rec_conv_b,
            "rec_w_a": rec_w_a, "rec_b_a": rec_b_a, "rec_w_x": rec_w_x, "rec_b_x": rec_b_x,
            "rec_lambda": rec_lambda, "rec_w_out": rec_w_out}

def second_block(x, norm_g, ffn_w_in, ffn_w_out, hyb_w_in, ssm_conv_w, ssm_conv_b, ssm_dt_bias,
              ssm_a_log, ssm_d, ssm_norm_g, fox_b_f, hyb_w_out, rec_w_in, rec_conv_w, rec_conv_b,
              rec_w_a, rec_b_a, rec_w_x, rec_b_x, rec_lambda, rec_w_out):
    for layer in range(DEPTH_2):
        g = norm_g[layer]
        h = swiglu_2(rms_norm(x, g[0]), ffn_w_in[layer, 0], ffn_w_out[layer, 0])
        x = x + 0.5 * rms_norm(h, g[1])
        h = rms_norm(x, g[2])
        if layer % 2 == 0:
            i = layer // 2
            h = hybrid_mixer(h, hyb_w_in[i], ssm_conv_w[i], ssm_conv_b[i], ssm_dt_bias[i],
                             ssm_a_log[i], ssm_d[i], ssm_norm_g[i], fox_b_f[i], hyb_w_out[i])
        else:
            j = layer // 2
            h = recurrent_mixer(h, rec_w_in[j], rec_conv_w[j], rec_conv_b[j], rec_w_a[j], rec_b_a[j],
                                rec_w_x[j], rec_b_x[j], rec_lambda[j], rec_w_out[j])
        x = x + rms_norm(h, g[3])
        h = swiglu_2(rms_norm(x, g[4]), ffn_w_in[layer, 1], ffn_w_out[layer, 1])
        x = x + 0.5 * rms_norm(h, g[5])
    return x


def setup_inputs(seed=0):
    out = dict(first_inputs(seed))
    for name, value in second_inputs(seed + 1).items():
        if name != "x":
            out[name + "_2"] = value
    return out


def reference(
    x, norm_gains, ffn1_w_in, ffn1_w_out, ffn2_w_in, ffn2_w_out, hgrn_w_in, hgrn_gnorm,
    hgrn_w_out, hgrn_lb_raw, diff_w_in, diff_lambda, diff_subln, diff_w_out, pool_w_in,
    pool_w_group, pool_scale, pool_w_out, norm_g_2, ffn_w_in_2, ffn_w_out_2, hyb_w_in_2,
    ssm_conv_w_2, ssm_conv_b_2, ssm_dt_bias_2, ssm_a_log_2, ssm_d_2, ssm_norm_g_2, fox_b_f_2,
    hyb_w_out_2, rec_w_in_2, rec_conv_w_2, rec_conv_b_2, rec_w_a_2, rec_b_a_2, rec_w_x_2,
    rec_b_x_2, rec_lambda_2, rec_w_out_2,
):
    x = first_block(
        x, norm_gains, ffn1_w_in, ffn1_w_out, ffn2_w_in, ffn2_w_out, hgrn_w_in, hgrn_gnorm,
        hgrn_w_out, hgrn_lb_raw, diff_w_in, diff_lambda, diff_subln, diff_w_out, pool_w_in,
        pool_w_group, pool_scale, pool_w_out,
    )
    return second_block(
        x, norm_g_2, ffn_w_in_2, ffn_w_out_2, hyb_w_in_2, ssm_conv_w_2, ssm_conv_b_2,
        ssm_dt_bias_2, ssm_a_log_2, ssm_d_2, ssm_norm_g_2, fox_b_f_2, hyb_w_out_2, rec_w_in_2,
        rec_conv_w_2, rec_conv_b_2, rec_w_a_2, rec_b_a_2, rec_w_x_2, rec_b_x_2, rec_lambda_2,
        rec_w_out_2,
    )


_drawn_inputs = setup_inputs


def setup_inputs(seed=0):
    import zlib

    import numpy as np

    out = dict(_drawn_inputs(seed))
    spreads = {}
    factors = {'ssm_conv_b_2': 5.172,
     'ssm_d_2': 2.833,
     'ssm_norm_g_2': 10.138,
     'rec_b_a_2': 46.761,
     'rec_b_x_2': 21.878,
     'fox_b_f_2': 2.829}
    for name, (base, spread) in spreads.items():
        noise = np.random.default_rng([zlib.crc32(name.encode()), seed]).standard_normal(out[name].shape)
        drawn = base * np.exp(spread * noise) if base else spread * noise
        out[name] = __import__('jax').numpy.asarray(drawn.astype(out[name].dtype))
    for name, factor in factors.items():
        out[name] = (out[name] * factor).astype(out[name].dtype)
    return out
```

```python
import math
from contextlib import ExitStack

import numpy as np

import concourse.bass as bass
import concourse.mybir as mybir
from concourse.alu_op_type import AluOpType as ALU

F32 = mybir.dt.float32
F32R = mybir.dt.float32r
I32 = mybir.dt.int32
ACT = mybir.ActivationFunctionType
AX_X = mybir.AxisListType.X

P = 128
T = 256
TT = T // P
D = 1024
KD = D // P
FF = 2816
KF = FF // P
PC = 256
KH = KF // 2
EPS = 1e-6
SSM_H = 16
HGB = 16
NB = T // HGB
BIG = 1e30

VEC_GAIN1, VEC_GAIN2 = 0, 24
VEC_LB = 36
VEC_POOL_SCALE, VEC_SSM_NORM = 40, 41
VEC_REC_CONV_W, VEC_REC_CONV_B, VEC_REC_BA, VEC_REC_BX, VEC_REC_LAM = 42, 46, 47, 48, 49
VEC_SSM_CONV_X, VEC_SSM_CONV_BX = 50, 54
VEC_SSM_CONV_BC, VEC_SSM_CONV_BBC = 55, 59
VEC_GNORM, VEC_SUBLN, VEC_DT_BIAS, VEC_A_LOG, VEC_FOX_B = 60, 62, 63, 64, 65
NVEC = 66
N_TABLE_LOADS = 19
FOX_ROW = 120

FFN, HGRN, DIFF, POOL, HYB, REC = "ffn", "hgrn", "diff", "pool", "hyb", "rec"


class Segment:

    def __init__(self, role, kt, bodies, source, width=PC):
        self.role, self.kt, self.bodies, self.source, self.width = role, kt, bodies, source, width


def columns(w, first=0):
    def source(i, slot):
        return w[:, bass.ds(first + (2 * i + slot) * PC, PC)].rearrange("(k p) c -> p k c", p=P)
    return source


def gate_and_up(w):
    def source(i, slot):
        return w[:, bass.ds(slot * FF + i * PC, PC)].rearrange("(k p) c -> p k c", p=P)
    return source


def row_halves(w, rows):
    def source(i, slot):
        return w[slot * rows:(slot + 1) * rows, bass.ds(i * PC, PC)].rearrange("(k p) c -> p k c", p=P)
    return source


def build(nc, a, out):
    def ffn(w_in, w_out, gain):
        return dict(kind=FFN, gain=gain, segs=[
            Segment("ffn", KD, FF // PC, gate_and_up(w_in)),
            Segment("down", KH, D // PC, row_halves(w_out, FF // 2))])

    def out_proj(w):
        return Segment("out", KD, D // PC // 2, columns(w))

    subs = []
    for l in range(4):
        g = VEC_GAIN1 + 6 * l
        subs.append(ffn(a["ffn1_w_in"][l], a["ffn1_w_out"][l], g))
        if l % 3 == 0:
            j = l // 3
            subs.append(dict(kind=HGRN, gain=g + 2, layer=l, j=j, segs=[
                Segment("proj", KD, 4 * D // (2 * PC), columns(a["hgrn_w_in"][j])), out_proj(a["hgrn_w_out"][j])]))
        elif l == 1:
            subs.append(dict(kind=DIFF, gain=g + 2, layer=l, segs=[
                Segment("proj", KD, 3 * D // (2 * PC), columns(a["diff_w_in"][0])), out_proj(a["diff_w_out"][0])]))
        else:
            wg = a["pool_w_group"][0]
            subs.append(dict(kind=POOL, gain=g + 2, segs=[
                Segment("proj", KD, D // (2 * PC), columns(a["pool_w_in"][0])),
                Segment("group", 4, 1, lambda i, slot: wg[2 * slot:2 * slot + 2].rearrange("g (t p) c -> p (g t) c", p=P)),
                out_proj(a["pool_w_out"][0])]))
        subs.append(ffn(a["ffn2_w_in"][l], a["ffn2_w_out"][l], g + 4))
    for l in range(2):
        g = VEC_GAIN2 + 6 * l
        subs.append(ffn(a["ffn_w_in_2"][l, 0], a["ffn_w_out_2"][l, 0], g))
        if l == 0:
            w = a["hyb_w_in_2"][0]
            n_zx, n_qkv = 1024 + 1536, 3 * D
            subs.append(dict(kind=HYB, gain=g + 2, segs=[
                Segment("proj", KD, n_zx // (2 * PC), columns(w)),
                Segment("small", KD, 1, lambda i, slot: w[:, (n_zx, n_zx + 16 + n_qkv + 8 - PC)[slot]:][:, 0:PC].rearrange(
                    "(k p) c -> p k c", p=P)),
                Segment("proj2", KD, n_qkv // (2 * PC), columns(w, n_zx + 16)),
                Segment("down", KD, D // PC, row_halves(a["hyb_w_out_2"][0], D))]))
        else:
            wa, wx = a["rec_w_a_2"][0], a["rec_w_x_2"][0]
            subs.append(dict(kind=REC, gain=g + 2, segs=[
                Segment("proj", KD, 2 * D // (2 * PC), columns(a["rec_w_in_2"][0])),
                Segment("block", KD, 1, lambda i, slot: (wa, wx)[slot].rearrange("n p c -> p n c"), width=P),
                out_proj(a["rec_w_out_2"][0])]))
        subs.append(ffn(a["ffn_w_in_2"][l, 1], a["ffn_w_out_2"][l, 1], g + 4))
    panels = fills = ffns = downs = 0
    turned = head_norms = items = log1ps = hgrns = 0
    flat = []
    for n, s in enumerate(subs):
        s["n"], s["fill"] = n, fills
        fills += {FFN: 1, HYB: 1, HGRN: 2, DIFF: 2, POOL: 3, REC: 3}[s["kind"]]
        s["turn0"], s["hn0"], s["att0"], s["ls0"], s["it"] = turned, head_norms, items, log1ps, hgrns
        turned += {HGRN: 8, HYB: 8, DIFF: 4}.get(s["kind"], 0)
        head_norms += s["kind"] in (HGRN, DIFF)
        items += 16 * (s["kind"] in (DIFF, HYB))
        log1ps += {HYB: 2, REC: 1}.get(s["kind"], 0)
        hgrns += s["kind"] == HGRN
        if s["kind"] == FFN:
            s["ffn"] = ffns
            ffns += 1
        for seg in s["segs"]:
            seg.g0 = panels
            panels += 2 * seg.bodies
            flat.append(seg)
            if seg.role == "down":
                seg.d0 = downs
                downs += seg.bodies
    for seg, nxt in zip(flat, flat[1:] + [None]):
        seg.next = nxt

    ctx = ExitStack()
    with ctx:
        def sb(name, shape, dt=F32):
            return ctx.enter_context(nc.sbuf_tensor(name, shape, dt))

        sems = {}

        def sem(name):
            if name not in sems:
                sems[name] = ctx.enter_context(nc.semaphore(name))
            return sems[name]

        raw = sb("raw", [P, 2, KH * PC])
        whi = sb("whi", [P, 2, KH * PC], F32R)
        wlo = sb("wlo", [P, 2, KH * PC], F32R)
        xs = sb("xs", [P, KD, 2 * T], F32R)
        h = sb("h", [P, KD, T])
        y = sb("y", [P, KD, T])
        corr = sb("corr", [P, 2, 2 * T])
        tsum = sb("tsum", [P, 2, 2 * T])
        gate = sb("gate", [P, 2 * T])
        silu = sb("silu", [P, 2 * T])
        hid = sb("hid", [P, 2 * T])
        rpre = sb("rpre", [P, T])
        rpost = sb("rpost", [P, T])
        rln = sb("rln", [P, T])
        vec = sb("vec", [P, KD, NVEC])
        ones = sb("ones", [P, P])
        ident = sb("ident", [P, P])
        eps = sb("eps", [P, 1])
        MB = 10
        small = sb("small", [P, 8])
        lbw = sb("lbw", [P, KD, 6])
        rec_col = sb("rec_col", [P, 6, KD])
        dist = sb("dist", [P, TT, T])
        causal = sb("causal", [P, TT, T])
        tri = sb("tri", [P, P])
        block_causal = sb("block_causal", [P, P])
        keep = sb("keep", [P, T])
        even_odd = sb("even_odd", [P, 2])
        steps = sb("steps", [P, 16])
        lamrow = sb("lamrow", [P, 4 * 64])
        skiprow = sb("skiprow", [P, SSM_H])
        mix_offset = nc.sbuf_base
        mix = sb("mix", [P, MB, KD, T])
        hs = nc.alloc_sbuf_tensor_at("hs", [P, KF, 2 * T], F32R, offset=mix_offset)
        even_tmp = mix[:, 2, 3, 0:4]
        sq = mix[:, MB - 1]
        upd = mix[:, MB - 2]

        pp = ctx.enter_context(nc.psum_tensor("pp", [P, 4, 2 * T], F32))
        pm = ctx.enter_context(nc.psum_tensor("pm", [P, 4, 2 * T], F32))
        psum_stat = pm[:, 3, 0:T]

        def main_half(slot):
            return pp[:, 2 * slot:2 * slot + 2, 0:T]

        def corr_half(slot):
            return pp[:, 2 * slot:2 * slot + 2, T:2 * T]

        def two(buf):
            return buf.rearrange("p (a t) -> p a t", a=2)

        def seg_loop(eng, seg, body, peel_first=False):
            nxt = 0 if seg.next is None else seg.next.kt * seg.next.width
            mine = seg.kt * seg.width
            first = 1 if peel_first else 0
            last = seg.bodies - (nxt != mine)
            if last <= first:
                for i in range(seg.bodies):
                    body(i, nxt if i == seg.bodies - 1 else mine)
                return
            if peel_first:
                body(0, mine)
            if last - first == 1:
                body(first, mine)
            else:
                with eng.Fori(first, last) as i:
                    body(i, mine)
            if nxt != mine:
                body(seg.bodies - 1, nxt)

        def fill_hi(act, fill, src, gain=None):
            for half in range(2):
                if gain is None:
                    q = slice(4 * half, 4 * half + 4)
                    e = nc.scalar.activation(xs[:, q, 0:T], src[:, q, :], ACT.Copy)
                else:
                    for k in range(4 * half, 4 * half + 4):
                        e = nc.scalar.activation(xs[:, k, 0:T], src[:, k, :], ACT.Copy, scale=vec[:, k, gain:gain + 1])
                e.then_inc(sem("x_hi"), 1)

        def fill_lo(dve, fill, src, gain=None):
            for half in range(2):
                dve.wait_ge(sem("x_hi"), 2 * fill + half + 1)
                if gain is None:
                    q = slice(4 * half, 4 * half + 4)
                    e = nc.vector.tensor_tensor(xs[:, q, T:2 * T], src[:, q, :], xs[:, q, 0:T].bitcast(F32), ALU.subtract)
                else:
                    for k in range(4 * half, 4 * half + 4):
                        e = nc.vector.scalar_tensor_tensor(xs[:, k, T:2 * T], src[:, k, :], vec[:, k, gain:gain + 1],
                                                           xs[:, k, 0:T].bitcast(F32), ALU.mult, ALU.subtract)
                e.then_inc(sem("x_lo"), 1)

        def act_log1p(act, n, e, w, ln):
            act.wait_ge(sem("log1p_negabs"), n + 1)
            nc.scalar.activation(e, e, ACT.Exp).then_inc(sem("log1p_exp"), 1)
            act.wait_ge(sem("log1p_w"), n + 1)
            nc.scalar.activation(ln, w, ACT.Ln).then_inc(sem("log1p_ln"), 1)

        def dve_log1p(dve, n, x, e, w, c, ln):
            v = nc.vector
            v.scalar_tensor_tensor(e, x, -1.0, x, ALU.mult, ALU.min).then_inc(sem("log1p_negabs"), 1)
            dve.wait_ge(sem("log1p_exp"), n + 1)
            v.tensor_scalar(w, e, 1.0, None, ALU.add).then_inc(sem("log1p_w"), 1)
            dve.drain()
            v.tensor_scalar(c, w, -1.0, None, ALU.add)
            dve.drain()
            v.tensor_tensor(c, e, c, ALU.subtract)
            dve.drain()
            v.reciprocal(e, w)
            dve.drain()
            v.tensor_tensor(c, c, e, ALU.mult)
            dve.drain()
            dve.wait_ge(sem("log1p_ln"), n + 1)
            v.tensor_tensor(ln, ln, c, ALU.add)
            dve.drain()

        def flat2(buf):
            return buf.rearrange("p k t -> p (k t)")

        def tok(buf):
            return flat2(buf).rearrange("p (a d) -> p a d", a=TT)

        def act_head_norm(act, n, o, r):
            act.wait_ge(sem("head_out"), n + 1)
            nc.scalar.activation(sq, o, ACT.Square).then_inc(sem("head_squares"), 1)
            act.wait_ge(sem("head_sums"), n + 1)
            nc.scalar.activation(r.rearrange("p (b k) t -> p b (k t)", b=4), pm[:, :, :], ACT.Ln, bias=eps[:, 0:1], scale=1.0 / P)
            act.drain()
            nc.scalar.activation(r, r, ACT.Exp, scale=-0.5).then_inc(sem("head_rstd"), 1)

        def pe_head_norm(pe, n):
            pe.wait_ge(sem("head_squares"), n + 1)
            for b in range(4):
                e = nc.tensor.matmul(pm[:, b, :], ones[:, :], flat2(sq)[:, b * 2 * T:(b + 1) * 2 * T], start=True, stop=True)
            e.then_inc(sem("head_sums"), 1)

        att_s = mix[:, 8].rearrange("p (w j g) t -> p w j g t", w=2, j=2)
        att_w = mix[:, 9, 0:2, :]
        att_wT = mix[:, 9, 2:4, :]
        att_small = mix[:, 9, 4, :].rearrange("p (j c) -> p j c", j=2)

        def pe_attention(pe, s, groups, Q, K, Vt, row_term=None):
            n0, dg = s["att0"], P // groups
            mm = nc.tensor.matmul

            def scores(it):
                hd, qt = it // 2, it % 2
                nk = (qt + 1) * P
                if it >= 2:
                    pe.wait_ge(sem("att_scores_read"), n0 + it - 1)
                for g in range(groups):
                    bank = pm[:, 2 * (it % 2) + g, 0:nk]
                    e = mm(bank, Q[g * dg:(g + 1) * dg, hd, qt * P:(qt + 1) * P], K[g * dg:(g + 1) * dg, hd, 0:nk],
                           start=True, stop=row_term is None)
                if row_term is not None:
                    lhsT, rhs = row_term(hd)
                    e = mm(pm[:, 2 * (it % 2), 0:nk], lhsT, rhs[:, 0:nk], start=False, stop=True)
                e.then_inc(sem("att_scores"), 1)

            def turn(it):
                pe.wait_ge(sem("att_weights"), n0 + it + 1)
                for k in range(it % 2 + 1):
                    e = nc.tensor.transpose(pp[:, 2 + it % 2, k * P:(k + 1) * P], att_w[:, it % 2, k * P:(k + 1) * P], ident[:, :])
                e.then_inc(sem("att_turned"), 1)

            def values(it):
                hd, qt = it // 2, it % 2
                pe.wait_ge(sem("att_wT"), n0 + it + 1)
                if qt == 0 and hd >= 2:
                    pe.wait_ge(sem("att_out_read"), n0 // 2 + hd - 1)
                for k in range(qt + 1):
                    e = mm(pp[:, hd % 2, qt * P:(qt + 1) * P], Vt[:, k, hd * P:(hd + 1) * P], att_wT[:, it % 2, k * P:(k + 1) * P],
                           start=(k == 0), stop=(k == qt))
                e.then_inc(sem("att_out"), 1)

            scores(0)
            for it in range(16):
                if it < 15:
                    scores(it + 1)
                turn(it)
                values(it)

        def act_attention(act, s, groups, scale):
            n0 = s["att0"]
            for it in range(16):
                j, nk = it % 2, (it % 2 + 1) * P
                act.wait_ge(sem("att_max"), n0 + it + 1)
                for g in range(groups):
                    e = nc.scalar.activation(att_s[:, 1, j, g, 0:nk], att_s[:, 0, j, g, 0:nk], ACT.Exp, scale=scale,
                                             bias=att_small[:, j, g:g + 1], accum_out=att_small[:, j, 2 + g:3 + g])
                e.then_inc(sem("att_exp"), 1)
                act.wait_ge(sem("att_turned"), n0 + it + 1)
                nc.scalar.activation(att_wT[:, j, 0:nk], pp[:, 2 + j, 0:nk], ACT.Copy).then_inc(sem("att_wT"), 1)

        def dve_attention(dve, s, groups, scale, bias, factor, o, second=None):
            v, n0 = nc.vector, s["att0"]

            def maxima(it):
                hd, j, nk = it // 2, it % 2, (it % 2 + 1) * P
                dve.wait_ge(sem("att_scores"), n0 + it + 1)
                if groups == 2:
                    b = bias[:, j, 0:nk].rearrange("p (a k) -> p a k", a=1).to_broadcast([P, 2, nk])
                    v.scalar_tensor_tensor(att_s[:, 0, j, :, 0:nk], b, factor(hd), pm[:, 2 * j:2 * j + 2, 0:nk],
                                           ALU.mult, ALU.add).then_inc(sem("att_scores_read"), 1)
                else:
                    v.scalar_tensor_tensor(att_s[:, 0, j, 0, 0:nk], bias[:, j, 0:nk], factor(hd), pm[:, 2 * j, 0:nk],
                                           ALU.mult, ALU.add).then_inc(sem("att_scores_read"), 1)
                dve.drain()
                v.tensor_reduce(att_small[:, j, 4:4 + groups], att_s[:, 0, j, 0:groups, 0:nk], AX_X, ALU.max)
                dve.drain()
                v.tensor_scalar(att_small[:, j, 0:groups], att_small[:, j, 4:4 + groups], -scale, None, ALU.mult
                                ).then_inc(sem("att_max"), 1)

            def weights(it):
                j, nk = it % 2, (it % 2 + 1) * P
                dve.wait_ge(sem("att_exp"), n0 + it + 1)
                v.reciprocal(att_small[:, j, 4:4 + groups], att_small[:, j, 2:2 + groups])
                dve.drain()
                e = v.tensor_scalar(att_w[:, j, 0:nk], att_s[:, 1, j, 0, 0:nk], att_small[:, j, 4:5], None, ALU.mult)
                if groups == 2:
                    v.tensor_tensor(att_small[:, j, 6:7], att_small[:, j, 5:6], second, ALU.mult)
                    dve.drain()
                    e = v.scalar_tensor_tensor(att_w[:, j, 0:nk], att_s[:, 1, j, 1, 0:nk], att_small[:, j, 6:7],
                                               att_w[:, j, 0:nk], ALU.mult, ALU.add)
                e.then_inc(sem("att_weights"), 1)

            def take(hd):
                dve.wait_ge(sem("att_out"), n0 + 2 * hd + 2)
                v.tensor_copy(o[:, hd, :], pp[:, hd % 2, 0:T]).then_inc(sem("att_out_read"), 1)

            maxima(0)
            for it in range(16):
                if it < 15:
                    maxima(it + 1)
                weights(it)
                if it % 2 == 1 and it >= 3:
                    take(it // 2 - 1)
            take(7)
            dve.drain()

        def pe_token_major(pe, src, name, count0, ready):
            pe.wait_ge(*ready)
            for b in range(4):
                t, half = b // 2, b % 2
                for k in range(4):
                    e = nc.tensor.transpose(pp[:, b, k * P:(k + 1) * P], src[:, 4 * half + k, t * P:(t + 1) * P], ident[:, :])
                e.then_inc(sem(name), 1)

        R_GATE, R_X, R_CONV, R_CORR, R_R, R_I, R_A, R_TH = (mix[:, b] for b in range(8))

        def act_rec(act, s, read_out, split, rstd):
            seg = s["segs"][1]
            n_cols = seg.next.kt * seg.next.width
            act_log1p(act, s["ls0"], rec_col[:, 0, :], rec_col[:, 1, :], rec_col[:, 3, :])
            act.wait_ge(sem("rec_conv"), 1)
            fill_hi(act, s["fill"] + 1, R_CONV)
            for slot, (dst, bias_row) in enumerate(((R_R, VEC_REC_BA), (R_I, VEC_REC_BX))):
                act.wait_ge(sem("panel_done"), seg.g0 + slot + 1)
                nc.scalar.activation(R_CORR[:, 0:4, :], pp[:, :, T:2 * T], ACT.Copy)
                nc.scalar.activation(R_CORR[:, 4:8, :], pm[:, :, T:2 * T], ACT.Copy).then_inc(sem("corr_copied"), 1)
                split(slot, 16 * (seg.g0 // 2 + 2), n_cols)
                act.wait_ge(sem("panel_out"), seg.g0 + slot + 1)
                for k in range(KD):
                    e = nc.scalar.activation(dst[:, k, :], dst[:, k, :], ACT.Sigmoid, bias=vec[:, k, bias_row:bias_row + 1])
                e.then_inc(sem("rec_sigmoid"), 1)
            act.wait_ge(sem("rec_lambda"), 1)
            act.drain()
            for k in range(KD):
                nc.scalar.activation(R_TH[:, k, :], R_R[:, k, :], ACT.Tanh, scale=rec_col[:, 4, k:k + 1])
            for k in range(KD):
                e = nc.scalar.activation(R_A[:, k, :], R_R[:, k, :], ACT.Exp, scale=rec_col[:, 4, k:k + 1])
            e.then_inc(sem("rec_a"), 1)
            act.wait_ge(sem("rec_one_minus_a2"), 1)
            nc.scalar.activation(R_TH, R_TH, ACT.Sqrt, scale=-1.0).then_inc(sem("rec_sqrt"), 1)
            nc.scalar.activation(R_GATE, R_GATE, ACT.Gelu_apprx_tanh).then_inc(sem("rec_gelu"), 1)
            act.wait_ge(sem("rec_gated"), 1)
            fill_hi(act, s["fill"] + 2, R_A)
            read_out(s["segs"][2], s)

        def dve_rec(dve, s, read_out, split):
            v, seg = nc.vector, s["segs"][1]
            read_out(s["segs"][0], s, mix[:, 0:2].rearrange("p b k t -> p (b k) t"))
            dve_conv(dve, R_CONV, R_X, range(KD), VEC_REC_CONV_W, VEC_REC_CONV_B)
            v.tensor_copy(rec_col[:, 5, :], vec[:, :, VEC_REC_LAM]).then_inc(sem("rec_conv"), 1)
            dve.drain()
            dve_log1p(dve, s["ls0"], rec_col[:, 5, :], rec_col[:, 0, :], rec_col[:, 1, :], rec_col[:, 2, :], rec_col[:, 3, :])
            v.scalar_tensor_tensor(rec_col[:, 4, :], rec_col[:, 5, :], 0.0, rec_col[:, 3, :], ALU.min, ALU.subtract)
            dve.drain()
            v.tensor_scalar(rec_col[:, 4, :], rec_col[:, 4, :], 8.0, None, ALU.mult).then_inc(sem("rec_lambda"), 1)
            fill_lo(dve, s["fill"] + 1, R_CONV)
            for slot, dst in enumerate((R_R, R_I)):
                dve.wait_ge(sem("corr_copied"), seg.g0 + slot + 1)
                v.tensor_tensor(dst[:, 0:4, :], pp[:, :, 0:T], R_CORR[:, 0:4, :], ALU.add)
                v.tensor_tensor(dst[:, 4:8, :], pm[:, :, 0:T], R_CORR[:, 4:8, :], ALU.add).then_inc(sem("panel_out"), 1)
                split(slot, seg.g0 + slot + 3, seg.next.kt * seg.next.width)
            dve.wait_ge(sem("rec_sigmoid"), 2)
            v.tensor_tensor(R_I, R_I, R_CONV, ALU.mult)
            dve.wait_ge(sem("rec_a"), 1)
            v.tensor_tensor(R_R, R_A, R_A, ALU.mult)
            dve.drain()
            v.scalar_tensor_tensor(R_TH, R_R, 1.0, R_TH, ALU.add, ALU.mult).then_inc(sem("rec_one_minus_a2"), 1)
            v.memset(R_A[:, :, 0:1], 0.0)
            dve.wait_ge(sem("rec_sqrt"), 1)
            v.tensor_tensor(R_I, R_I, R_TH, ALU.mult)
            dve.drain()
            v.tensor_tensor_scan(flat2(R_R), flat2(R_A), flat2(R_I), 0.0, ALU.mult, ALU.add)
            dve.drain()
            dve.wait_ge(sem("rec_gelu"), 1)
            v.tensor_tensor(R_A, R_R, R_GATE, ALU.mult).then_inc(sem("rec_gated"), 1)
            fill_lo(dve, s["fill"] + 2, R_A)
            read_out(s["segs"][2], s)

        def pe_rec(pe, s, products, x_ready):
            seg = s["segs"][1]
            pe.wait_ge(sem("x_lo"), 2 * s["fill"] + 4)
            for slot in range(2):
                pe.wait_ge(sem("weights_lo"), seg.g0 + slot + 1)
                pe.wait_ge(sem("panel_out"), seg.g0 + slot)
                for n in range(KD):
                    bank = pp[:, n, :] if n < 4 else pm[:, n - 4, :]
                    nc.tensor.matmul(bank, whi[:, slot, n * P:(n + 1) * P], xs[:, n, :], start=True, stop=False)
                    e = nc.tensor.matmul(bank[:, 0:T], wlo[:, slot, n * P:(n + 1) * P], xs[:, n, 0:T], start=False, stop=True)
                e.then_inc(sem("panel_done"), 1)
            products(s["segs"][2], xs, x_ready(s["fill"] + 2))

        def dve_conv(dve, dst, src, tiles, w_row, b_row, vec_tile=lambda k: k):
            v = nc.vector
            for k in tiles:
                q = vec_tile(k)
                v.tensor_scalar(dst[:, k, :], src[:, k, :], vec[:, q, w_row + 3:w_row + 4], vec[:, q, b_row:b_row + 1],
                                ALU.mult, ALU.add)
            for j in (2, 1, 0):
                d = 3 - j
                dve.drain()
                for k in tiles:
                    q = vec_tile(k)
                    v.scalar_tensor_tensor(dst[:, k, d:T], src[:, k, 0:T - d], vec[:, q, w_row + j:w_row + j + 1],
                                           dst[:, k, d:T], ALU.mult, ALU.add)
            dve.drain()

        def act_pool(act, s, read_out, split, rstd):
            seg = s["segs"][1]
            act.wait_ge(sem("pool_means"), 1)
            fill_hi(act, s["fill"] + 1, mix[:, 4])
            for slot in range(2):
                act.wait_ge(sem("panel_done"), seg.g0 + slot + 1)
                nc.scalar.activation(mix[:, 5, 4 * slot:4 * slot + 4, :], (pp, pm)[slot][:, :, T:2 * T], ACT.Copy
                                     ).then_inc(sem("corr_copied"), 1)
                split(slot, 16 * (seg.g0 // 2 + 2), seg.next.kt * seg.next.width)
            act.wait_ge(sem("panel_out"), seg.g0 + 2)
            fill_hi(act, s["fill"] + 2, mix[:, 4], VEC_POOL_SCALE)
            read_out(s["segs"][2], s)

        def dve_pool(dve, s, read_out, split):
            v, seg = nc.vector, s["segs"][1]
            U, W1, W2, RC, PO = (mix[:, b] for b in range(5))
            read_out(s["segs"][0], s, U)
            for g in range(4):
                v.memset(RC[:, g, :], 1.0 / 2 ** (g + 1))
                v.tensor_scalar(RC[:, 4 + g, 0:16], steps[:, :], float(2 ** (g + 1)), None, ALU.min)
            dve.drain()
            v.reciprocal(RC[:, 0:4, 0:16], RC[:, 4:8, 0:16])
            for dst, src, k0, d in ((W1, U, 0, 1), (W2, W1, 2, 2), (W1, W2, 4, 4), (W2, W1, 6, 8)):
                v.tensor_copy(dst[:, k0:, 0:d], src[:, k0:, 0:d])
                v.tensor_tensor(dst[:, k0:, d:T], src[:, k0:, d:T], src[:, k0:, 0:T - d], ALU.add)
                dve.drain()
            for g, W in enumerate((W1, W2, W1, W2)):
                v.tensor_tensor(PO[:, 2 * g:2 * g + 2, :], W[:, 2 * g:2 * g + 2, :], RC[:, g:g + 1, :].to_broadcast([P, 2, T]),
                                ALU.mult)
            dve.drain()
            v.tensor_tensor(PO, PO, U, ALU.subtract).then_inc(sem("pool_means"), 1)
            fill_lo(dve, s["fill"] + 1, PO)
            for slot in range(2):
                dve.wait_ge(sem("corr_copied"), seg.g0 + slot + 1)
                q = slice(4 * slot, 4 * slot + 4)
                v.tensor_tensor(PO[:, q, :], (pp, pm)[slot][:, :, 0:T], mix[:, 5, q, :], ALU.add).then_inc(sem("panel_out"), 1)
                split(slot, seg.g0 + slot + 3, seg.next.kt * seg.next.width)
            fill_lo(dve, s["fill"] + 2, PO, VEC_POOL_SCALE)
            read_out(s["segs"][2], s)

        def pe_pool(pe, s, products, x_ready):
            seg = s["segs"][1]
            pe.wait_ge(sem("x_lo"), 2 * s["fill"] + 4)
            for slot in range(2):
                pe.wait_ge(sem("weights_lo"), seg.g0 + slot + 1)
                pe.wait_ge(sem("panel_out"), seg.g0 + slot)
                for n in range(4):
                    bank = (pp, pm)[slot][:, n, :]
                    for t in range(2):
                        c = (2 * (n // 2) + t) * PC + (n % 2) * P
                        k = 2 * (2 * slot + n // 2) + t
                        nc.tensor.matmul(bank, whi[:, slot, c:c + P], xs[:, k, :], start=(t == 0), stop=False)
                        e = nc.tensor.matmul(bank[:, 0:T], wlo[:, slot, c:c + P], xs[:, k, 0:T], start=False, stop=(t == 1))
                e.then_inc(sem("panel_done"), 1)
            products(s["segs"][2], xs, x_ready(s["fill"] + 2))

        DA_SCALE = 64 ** -0.5

        def act_diff(act, s, read_out, split, rstd):
            act.wait_ge(sem("diff_lambda_sums"), 1)
            nc.scalar.activation(small[:, 2:4], small[:, 0:2], ACT.Exp).then_inc(sem("diff_lambda_exp"), 1)
            for b in range(4):
                act.wait_ge(sem("turned"), s["turn0"] + b + 1)
                nc.scalar.activation(tok(mix[:, 3])[:, b // 2, 512 * (b % 2):512 * (b % 2) + 512], pp[:, b, :], ACT.Copy
                                     ).then_inc(sem("turned_read"), 1)
            act_attention(act, s, 2, DA_SCALE)
            act_head_norm(act, s["hn0"], mix[:, 4], mix[:, 5])
            act.wait_ge(sem("heads_done"), s["hn0"] + 1)
            fill_hi(act, s["fill"] + 1, mix[:, 4])
            read_out(s["segs"][1], s)

        def dve_diff(dve, s, read_out, split):
            v = nc.vector
            lam_init = 0.8 - 0.6 * math.exp(-0.3 * s["layer"])
            read_out(s["segs"][0], s, mix[:, 0:3].rearrange("p b k t -> p (b k) t"))
            dve.wait_ge(sem("rows_loaded"), 32)
            lam = lamrow[:, :].rearrange("p (a b d) -> p a b d", a=2, b=2)
            v.tensor_tensor(tsum[:, 0, 0:128].rearrange("p (a d) -> p a d", a=2), lam[:, :, 0, :], lam[:, :, 1, :], ALU.mult
                            ).then_inc(sem("diff_projected"), 1)
            dve.drain()
            v.tensor_reduce(small[:, 0:2], tsum[:, 0, 0:128].rearrange("p (a d) -> p a d", a=2), AX_X, ALU.add
                            ).then_inc(sem("diff_lambda_sums"), 1)
            dve.wait_ge(sem("diff_lambda_exp"), 1)
            v.tensor_tensor(small[:, 4:5], small[:, 3:4], small[:, 2:3], ALU.subtract)
            dve.drain()
            v.tensor_scalar(small[:, 5:6], small[:, 4:5], -lam_init, None, ALU.add)
            dve.drain()
            slope = [2.0 ** (-8.0 * (hd + 1) / 8) for hd in range(8)]
            dve_attention(dve, s, 2, DA_SCALE, dist, lambda hd: -slope[hd] / DA_SCALE, mix[:, 4], small[:, 5:6])
            v.tensor_scalar(small[:, 6:7], vec[:, 0, VEC_SUBLN:VEC_SUBLN + 1], 1.0 - lam_init, None, ALU.mult
                            ).then_inc(sem("head_out"), 1)
            dve.drain()
            dve.wait_ge(sem("head_rstd"), s["hn0"] + 1)
            v.scalar_tensor_tensor(mix[:, 4], mix[:, 4], small[:, 6:7], mix[:, 5], ALU.mult, ALU.mult
                                   ).then_inc(sem("heads_done"), 1)
            fill_lo(dve, s["fill"] + 1, mix[:, 4])
            read_out(s["segs"][1], s)

        def pe_diff(pe, s, products, x_ready):
            pe_token_major(pe, mix[:, 2], "turned", s["turn0"], (sem("diff_projected"), 1))
            pe.wait_ge(sem("turned_read"), s["turn0"] + 4)
            pe_attention(pe, s, 2, mix[:, 0], mix[:, 1], tok(mix[:, 3]))
            pe_head_norm(pe, s["hn0"])
            products(s["segs"][1], xs, x_ready(s["fill"] + 1))

        def act_hgrn(act, s, read_out, split, rstd):
            Q, F, V, G, K, D1, B, QR, VT, KO = (mix[:, b] for b in range(10))
            it = s["it"] + 1
            if s["layer"] > 0:
                act.wait_ge(sem("lower_bound_shifted"), 1)
                nc.scalar.activation(lbw[:, :, 0:4], lbw[:, :, 0:4], ACT.Exp).then_inc(sem("lower_bound_exp"), 1)
            act.wait_ge(sem("hgrn_projected"), it)
            nc.scalar.activation(F, F, ACT.Sigmoid).then_inc(sem("hgrn_sigmoid"), 1)
            act.wait_ge(sem("turned"), s["turn0"] + 4)
            for b in range(4):
                e = nc.scalar.activation(tok(VT)[:, b // 2, 512 * (b % 2):512 * (b % 2) + 512], pp[:, b, :], ACT.Copy)
                e.then_inc(sem("turned_read"), 1)
            act.wait_ge(sem("hgrn_forget"), it)
            nc.scalar.activation(D1, F, ACT.Ln).then_inc(sem("hgrn_log"), 1)
            act.wait_ge(sem("hgrn_differences"), it)
            nc.scalar.activation(QR, D1, ACT.Exp).then_inc(sem("hgrn_exp"), 1)
            act.drain()
            nc.scalar.activation(D1, D1, ACT.Exp, scale=-1.0).then_inc(sem("hgrn_exp"), 1)
            nc.scalar.activation(B, B, ACT.Exp).then_inc(sem("hgrn_exp"), 1)
            nc.scalar.activation(F, F, ACT.Exp).then_inc(sem("hgrn_exp"), 1)
            nc.scalar.activation(G, G, ACT.Silu).then_inc(sem("hgrn_silu"), 1)
            act_head_norm(act, s["hn0"], D1, QR)
            act.wait_ge(sem("heads_done"), s["hn0"] + 1)
            fill_hi(act, s["fill"] + 1, D1)
            read_out(s["segs"][1], s)

        def dve_hgrn(dve, s, read_out, split):
            v = nc.vector
            Q, F, V, G, K, D1, B, QR, VT, KO = (mix[:, b] for b in range(10))
            it = s["it"] + 1
            read_out(s["segs"][0], s, mix[:, 0:4].rearrange("p b k t -> p (b k) t"))
            v.memset(small[:, 0:1], 0.0).then_inc(sem("hgrn_projected"), 1)
            if s["layer"] == 0:
                v.memset(lbw[:, :, 4:5], 0.0)
            else:
                rows = vec[:, :, VEC_LB:VEC_LB + 4]
                v.tensor_reduce(lbw[:, :, 4:5], rows, AX_X, ALU.max)
                dve.drain()
                v.tensor_tensor(lbw[:, :, 0:4], rows, lbw[:, :, 4:5].to_broadcast([P, KD, 4]), ALU.subtract
                                ).then_inc(sem("lower_bound_shifted"), 1)
                dve.wait_ge(sem("lower_bound_exp"), 1)
                v.tensor_reduce(lbw[:, :, 4:5], lbw[:, :, 0:4], AX_X, ALU.add)
                v.tensor_reduce(lbw[:, :, 5:6], lbw[:, :, 1:s["layer"] + 1], AX_X, ALU.add)
                dve.drain()
                v.reciprocal(lbw[:, :, 4:5], lbw[:, :, 4:5])
                dve.drain()
                v.tensor_tensor(lbw[:, :, 4:5], lbw[:, :, 4:5], lbw[:, :, 5:6], ALU.mult)
            dve.drain()
            v.tensor_scalar(lbw[:, :, 5:6], lbw[:, :, 4:5], -1.0, 1.0, ALU.mult, ALU.add)
            dve.drain()
            dve.wait_ge(sem("hgrn_sigmoid"), it)
            for k in range(KD):
                e = v.tensor_scalar(F[:, k, :], F[:, k, :], lbw[:, k, 5:6], lbw[:, k, 4:5], ALU.mult, ALU.add)
            e.then_inc(sem("hgrn_forget"), 1)
            dve.drain()
            v.tensor_scalar(K, F, -1.0, 1.0, ALU.mult, ALU.add)
            dve.wait_ge(sem("hgrn_log"), it)
            for k in range(KD):
                v.tensor_tensor_scan(B[:, k, :], keep[:, :], D1[:, k, :], 0.0, ALU.mult, ALU.add)
            dve.drain()
            blk = lambda buf: flat2(buf).rearrange("p (n t) -> p n t", t=HGB)
            n_blk = KD * NB
            v.tensor_tensor(blk(D1), blk(B), blk(B)[:, :, HGB // 2:HGB // 2 + 1].to_broadcast([P, n_blk, HGB]), ALU.subtract)
            v.tensor_tensor(blk(F), blk(B)[:, :, HGB - 1:HGB].to_broadcast([P, n_blk, HGB]), blk(B), ALU.subtract
                            ).then_inc(sem("hgrn_differences"), 1)
            for n, (dst, src, e) in enumerate(((QR, Q, QR), (D1, K, D1), (Q, Q, B), (K, K, F))):
                dve.wait_ge(sem("hgrn_exp"), 4 * (it - 1) + n + 1)
                v.tensor_tensor(dst, src, e, ALU.mult).then_inc(sem("hgrn_operand"), 1)
            for b in range(4):
                dve.wait_ge(sem("turned"), s["turn0"] + 4 + b + 1)
                o = slice(512 * (b % 2), 512 * (b % 2) + 512)
                v.tensor_scalar(tok(F)[:, b // 2, o], pp[:, b, :], even_odd[:, 0:1], None, ALU.mult)
                v.tensor_scalar(tok(KO)[:, b // 2, o], pp[:, b, :], even_odd[:, 1:2], None, ALU.mult
                                ).then_inc(sem("turned_read"), 1)
            AT = flat2(V).rearrange("p (n c) -> p n c", c=P)
            v.memset(V, 0.0)
            dve.drain()
            for b in range(4):
                dve.wait_ge(sem("hgrn_scores"), 4 * (it - 1) + b + 1)
                for j in range(4):
                    e = v.copy_predicated(AT[:, 4 * b + j, :], block_causal[:, :].bitcast(I32), pm[:, b, j * P:(j + 1) * P])
                e.then_inc(sem("hgrn_masked"), 1)
            S = flat2(K).rearrange("p (j c) -> p j c", j=2)
            for n in range(NB - 1):
                dve.wait_ge(sem("hgrn_update"), (NB - 1) * (it - 1) + n + 1)
                for hd in range(8):
                    u = pm[:, 2 * (n % 2) + hd // 4, (hd % 4) * P:(hd % 4) * P + P]
                    o = slice(hd * P, hd * P + P)
                    if n == 0:
                        e = v.tensor_copy(S[:, 1, o], u)
                    else:
                        c = HGB * n + HGB - 1
                        e = v.scalar_tensor_tensor(S[:, (n + 1) % 2, o], S[:, n % 2, o], B[:, hd, c:c + 1], u, ALU.mult, ALU.add)
                e.then_inc(sem("hgrn_state"), 1)
                dve.drain()
            dve.wait_ge(sem("hgrn_out"), it)
            v.tensor_copy(D1.rearrange("p (b k) t -> p b (k t)", b=4), pp[:, :, :]).then_inc(sem("head_out"), 1)
            dve.drain()
            dve.wait_ge(sem("hgrn_silu"), it)
            dve.wait_ge(sem("head_rstd"), s["hn0"] + 1)
            j = VEC_GNORM + s["j"]
            v.scalar_tensor_tensor(D1, D1, vec[:, 0, j:j + 1], QR, ALU.mult, ALU.mult)
            dve.drain()
            v.tensor_tensor(D1, D1, G, ALU.mult).then_inc(sem("heads_done"), 1)
            fill_lo(dve, s["fill"] + 1, D1)
            read_out(s["segs"][1], s)

        def pe_hgrn(pe, s, products, x_ready):
            mm = nc.tensor.matmul
            Q, F, V, G, K, D1, B, QR, VT, KO = (mix[:, b] for b in range(10))
            i0 = s["it"]
            pe_token_major(pe, V, "turned", s["turn0"], (sem("hgrn_projected"), i0 + 1))
            pe.wait_ge(sem("hgrn_operand"), 4 * i0 + 4)
            pe.wait_ge(sem("turned_read"), s["turn0"] + 4)
            pe_token_major(pe, K, "turned", s["turn0"] + 4, (sem("hgrn_operand"), 4 * i0 + 4))
            for b in range(4):
                for j in range(4):
                    hd, t = (4 * b + j) // 2, j % 2
                    o = slice(t * P, t * P + P)
                    e = mm(pm[:, b, j * P:(j + 1) * P], D1[:, hd, o], QR[:, hd, o], start=True, stop=True)
                e.then_inc(sem("hgrn_scores"), 1)
            AT = flat2(V).rearrange("p (n c) -> p n c", c=P)
            out_cols = lambda hd, a, b: pp[:, hd // 2, (hd % 2) * T + a:(hd % 2) * T + b]
            pe.wait_ge(sem("turned_read"), s["turn0"] + 8)
            for hd in range(8):
                if hd % 2 == 0:
                    pe.wait_ge(sem("hgrn_masked"), 4 * i0 + hd // 2 + 1)
                for t in range(TT):
                    mm(out_cols(hd, t * P, t * P + P), tok(VT)[:, t, hd * P:hd * P + P], AT[:, 2 * hd + t, :],
                       start=(hd % 2 == 0 and t == 0), stop=False, skip_group_check=True)
            S = flat2(K).rearrange("p (j c) -> p j c", j=2)
            for n in range(NB):
                t, nb = n // 8, n % 8
                rows = slice(32 * (nb // 2), 32 * (nb // 2) + 32)
                kt = tok((F, KO)[nb % 2])
                if n < NB - 1:
                    if n >= 2:
                        pe.wait_ge(sem("hgrn_state"), (NB - 1) * i0 + n - 1)
                    for hd in range(8):
                        e = mm(pm[:, 2 * (n % 2) + hd // 4, (hd % 4) * P:(hd % 4) * P + P],
                               kt[rows, t, hd * P:hd * P + P], tok(VT)[rows, t, hd * P:hd * P + P], start=True, stop=True)
                    e.then_inc(sem("hgrn_update"), 1)
                if n >= 1:
                    pe.wait_ge(sem("hgrn_state"), (NB - 1) * i0 + n)
                    for hd in range(8):
                        e = mm(out_cols(hd, HGB * n, HGB * n + HGB), S[:, n % 2, hd * P:hd * P + P],
                               Q[:, hd, HGB * n:HGB * n + HGB], start=False, stop=(n == NB - 1), skip_group_check=True)
            e.then_inc(sem("hgrn_out"), 1)
            pe_head_norm(pe, s["hn0"])
            products(s["segs"][1], xs, x_ready(s["fill"] + 1))
        FOX_SCALE = P ** -0.5
        SSM_HD = D // SSM_H
        H_DT, H_F = mix[:, 2, 4, :], mix[:, 2, 5, :]
        H_ACS, H_CUM = mix[:, 7, 4, :], mix[:, 7, 5, :]
        H_COLS = mix[:, 7, 6, 0:64].rearrange("p (a h) -> p a h", a=4)
        H_LAST, H_DECAY = mix[:, 7, 6, 64:80], mix[:, 7, 6, 80:96]
        H_CB = flat2(mix[:, 8])[:, 0:512].rearrange("p (g t) -> p g t", g=2)
        H_BT = flat2(mix[:, 8])[:, 512:768]
        H_XD = flat2(mix[:, 2])[:, 0:D]
        H_ST = flat2(mix[:, 9])[:, 0:D]
        H_YO = flat2(mix[:, 9])[:, D:2 * D]

        def seg_decay(hd):
            return mix[:, 8, 3 + hd % 2, :]

        def seg_weight(hd):
            return mix[:, 8, 5 + hd % 2, :]

        def act_hyb(act, s, read_out, split, rstd):
            read_out(s["segs"][1], s)
            read_out(s["segs"][2], s)
            act.wait_ge(sem("hyb_conv"), 1)
            nc.scalar.activation(mix[:, 6], mix[:, 6], ACT.Silu)
            nc.scalar.activation(mix[:, 7, 0:4, :], mix[:, 7, 0:4, :], ACT.Silu)
            nc.scalar.activation(mix[:, 0], mix[:, 0], ACT.Silu).then_inc(sem("hyb_silu"), 1)
            nc.scalar.activation(small[:, 0:1], vec[:, 0, VEC_A_LOG:VEC_A_LOG + 1], ACT.Exp).then_inc(sem("hyb_a"), 1)
            for n in range(2):
                act_log1p(act, s["ls0"] + n, mix[:, 9, 4 * n, :], mix[:, 9, 4 * n + 1, :], mix[:, 9, 4 * n + 3, :])
            act.wait_ge(sem("hyb_decay_log"), 1)
            nc.scalar.activation(H_DECAY, H_DECAY, ACT.Exp).then_inc(sem("hyb_decay"), 1)
            act.wait_ge(sem("hyb_states"), 1)
            nc.scalar.activation(H_ST.rearrange("p (g c) -> p g c", g=2), pm[:, 2:4, :], ACT.Copy).then_inc(sem("hyb_states_read"), 1)
            for hd in range(SSM_H):
                act.wait_ge(sem("seg_log"), hd + 1)
                nc.scalar.activation(seg_decay(hd), seg_decay(hd), ACT.Exp).then_inc(sem("seg_exp"), 1)
            act.wait_ge(sem("hyb_off"), 1)
            act.wait_ge(sem("seg_weights"), SSM_H)
            nc.scalar.activation(flat2(mix[:, 8])[:, 0:D].rearrange("p (g c) -> p g c", g=2), pm[:, 0:2, :], ACT.Exp
                                 ).then_inc(sem("hyb_decay_out"), 1)
            act.wait_ge(sem("hyb_gated"), 1)
            nc.scalar.activation(mix[:, 9], mix[:, 6], ACT.Square).then_inc(sem("hyb_squares"), 1)
            act.wait_ge(sem("hyb_sums"), 1)
            nc.scalar.activation(corr[:, 0, :], pm[:, 0, :], ACT.Ln, bias=eps[:, 0:1], scale=1.0 / 512)
            act.drain()
            nc.scalar.activation(corr[:, 0, :], corr[:, 0, :], ACT.Exp, scale=-0.5).then_inc(sem("hyb_rstd"), 1)
            for b in range(4):
                act.wait_ge(sem("turned"), s["turn0"] + 4 + b + 1)
                nc.scalar.activation(tok(mix[:, 1])[:, b // 2, 512 * (b % 2):512 * (b % 2) + 512], pp[:, b, :], ACT.Copy
                                     ).then_inc(sem("turned_read"), 1)
            act_attention(act, s, 1, FOX_SCALE)
            act.wait_ge(sem("att_out_read"), (s["att0"] + 16) // 2)
            for k in range(KD):
                e = nc.scalar.activation(hs[:, k, 0:T], mix[:, 6, k, :], ACT.Copy, scale=vec[:, k, VEC_SSM_NORM:VEC_SSM_NORM + 1])
            e.then_inc(sem("cat_hi"), 1)
            nc.scalar.activation(hs[:, KD:2 * KD, 0:T], y[:, :, :], ACT.Copy).then_inc(sem("cat_hi"), 1)
            read_out(s["segs"][3], s)

        def dve_hyb(dve, s, read_out, split):
            v = nc.vector
            read_out(s["segs"][0], s, mix[:, 0:3].rearrange("p b k t -> p (b k) t"))
            read_out(s["segs"][1], s, (H_DT, H_F))
            read_out(s["segs"][2], s, mix[:, 3:6].rearrange("p b k t -> p (b k) t"))
            dve_conv(dve, mix[:, 6], mix[:, 1], range(KD), VEC_SSM_CONV_X, VEC_SSM_CONV_BX)
            dve_conv(dve, mix[:, 7], mix[:, 2], range(4), VEC_SSM_CONV_BC, VEC_SSM_CONV_BBC)
            v.tensor_scalar(H_DT, H_DT, vec[:, 0, VEC_DT_BIAS:VEC_DT_BIAS + 1], None, ALU.add)
            v.tensor_scalar(H_F, H_F, vec[:, 0, VEC_FOX_B:VEC_FOX_B + 1], None, ALU.add).then_inc(sem("hyb_conv"), 1)
            dve.drain()
            for n, x in enumerate((H_DT, H_F)):
                dve_log1p(dve, s["ls0"] + n, x, *(mix[:, 9, 4 * n + j, :] for j in range(4)))
            v.scalar_tensor_tensor(H_DT, H_DT, 0.0, mix[:, 9, 3, :], ALU.max, ALU.add)
            v.scalar_tensor_tensor(H_F, H_F, 0.0, mix[:, 9, 7, :], ALU.min, ALU.subtract)
            dve.drain()
            dve.wait_ge(sem("hyb_a"), 1)
            v.tensor_scalar(mix[:, 9, 0, :], H_DT, small[:, 0:1], -1.0, ALU.mult, ALU.mult)
            dve.drain()
            for c in range(TT):
                o = slice(c * P, c * P + P)
                v.tensor_tensor_scan(H_ACS[:, o], ones[:, :], mix[:, 9, 0, o], 0.0, ALU.mult, ALU.add)
                v.tensor_tensor_scan(mix[:, 9, 1, o], ones[:, :], H_F[:, o], mix[:, 9, 1, P - 1:P] if c else 0.0,
                                     ALU.mult, ALU.add)
                dve.drain()
            v.tensor_scalar(H_CUM, mix[:, 9, 1, :], -1.0 / FOX_SCALE, None, ALU.mult).then_inc(sem("hyb_scans"), 1)
            dve.wait_ge(sem("hyb_cols"), 1)
            v.tensor_copy(H_COLS, pm[:, 0, :].rearrange("p (a r) -> p a r", a=4)[:, :, 0:SSM_H])
            v.tensor_copy(H_LAST, pm[:, 1, 0:SSM_H])
            dve.drain()
            v.tensor_tensor(H_DECAY, H_LAST, H_COLS[:, 2, :], ALU.subtract).then_inc(sem("hyb_decay_log"), 1)
            dve.wait_ge(sem("hyb_cb"), 1)
            v.tensor_tensor(flat2(mix[:, 8])[:, 0:512].rearrange("p (n t) -> p n t", n=4),
                            pm[:, 3, :].rearrange("p (n t) -> p n t", n=4),
                            tri[:, :].rearrange("p (a t) -> p a t", a=1).to_broadcast([P, 4, P]), ALU.mult)
            v.tensor_copy(H_BT, pm[:, 2, 0:256]).then_inc(sem("hyb_cb_read"), 1)
            for b in range(4):
                t, half = b // 2, b % 2
                dve.wait_ge(sem("turned"), s["turn0"] + b + 1)
                v.tensor_tensor(tok(mix[:, 1])[:, t, 512 * half:512 * half + 512].rearrange("p (h d) -> p h d", h=8),
                                pp[:, b, :].rearrange("p (h d) -> p h d", h=8),
                                H_COLS[:, t, 8 * half:8 * half + 8].rearrange("p (h a) -> p h a", a=1).to_broadcast([P, 8, SSM_HD]),
                                ALU.mult).then_inc(sem("turned_read"), 1)
            dve.drain()
            dve.wait_ge(sem("hyb_decay"), 1)
            v.tensor_tensor(H_XD.rearrange("p (h d) -> p h d", h=SSM_H),
                            tok(mix[:, 1])[:, 0, :].rearrange("p (h d) -> p h d", h=SSM_H),
                            H_DECAY.rearrange("p (h a) -> p h a", a=1).to_broadcast([P, SSM_H, SSM_HD]),
                            ALU.mult).then_inc(sem("hyb_x"), 1)

            def difference(hd):
                dve.wait_ge(sem("seg_sums"), hd + 1)
                for c in range(TT):
                    o = slice(c * P, c * P + P)
                    e = v.tensor_scalar(seg_decay(hd)[:, o], pm[:, hd % 2, o], H_COLS[:, 2 + c, hd:hd + 1], 0.0,
                                        ALU.subtract, ALU.min)
                e.then_inc(sem("seg_log"), 1)

            difference(0)
            for hd in range(SSM_H):
                if hd < SSM_H - 1:
                    difference(hd + 1)
                dve.wait_ge(sem("seg_exp"), hd + 1)
                if hd >= 2:
                    dve.wait_ge(sem("seg_out"), hd - 1)
                v.tensor_tensor(seg_weight(hd), seg_decay(hd), H_CB[:, hd // 8, :], ALU.mult).then_inc(sem("seg_weights"), 1)
            dve.wait_ge(sem("rows_loaded"), 32)
            v.tensor_copy(rec_col[0:64, 5, :], skiprow[0:64, 0::2])
            v.tensor_copy(rec_col[64:P, 5, :], skiprow[64:P, 1::2])
            dve.drain()
            dve.wait_ge(sem("seg_out"), SSM_H)
            for k in range(KD):
                v.scalar_tensor_tensor(mix[:, 6, k, :], mix[:, 6, k, :], rec_col[:, 5, k:k + 1],
                                       pp[:, k // 2, (k % 2) * T:(k % 2) * T + T], ALU.mult, ALU.add)
            dve.wait_ge(sem("hyb_decay_out"), 1)
            v.tensor_tensor(H_YO.rearrange("p (g c) -> p g c", g=2), pm[:, 2:4, :],
                            flat2(mix[:, 8])[:, 0:D].rearrange("p (g c) -> p g c", g=2), ALU.mult)
            dve.drain()
            v.tensor_tensor(mix[:, 6, :, P:T], mix[:, 6, :, P:T], H_YO.rearrange("p (k t) -> p k t", k=KD), ALU.add)
            dve.drain()
            v.tensor_tensor(mix[:, 6], mix[:, 6], mix[:, 0], ALU.mult).then_inc(sem("hyb_gated"), 1)
            dve.drain()
            dve.wait_ge(sem("hyb_rstd"), 1)
            for g in range(2):
                v.tensor_tensor(mix[:, 6, 4 * g:4 * g + 4, :], mix[:, 6, 4 * g:4 * g + 4, :],
                                corr[:, 0, g * T:g * T + T].rearrange("p (a t) -> p a t", a=1).to_broadcast([P, 4, T]), ALU.mult)
            dve.drain()
            dve_attention(dve, s, 1, FOX_SCALE, causal, lambda hd: -1.0, y)
            for k in range(KD):
                if k == 0:
                    dve.wait_ge(sem("cat_hi"), 1)
                e = v.scalar_tensor_tensor(hs[:, k, T:2 * T], mix[:, 6, k, :], vec[:, k, VEC_SSM_NORM:VEC_SSM_NORM + 1],
                                           hs[:, k, 0:T].bitcast(F32), ALU.mult, ALU.subtract)
            e.then_inc(sem("cat_lo"), 1)
            dve.wait_ge(sem("cat_hi"), 2)
            v.tensor_tensor(hs[:, KD:2 * KD, T:2 * T], y[:, :, :], hs[:, KD:2 * KD, 0:T].bitcast(F32), ALU.subtract
                            ).then_inc(sem("cat_lo"), 1)
            dve.drain()
            read_out(s["segs"][3], s)

        def pe_hyb(pe, s, products, x_ready):
            mm = nc.tensor.matmul
            products(s["segs"][1], xs)
            products(s["segs"][2], xs)
            B = [mix[:, 7, g, :] for g in range(2)]
            C = [mix[:, 7, 2 + g, :] for g in range(2)]
            chunk = [slice(0, P), slice(P, T)]
            pe.wait_ge(sem("hyb_scans"), 1)
            for n, src in enumerate((H_DT, H_DT, H_ACS, H_ACS)):
                nc.tensor.transpose(pm[:, 0, n * P:(n + 1) * P], src[:, chunk[n % 2]], ident[:, :])
            mm(pm[:, 1, 0:SSM_H], H_ACS[:, P - 1:P].to_broadcast([P, P]), ident[:, 0:SSM_H], start=True, stop=True
               ).then_inc(sem("hyb_cols"), 1)
            pe.wait_ge(sem("hyb_silu"), 1)
            for g in range(2):
                nc.tensor.transpose(pm[:, 2, g * P:(g + 1) * P], B[g][:, chunk[0]], ident[:, :])
                for c in range(TT):
                    e = mm(pm[:, 3, (2 * g + c) * P:(2 * g + c + 1) * P], B[g][:, chunk[c]], C[g][:, chunk[c]],
                           start=True, stop=True)
            e.then_inc(sem("hyb_cb"), 1)
            pe_token_major(pe, mix[:, 6], "turned", s["turn0"], (sem("hyb_silu"), 1))
            pe.wait_ge(sem("hyb_cb_read"), 1)
            pe.wait_ge(sem("hyb_x"), 1)
            for g in range(2):
                e = mm(pm[:, 2 + g, :], H_BT[:, g * P:(g + 1) * P], H_XD[:, g * 512:(g + 1) * 512], start=True, stop=True)
            e.then_inc(sem("hyb_states"), 1)

            def sums_on_all(hd):
                if hd >= 2:
                    pe.wait_ge(sem("seg_log"), hd - 1)
                mm(pm[:, hd % 2, 0:T], ident[:, hd:hd + 1].to_broadcast([P, P]), H_ACS, start=True, stop=True
                   ).then_inc(sem("seg_sums"), 1)

            sums_on_all(0)
            for hd in range(SSM_H):
                if hd < SSM_H - 1:
                    sums_on_all(hd + 1)
                pe.wait_ge(sem("seg_weights"), hd + 1)
                k, r = hd // 2, SSM_HD * (hd % 2)
                for c in range(TT):
                    e = mm(pp[r:r + SSM_HD, k // 2, (k % 2) * T + c * P:(k % 2) * T + (c + 1) * P],
                           tok(mix[:, 1])[:, c, hd * SSM_HD:(hd + 1) * SSM_HD], seg_weight(hd)[:, chunk[c]], start=True, stop=True)
                e.then_inc(sem("seg_out"), 1)
            pe.wait_ge(sem("hyb_states_read"), 1)
            pe.wait_ge(sem("seg_log"), SSM_H)
            for k in range(KD):
                o = slice((k % 4) * P, (k % 4) * P + P)
                mm(pm[:, 2 + k // 4, o], H_ST[:, k * P:(k + 1) * P], C[k // 4][:, chunk[1]], start=True, stop=True)
                for hd in (2 * k, 2 * k + 1):
                    r = SSM_HD * (hd % 2)
                    e = mm(pm[r:r + SSM_HD, k // 4, o], ident[:, hd:hd + 1].to_broadcast([P, SSM_HD]), H_ACS[:, chunk[1]],
                           start=True, stop=True)
            e.then_inc(sem("hyb_off"), 1)
            pe.wait_ge(sem("hyb_squares"), 1)
            for g in range(2):
                for k in range(4):
                    e = mm(pm[:, 0, g * T:(g + 1) * T], ones[:, :], mix[:, 9, 4 * g + k, :], start=(k == 0), stop=(k == 3))
            e.then_inc(sem("hyb_sums"), 1)
            pe_token_major(pe, mix[:, 5], "turned", s["turn0"] + 4, (sem("hyb_gated"), 1))
            pe.wait_ge(sem("turned_read"), s["turn0"] + 8)
            pe.wait_ge(sem("hyb_rstd"), 1)
            pe_attention(pe, s, 1, mix[:, 3], mix[:, 4], tok(mix[:, 1]),
                         lambda hd: (ident[:, FOX_ROW + hd:FOX_ROW + hd + 1].to_broadcast([P, P]), H_CUM))
            products(s["segs"][3], hs, {0: (sem("cat_lo"), 1)}, second_half=KD, b_wait=(sem("cat_lo"), 2))

        ACT_MIX = {HGRN: act_hgrn, DIFF: act_diff, POOL: act_pool, HYB: act_hyb, REC: act_rec}
        DVE_MIX = {HGRN: dve_hgrn, DIFF: dve_diff, POOL: dve_pool, HYB: dve_hyb, REC: dve_rec}
        PE_MIX = {HGRN: pe_hgrn, DIFF: pe_diff, POOL: pe_pool, HYB: pe_hyb, REC: pe_rec}

        block = ctx.enter_context(nc.Block())

        @block.sync
        def _(sp):
            rows = mix[:, 0].rearrange("p k t -> p (k t)")
            sp.wait_ge(sem("table_cleared"), 1)

            def row(r, src, n=1, c0=0, c=D):
                sp.dma_start(rows[r:r + n, c0:c0 + c], src).then_inc(sem("table_loaded"), 16)
            row(VEC_GAIN1, a["norm_gains"].rearrange("l s d -> (l s) d"), 24)
            row(VEC_GAIN2, a["norm_g_2"].rearrange("l s d -> (l s) d"), 12)
            row(VEC_LB, a["hgrn_lb_raw"], 4)
            row(VEC_POOL_SCALE, a["pool_scale"])
            row(VEC_SSM_NORM, a["ssm_norm_g_2"])
            row(VEC_REC_CONV_W, a["rec_conv_w_2"][0], 4)
            row(VEC_REC_CONV_B, a["rec_conv_b_2"])
            row(VEC_REC_BA, a["rec_b_a_2"])
            row(VEC_REC_BX, a["rec_b_x_2"])
            row(VEC_REC_LAM, a["rec_lambda_2"])
            row(VEC_SSM_CONV_X, a["ssm_conv_w_2"][0][:, 0:D], 4)
            row(VEC_SSM_CONV_BX, a["ssm_conv_b_2"][:, 0:D])
            row(VEC_SSM_CONV_BC, a["ssm_conv_w_2"][0][:, D:D + 512], 4, 0, 512)
            row(VEC_SSM_CONV_BBC, a["ssm_conv_b_2"][:, D:D + 512], 1, 0, 512)
            row(VEC_GNORM, a["hgrn_gnorm"], 2, 0, P)
            row(VEC_SUBLN, a["diff_subln"], 1, 0, P)
            row(VEC_DT_BIAS, a["ssm_dt_bias_2"], 1, 0, 16)
            row(VEC_A_LOG, a["ssm_a_log_2"], 1, 0, 16)
            row(VEC_FOX_B, a["fox_b_f_2"], 1, FOX_ROW, 8)
            sp.dma_start(mix[:, 1].rearrange("p k t -> p (k t)").rearrange("p (a d) -> p a d", a=TT),
                         a["x"][0].rearrange("(a p) d -> p a d", p=P)).then_inc(sem("x_loaded"), 16)
            sp.dma_start(lamrow[:, :], a["diff_lambda"].rearrange("o f d -> o (f d)").to_broadcast([P, 4 * 64])
                         ).then_inc(sem("rows_loaded"), 16)
            sp.dma_start(skiprow[:, :], a["ssm_d_2"].to_broadcast([P, SSM_H])).then_inc(sem("rows_loaded"), 16)

            for seg in flat:
                def load(i, slot, g, seg=seg):
                    if g is not None:
                        sp.wait_ge(sem("weights_hi"), g - 1)
                        sp.wait_ge(sem("weights_lo"), g - 1)
                    sp.dma_start(raw[:, slot, 0:seg.kt * seg.width].rearrange("p (k c) -> p k c", c=seg.width),
                                 seg.source(i, slot)).then_inc(sem("raw_landed_" + "AB"[slot]), 16)
                start = 0
                if seg.g0 == 0:
                    load(0, 0, None)
                    load(0, 1, None)
                    start = 1
                if seg.bodies - start == 1:
                    load(start, 0, seg.g0 + 2 * start)
                    load(start, 1, seg.g0 + 2 * start + 1)
                elif seg.bodies > start:
                    with sp.Fori(start, seg.bodies) as i:
                        load(i, 0, 2 * i + seg.g0)
                        load(i, 1, 2 * i + (seg.g0 + 1))
            for t in range(TT):
                sp.wait_ge(sem("result_ready"), t + 1)
                sp.dma_start(out[0, t * P:(t + 1) * P, :], mix[:, 0].rearrange("p k t -> p (k t)")[:, t * D:(t + 1) * D]
                             ).then_inc(sem("result_stored"), 16)
            sp.wait_ge(sem("result_stored"), 16 * TT)

        @block.gpsimd
        def _(pool):
            pool.memset(mix[:, 0], 0.0).then_inc(sem("table_cleared"), 1)
            pool.memset(ones[:, :], 1.0)
            pool.memset(tri[:, :], 1.0)
            pool.memset(keep[:, :], 1.0)
            pool.memset(causal[:, :, :], 0.0)
            pool.memset(even_tmp, 1.0)
            pool.iota(mix[:, 2, 0:2, :].bitcast(I32), pattern=[[P, TT], [-1, T]], base=0, channel_multiplier=1)
            pool.iota(mix[:, 2, 2, 0:16].bitcast(I32), pattern=[[1, 16]], base=1, channel_multiplier=0)
            pool.memset(eps[:, :], EPS)
            pool.memset(ident[:, :], 0.0)
            pool.drain()
            pool.affine_select(out=ident[:, :], in_=ident[:, :], compare_op=ALU.not_equal, fill=1.0, base=0,
                               pattern=[[-1, P]], channel_multiplier=1)
            pool.affine_select(out=tri[:, :], in_=tri[:, :], compare_op=ALU.is_ge, fill=0.0, base=0,
                               pattern=[[1, P]], channel_multiplier=-1)
            pool.affine_select(out=causal[:, :, :], in_=causal[:, :, :], compare_op=ALU.is_ge, fill=BIG, base=0,
                               pattern=[[P, TT], [-1, T]], channel_multiplier=1)
            pool.memset(keep[:, :].rearrange("p (n t) -> p n t", t=HGB)[:, :, 0:1], 0.0)
            pool.affine_select(out=even_tmp, in_=even_tmp, compare_op=ALU.is_ge, fill=0.0, base=0,
                               pattern=[[-32, 4]], channel_multiplier=1)
            pool.drain()
            pool.affine_select(out=even_tmp, in_=even_tmp, compare_op=ALU.is_ge, fill=0.0, base=HGB - 1,
                               pattern=[[32, 4]], channel_multiplier=-1)
            pool.affine_select(out=block_causal[:, :].rearrange("p (n t) -> p n t", t=HGB),
                               in_=tri[:, :].rearrange("p (n t) -> p n t", t=HGB), compare_op=ALU.is_ge, fill=0.0, base=0,
                               pattern=[[-HGB, P // HGB], [0, HGB]], channel_multiplier=1
                               ).then_inc(sem("constants_ready"), 1)

        @block.scalar
        def _(act):
            def split(slot, landed, cols):
                act.wait_ge(sem("raw_landed_" + "AB"[slot]), landed)
                nc.scalar.activation(whi[:, slot, 0:cols], raw[:, slot, 0:cols], ACT.Copy).then_inc(sem("weights_hi"), 1)

            def square(src, dst, n):
                nc.scalar.activation(dst, src, ACT.Square).then_inc(sem("squares_ready"), 1)

            def rstd(dst, n, width=D):
                act.wait_ge(sem("squares_summed"), n + 1)
                nc.scalar.activation(rln[:, :], psum_stat, ACT.Ln, bias=eps[:, 0:1], scale=1.0 / width)
                act.drain()
                nc.scalar.activation(dst, rln[:, :], ACT.Exp, scale=-0.5).then_inc(sem("rstd_ready"), 1)
                act.drain()

            def open_sublayer(s):
                for half in range(2):
                    act.wait_ge(sem("h_ready"), 2 * s["n"] + half + 1)
                    for k in range(4 * half, 4 * half + 4):
                        e = nc.scalar.activation(xs[:, k, 0:T], h[:, k, :], ACT.Copy, scale=vec[:, k, s["gain"]:s["gain"] + 1])
                    e.then_inc(sem("x_hi"), 1)
                square(h[:, :, :], sq, 2 * s["n"])

            def read_out(seg, s, after_first=None):
                def body(i, nxt):
                    g = 2 * i + seg.g0
                    for slot in range(2):
                        act.wait_ge(sem("panel_done"), g + (slot + 1))
                        nc.scalar.activation(two(corr[:, slot, :]), corr_half(slot), ACT.Copy).then_inc(sem("corr_copied"), 1)
                        if nxt:
                            split(slot, 16 * i + 16 * (seg.g0 // 2 + 2), nxt)
                        if slot == 0 and after_first is not None and isinstance(i, int) and i == 0:
                            after_first()
                        if seg.role == "ffn":
                            f = s["ffn"] * seg.bodies
                            if slot == 0:
                                act.wait_ge(sem("gate_ready"), i + (f + 1))
                                nc.scalar.activation(silu[:, :], gate[:, :], ACT.Silu).then_inc(sem("silu_ready"), 1)
                            else:
                                act.wait_ge(sem("hidden_ready"), i + (f + 1))
                                nc.scalar.activation(hs[:, bass.ds(2 * i, 2), 0:T], two(hid[:, :]), ACT.Copy
                                                     ).then_inc(sem("hidden_hi"), 1)
                seg_loop(act, seg, body, peel_first=after_first is not None)

            for slot in range(2):
                split(slot, 16, flat[0].kt * flat[0].width)
            for s in subs:
                open_sublayer(s)
                segs = s["segs"]
                read_out(segs[0], s, after_first=lambda: rstd(rpre[:, :], 2 * s["n"]))
                if s["kind"] == FFN:
                    read_out(segs[1], s)
                else:
                    ACT_MIX[s["kind"]](act, s, read_out, split, rstd)
                act.wait_ge(sem("panel_out"), segs[-1].g0 + 2 * segs[-1].bodies)
                square(y[:, :, :], sq, 2 * s["n"] + 1)
                rstd(rpost[:, :], 2 * s["n"] + 1)

        @block.vector
        def _(dve):
            v = nc.vector

            def split(slot, count, cols):
                dve.wait_ge(sem("weights_hi"), count)
                v.tensor_tensor(wlo[:, slot, 0:cols], raw[:, slot, 0:cols], whi[:, slot, 0:cols].bitcast(F32),
                                ALU.subtract).then_inc(sem("weights_lo"), 1)

            def open_sublayer(s):
                for half in range(2):
                    dve.wait_ge(sem("x_hi"), 2 * s["fill"] + half + 1)
                    for k in range(4 * half, 4 * half + 4):
                        e = v.scalar_tensor_tensor(xs[:, k, T:2 * T], h[:, k, :], vec[:, k, s["gain"]:s["gain"] + 1],
                                                   xs[:, k, 0:T].bitcast(F32), ALU.mult, ALU.subtract)
                    e.then_inc(sem("x_lo"), 1)

            def close_sublayer(s):
                g = s["gain"] + 1
                dve.wait_ge(sem("rstd_ready"), 2 * s["n"] + 2)
                for half in range(2):
                    ks = range(4 * half, 4 * half + 4)
                    for k in ks:
                        v.scalar_tensor_tensor(upd[:, k, :], y[:, k, :], vec[:, k, g:g + 1], rpost[:, :], ALU.mult, ALU.mult)
                    dve.drain()
                    q = slice(4 * half, 4 * half + 4)
                    v.tensor_tensor(h[:, q, :], h[:, q, :], upd[:, q, :], ALU.add).then_inc(sem("h_ready"), 1)
                dve.drain()

            def read_out(seg, s, dst=None):
                r2 = rpre[:, :].rearrange("p (a t) -> p a t", a=1).to_broadcast([P, 2, T])

                def body(i, nxt):
                    g = 2 * i + seg.g0
                    for slot in range(2):
                        dve.wait_ge(sem("corr_copied"), g + (slot + 1))
                        t = two(tsum[:, slot, :])
                        if seg.role == "out":
                            v.tensor_tensor(y[:, bass.ds(4 * i + 2 * slot, 2), :], main_half(slot), two(corr[:, slot, :]),
                                            ALU.add).then_inc(sem("panel_out"), 1)
                        elif seg.role == "down":
                            if slot == 0:
                                v.tensor_tensor(y[:, bass.ds(2 * i, 2), :], main_half(slot), two(corr[:, slot, :]),
                                                ALU.add).then_inc(sem("panel_out"), 1)
                            else:
                                v.tensor_tensor(t, main_half(slot), two(corr[:, slot, :]), ALU.add)
                                dve.drain()
                                v.tensor_tensor(y[:, bass.ds(2 * i, 2), :], y[:, bass.ds(2 * i, 2), :], t,
                                                ALU.add).then_inc(sem("panel_out"), 1)
                        else:
                            v.tensor_tensor(t, main_half(slot), two(corr[:, slot, :]), ALU.add).then_inc(sem("panel_out"), 1)
                            dve.drain()
                            if seg.role == "ffn":
                                f = s["ffn"] * seg.bodies
                                if slot == 0:
                                    v.tensor_tensor(two(gate[:, :]), t, r2, ALU.mult).then_inc(sem("gate_ready"), 1)
                                else:
                                    v.tensor_tensor(t, t, r2, ALU.mult)
                                    dve.drain()
                                    dve.wait_ge(sem("silu_ready"), i + (f + 1))
                                    v.tensor_tensor(hid[:, :], tsum[:, slot, :], silu[:, :], ALU.mult
                                                    ).then_inc(sem("hidden_ready"), 1)
                            elif seg.role == "small":
                                v.tensor_tensor(dst[slot], tsum[:, slot, slot * T:slot * T + T], rpre[:, :], ALU.mult)
                            else:
                                v.tensor_tensor(dst[:, bass.ds(4 * i + 2 * slot, 2), :], t, r2, ALU.mult)
                        if nxt:
                            split(slot, g + (slot + 3), nxt)
                        if seg.role == "ffn" and slot == 1:
                            dve.wait_ge(sem("hidden_hi"), i + (f + 1))
                            v.tensor_tensor(hs[:, bass.ds(2 * i, 2), T:2 * T], two(hid[:, :]),
                                            hs[:, bass.ds(2 * i, 2), 0:T].bitcast(F32), ALU.subtract
                                            ).then_inc(sem("hidden_lo"), 1)
                            dve.drain()
                seg_loop(dve, seg, body)
                dve.drain()

            for slot in range(2):
                split(slot, slot + 1, flat[0].kt * flat[0].width)
            dve.wait_ge(sem("constants_ready"), 1)
            v.tensor_copy(dist[:, :, :], mix[:, 2, 0:2, :].bitcast(I32))
            v.tensor_copy(steps[:, :], mix[:, 2, 2, 0:16].bitcast(I32))
            v.tensor_reduce(even_odd[:, 0:1], even_tmp, AX_X, ALU.add)
            dve.drain()
            v.tensor_scalar(even_odd[:, 1:2], even_odd[:, 0:1], -1.0, 1.0, ALU.mult, ALU.add)
            v.scalar_tensor_tensor(dist[:, :, :], dist[:, :, :], -1.0, dist[:, :, :], ALU.mult, ALU.max)
            dve.drain()
            for t in range(TT):
                v.memset(dist[0:64, t, t * P + 64:(t + 1) * P], BIG)
            for b in range(2):
                dve.wait_ge(sem("vectors_turned"), b + 1)
                v.tensor_copy(vec[:, 4 * b:4 * b + 4, :],
                              pm[:, b, :].rearrange("p (k r) -> p k r", r=P)[:, :, 0:NVEC])
            dve.drain()
            for g in (1, 5):
                half = vec[:, :, 0:36].rearrange("p k (l s) -> p k l s", s=6)[:, :, :, g]
                e = v.tensor_scalar(half, half, 0.5, None, ALU.mult)
            e.then_inc(sem("vectors_ready"), 1)
            for b in range(4):
                dve.wait_ge(sem("x_turned"), b + 1)
                e = v.tensor_copy(h[:, 2 * b:2 * b + 2, :], two(pp[:, b, :]))
                if b % 2:
                    e.then_inc(sem("h_ready"), 1)
            dve.drain()
            for s in subs:
                open_sublayer(s)
                segs = s["segs"]
                dve.wait_ge(sem("rstd_ready"), 2 * s["n"] + 1)
                if s["kind"] == FFN:
                    read_out(segs[0], s)
                    read_out(segs[1], s)
                else:
                    DVE_MIX[s["kind"]](dve, s, read_out, split)
                close_sublayer(s)
            for t in range(TT):
                for half in range(2):
                    dve.wait_ge(sem("result_turned"), 2 * t + half + 1)
                    e = v.tensor_copy(mix[:, 0].rearrange("p k t -> p (k t)")[:, t * D + half * 512:t * D + half * 512 + 512],
                                      pp[:, half, :])
                e.then_inc(sem("result_ready"), 1)

        @block.tensor
        def _(pe):
            mm = nc.tensor.matmul

            def tile_products(seg, slot, ft, bank, x, k0, x_wait=None):
                for k in range(seg.kt):
                    if x_wait is not None and k in x_wait:
                        pe.wait_ge(*x_wait[k])
                    c = k * PC + ft * P
                    mm(bank, whi[:, slot, c:c + P], x[:, k0 + k, :], start=(k == 0), stop=False)
                    e = mm(bank[:, 0:T], wlo[:, slot, c:c + P], x[:, k0 + k, 0:T], start=False, stop=(k == seg.kt - 1))
                return e

            def products(seg, x, x_wait=None, second_half=0, after_first=None, b_wait=None):
                def body(i, nxt):
                    g = 2 * i + seg.g0
                    first = isinstance(i, int) and i == 0
                    for slot in range(2):
                        pe.wait_ge(sem("weights_lo"), g + (slot + 1))
                        if not (first and seg.g0 == 0):
                            pe.wait_ge(sem("panel_out"), g + (slot - 1))
                        if first and slot == 1 and b_wait is not None:
                            pe.wait_ge(*b_wait)
                        for ft in range(2):
                            e = tile_products(seg, slot, ft, pp[:, 2 * slot + ft, :], x, second_half * slot,
                                              x_wait if first and slot == 0 and ft == 0 else None)
                        e.then_inc(sem("panel_done"), 1)
                        if first and slot == 0 and after_first is not None:
                            after_first()
                peel = x_wait is not None or after_first is not None
                if peel and seg.bodies > 1:
                    body(0, 0)
                    if seg.bodies == 2:
                        body(1, 0)
                    else:
                        with pe.Fori(1, seg.bodies) as i:
                            body(i, 0)
                elif seg.bodies == 1 or peel:
                    body(0, 0)
                else:
                    with pe.Fori(0, seg.bodies) as i:
                        body(i, 0)

            def column_sums(n, tiles=KD):
                pe.wait_ge(sem("squares_ready"), n + 1)
                for k in range(tiles):
                    e = mm(psum_stat, ones[:, :], sq[:, k, :], start=(k == 0), stop=(k == tiles - 1))
                e.then_inc(sem("squares_summed"), 1)

            def x_ready(fill):
                return {0: (sem("x_lo"), 2 * fill + 1), 4: (sem("x_lo"), 2 * fill + 2)}

            pe.wait_ge(sem("constants_ready"), 1)
            pe.wait_ge(sem("table_loaded"), 16 * N_TABLE_LOADS)
            for b in range(2):
                for k in range(4):
                    f = 4 * b + k
                    e = nc.tensor.transpose(pm[:, b, k * P:k * P + NVEC],
                                            mix[:, 0].rearrange("p k t -> p (k t)")[0:NVEC, f * P:f * P + P],
                                            ident[0:NVEC, 0:NVEC])
                e.then_inc(sem("vectors_turned"), 1)
            pe.wait_ge(sem("x_loaded"), 16)
            xin = mix[:, 1].rearrange("p k t -> p (k t)").rearrange("p (a d) -> p a d", a=TT)
            for b in range(4):
                for k in range(2):
                    for t in range(TT):
                        f = 2 * b + k
                        e = nc.tensor.transpose(pp[:, b, k * T + t * P:k * T + t * P + P], xin[:, t, f * P:f * P + P],
                                                ident[:, :])
                e.then_inc(sem("x_turned"), 1)
            pe.wait_ge(sem("h_ready"), 2)
            for s in subs:
                segs = s["segs"]
                products(segs[0], xs, x_ready(s["fill"]), after_first=lambda: column_sums(2 * s["n"]))
                if s["kind"] == FFN:
                    f = s["ffn"] * segs[0].bodies
                    products(segs[1], hs, {0: (sem("hidden_lo"), f + 6)}, second_half=KH,
                             b_wait=(sem("hidden_lo"), f + segs[0].bodies))
                else:
                    PE_MIX[s["kind"]](pe, s, products, x_ready)
                column_sums(2 * s["n"] + 1)
            pe.wait_ge(sem("h_ready"), 2 * len(subs) + 2)
            for t in range(TT):
                for half in range(2):
                    if t:
                        pe.wait_ge(sem("result_ready"), t)
                    for k in range(4):
                        e = nc.tensor.transpose(pp[:, half, k * P:k * P + P], h[:, 4 * half + k, t * P:t * P + P], ident[:, :])
                    e.then_inc(sem("result_turned"), 1)


INS = ["x", "norm_gains", "ffn1_w_in", "ffn1_w_out", "ffn2_w_in", "ffn2_w_out", "hgrn_w_in", "hgrn_gnorm",
       "hgrn_w_out", "hgrn_lb_raw", "diff_w_in", "diff_lambda", "diff_subln", "diff_w_out", "pool_w_in",
       "pool_w_group", "pool_scale", "pool_w_out", "norm_g_2", "ffn_w_in_2", "ffn_w_out_2", "hyb_w_in_2",
       "ssm_conv_w_2", "ssm_conv_b_2", "ssm_dt_bias_2", "ssm_a_log_2", "ssm_d_2", "ssm_norm_g_2", "fox_b_f_2",
       "hyb_w_out_2", "rec_w_in_2", "rec_conv_w_2", "rec_conv_b_2", "rec_w_a_2", "rec_b_a_2", "rec_w_x_2",
       "rec_b_x_2", "rec_lambda_2", "rec_w_out_2"]


def kernel(**inputs):
    import concourse.bacc as bacc
    from concourse.bass_utils import run_bass_kernel_spmd

    nc = bacc.Bacc("TRN2", target_bir_lowering=False, num_devices=1)
    arrays, aps = {}, {}
    for name in INS:
        arrays[name] = np.ascontiguousarray(inputs[name])
        aps[name] = nc.dram_tensor(name, arrays[name].shape, mybir.dt.from_np(arrays[name].dtype),
                                   kind="ExternalInput").ap()
    out = nc.dram_tensor("out", (1, T, D), F32, kind="ExternalOutput").ap()
    build(nc, aps, out)
    return run_bass_kernel_spmd(nc, [arrays], core_ids=[0]).results[0]["out"]
```

```python
import math
from contextlib import ExitStack

import numpy as np

import concourse.bass as bass
import concourse.mybir as mybir
from concourse.alu_op_type import AluOpType as ALU

F32 = mybir.dt.float32
F32R = mybir.dt.float32r
I32 = mybir.dt.int32
ACT = mybir.ActivationFunctionType
AX_X = mybir.AxisListType.X

P = 128
T = 256
TT = T // P
D = 1024
KD = D // P
FF = 2816
KF = FF // P
PC = 256
KH = KF // 2
EPS = 1e-6
SSM_H = 16
HGB = 16
NB = T // HGB
BIG = 1e30

VEC_GAIN1, VEC_GAIN2 = 0, 24
VEC_LB = 36
VEC_POOL_SCALE, VEC_SSM_NORM = 40, 41
VEC_REC_CONV_W, VEC_REC_CONV_B, VEC_REC_BA, VEC_REC_BX, VEC_REC_LAM = 42, 46, 47, 48, 49
VEC_SSM_CONV_X, VEC_SSM_CONV_BX = 50, 54
VEC_SSM_CONV_BC, VEC_SSM_CONV_BBC = 55, 59
VEC_GNORM, VEC_SUBLN, VEC_DT_BIAS, VEC_A_LOG, VEC_FOX_B = 60, 62, 63, 64, 65
NVEC = 66
N_TABLE_LOADS = 19
FOX_ROW = 120

FFN, HGRN, DIFF, POOL, HYB, REC = "ffn", "hgrn", "diff", "pool", "hyb", "rec"


class Segment:

    def __init__(self, role, kt, bodies, source, width=PC):
        self.role, self.kt, self.bodies, self.source, self.width = role, kt, bodies, source, width


def columns(w, first=0):
    def source(i, slot):
        return w[:, bass.ds(first + (2 * i + slot) * PC, PC)].rearrange("(k p) c -> p k c", p=P)
    return source


def gate_and_up(w):
    def source(i, slot):
        return w[:, bass.ds(slot * FF + i * PC, PC)].rearrange("(k p) c -> p k c", p=P)
    return source


def row_halves(w, rows):
    def source(i, slot):
        return w[slot * rows:(slot + 1) * rows, bass.ds(i * PC, PC)].rearrange("(k p) c -> p k c", p=P)
    return source


def build(nc, a, out):
    def ffn(w_in, w_out, gain):
        return dict(kind=FFN, gain=gain, segs=[
            Segment("ffn", KD, FF // PC, gate_and_up(w_in)),
            Segment("down", KH, D // PC, row_halves(w_out, FF // 2))])

    def out_proj(w):
        return Segment("out", KD, D // PC // 2, columns(w))

    subs = []
    for l in range(4):
        g = VEC_GAIN1 + 6 * l
        subs.append(ffn(a["ffn1_w_in"][l], a["ffn1_w_out"][l], g))
        if l % 3 == 0:
            j = l // 3
            subs.append(dict(kind=HGRN, gain=g + 2, layer=l, j=j, segs=[
                Segment("proj", KD, 4 * D // (2 * PC), columns(a["hgrn_w_in"][j])), out_proj(a["hgrn_w_out"][j])]))
        elif l == 1:
            subs.append(dict(kind=DIFF, gain=g + 2, layer=l, segs=[
                Segment("proj", KD, 3 * D // (2 * PC), columns(a["diff_w_in"][0])), out_proj(a["diff_w_out"][0])]))
        else:
            wg = a["pool_w_group"][0]
            subs.append(dict(kind=POOL, gain=g + 2, segs=[
                Segment("proj", KD, D // (2 * PC), columns(a["pool_w_in"][0])),
                Segment("group", 4, 1, lambda i, slot: wg[2 * slot:2 * slot + 2].rearrange("g (t p) c -> p (g t) c", p=P)),
                out_proj(a["pool_w_out"][0])]))
        subs.append(ffn(a["ffn2_w_in"][l], a["ffn2_w_out"][l], g + 4))
    for l in range(2):
        g = VEC_GAIN2 + 6 * l
        subs.append(ffn(a["ffn_w_in_2"][l, 0], a["ffn_w_out_2"][l, 0], g))
        if l == 0:
            w = a["hyb_w_in_2"][0]
            n_zx, n_qkv = 1024 + 1536, 3 * D
            subs.append(dict(kind=HYB, gain=g + 2, segs=[
                Segment("proj", KD, n_zx // (2 * PC), columns(w)),
                Segment("small", KD, 1, lambda i, slot: w[:, (n_zx, n_zx + 16 + n_qkv + 8 - PC)[slot]:][:, 0:PC].rearrange(
                    "(k p) c -> p k c", p=P)),
                Segment("proj2", KD, n_qkv // (2 * PC), columns(w, n_zx + 16)),
                Segment("down", KD, D // PC, row_halves(a["hyb_w_out_2"][0], D))]))
        else:
            wa, wx = a["rec_w_a_2"][0], a["rec_w_x_2"][0]
            subs.append(dict(kind=REC, gain=g + 2, segs=[
                Segment("proj", KD, 2 * D // (2 * PC), columns(a["rec_w_in_2"][0])),
                Segment("block", KD, 1, lambda i, slot: (wa, wx)[slot].rearrange("n p c -> p n c"), width=P),
                out_proj(a["rec_w_out_2"][0])]))
        subs.append(ffn(a["ffn_w_in_2"][l, 1], a["ffn_w_out_2"][l, 1], g + 4))
    panels = fills = ffns = downs = 0
    turned = head_norms = items = log1ps = hgrns = 0
    flat = []
    for n, s in enumerate(subs):
        s["n"], s["fill"] = n, fills
        fills += {FFN: 1, HYB: 1, HGRN: 2, DIFF: 2, POOL: 3, REC: 3}[s["kind"]]
        s["turn0"], s["hn0"], s["att0"], s["ls0"], s["it"] = turned, head_norms, items, log1ps, hgrns
        turned += {HGRN: 8, HYB: 8, DIFF: 4}.get(s["kind"], 0)
        head_norms += s["kind"] in (HGRN, DIFF)
        items += 16 * (s["kind"] in (DIFF, HYB))
        log1ps += {HYB: 2, REC: 1}.get(s["kind"], 0)
        hgrns += s["kind"] == HGRN
        if s["kind"] == FFN:
            s["ffn"] = ffns
            ffns += 1
        for seg in s["segs"]:
            seg.g0 = panels
            panels += 2 * seg.bodies
            flat.append(seg)
            if seg.role == "down":
                seg.d0 = downs
                downs += seg.bodies
    for seg, nxt in zip(flat, flat[1:] + [None]):
        seg.next = nxt

    ctx = ExitStack()
    with ctx:
        def sb(name, shape, dt=F32):
            return ctx.enter_context(nc.sbuf_tensor(name, shape, dt))

        sems = {}

        def sem(name):
            if name not in sems:
                sems[name] = ctx.enter_context(nc.semaphore(name))
            return sems[name]

        raw = sb("raw", [P, 2, KH * PC])
        whi = sb("whi", [P, 2, KH * PC], F32R)
        wlo = sb("wlo", [P, 2, KH * PC], F32R)
        xs = sb("xs", [P, KD, 2 * T], F32R)
        h = sb("h", [P, KD, T])
        y = sb("y", [P, KD, T])
        corr = sb("corr", [P, 2, 2 * T])
        tsum = sb("tsum", [P, 2, 2 * T])
        gate = sb("gate", [P, 2 * T])
        silu = sb("silu", [P, 2 * T])
        hid = sb("hid", [P, 2 * T])
        rpre = sb("rpre", [P, T])
        rpost = sb("rpost", [P, T])
        rln = sb("rln", [P, T])
        vec = sb("vec", [P, KD, NVEC])
        ones = sb("ones", [P, P])
        ident = sb("ident", [P, P])
        eps = sb("eps", [P, 1])
        MB = 10
        small = sb("small", [P, 8])
        lbw = sb("lbw", [P, KD, 6])
        rec_col = sb("rec_col", [P, 6, KD])
        dist = sb("dist", [P, TT, T])
        causal = sb("causal", [P, TT, T])
        tri = sb("tri", [P, P])
        block_causal = sb("block_causal", [P, P])
        keep = sb("keep", [P, T])
        even_odd = sb("even_odd", [P, 2])
        steps = sb("steps", [P, 16])
        lamrow = sb("lamrow", [P, 4 * 64])
        skiprow = sb("skiprow", [P, SSM_H])
        mix_offset = nc.sbuf_base
        mix = sb("mix", [P, MB, KD, T])
        hs = nc.alloc_sbuf_tensor_at("hs", [P, KF, 2 * T], F32R, offset=mix_offset)
        even_tmp = mix[:, 2, 3, 0:4]
        sq = mix[:, MB - 1]
        upd = mix[:, MB - 2]

        pp = ctx.enter_context(nc.psum_tensor("pp", [P, 4, 2 * T], F32))
        pm = ctx.enter_context(nc.psum_tensor("pm", [P, 4, 2 * T], F32))
        psum_stat = pm[:, 3, 0:T]

        def main_half(slot):
            return pp[:, 2 * slot:2 * slot + 2, 0:T]

        def corr_half(slot):
            return pp[:, 2 * slot:2 * slot + 2, T:2 * T]

        def two(buf):
            return buf.rearrange("p (a t) -> p a t", a=2)

        def seg_loop(eng, seg, body, peel_first=False, unroll=False):
            nxt = 0 if seg.next is None else seg.next.kt * seg.next.width
            mine = seg.kt * seg.width
            if unroll:
                for i in range(seg.bodies):
                    body(i, nxt if i == seg.bodies - 1 else mine)
                return
            first = 1 if peel_first else 0
            last = seg.bodies - (nxt != mine)
            if last <= first:
                for i in range(seg.bodies):
                    body(i, nxt if i == seg.bodies - 1 else mine)
                return
            if peel_first:
                body(0, mine)
            if last - first == 1:
                body(first, mine)
            else:
                with eng.Fori(first, last) as i:
                    body(i, mine)
            if nxt != mine:
                body(seg.bodies - 1, nxt)

        def fill_hi(act, fill, src, gain=None):
            for pair in range(4):
                if gain is None:
                    q = slice(2 * pair, 2 * pair + 2)
                    e = nc.scalar.activation(xs[:, q, 0:T], src[:, q, :], ACT.Copy)
                else:
                    for k in (2 * pair, 2 * pair + 1):
                        e = nc.scalar.activation(xs[:, k, 0:T], src[:, k, :], ACT.Copy, scale=vec[:, k, gain:gain + 1])
                e.then_inc(sem("x_hi"), 1)

        def fill_lo(dve, fill, src, gain=None):
            for pair in range(4):
                dve.wait_ge(sem("x_hi"), 4 * fill + pair + 1)
                if gain is None:
                    q = slice(2 * pair, 2 * pair + 2)
                    e = nc.vector.tensor_tensor(xs[:, q, T:2 * T], src[:, q, :], xs[:, q, 0:T].bitcast(F32), ALU.subtract)
                else:
                    for k in (2 * pair, 2 * pair + 1):
                        e = nc.vector.scalar_tensor_tensor(xs[:, k, T:2 * T], src[:, k, :], vec[:, k, gain:gain + 1],
                                                           xs[:, k, 0:T].bitcast(F32), ALU.mult, ALU.subtract)
                e.then_inc(sem("x_lo"), 1)

        def act_log1p(act, n, e, w, ln):
            act.wait_ge(sem("log1p_negabs"), n + 1)
            nc.scalar.activation(e, e, ACT.Exp).then_inc(sem("log1p_exp"), 1)
            act.wait_ge(sem("log1p_w"), n + 1)
            nc.scalar.activation(ln, w, ACT.Ln).then_inc(sem("log1p_ln"), 1)

        def dve_log1p(dve, n, x, e, w, c, ln):
            v = nc.vector
            v.scalar_tensor_tensor(e, x, -1.0, x, ALU.mult, ALU.min).then_inc(sem("log1p_negabs"), 1)
            dve.wait_ge(sem("log1p_exp"), n + 1)
            v.tensor_scalar(w, e, 1.0, None, ALU.add).then_inc(sem("log1p_w"), 1)
            dve.drain()
            v.tensor_scalar(c, w, -1.0, None, ALU.add)
            dve.drain()
            v.tensor_tensor(c, e, c, ALU.subtract)
            dve.drain()
            v.reciprocal(e, w)
            dve.drain()
            v.tensor_tensor(c, c, e, ALU.mult)
            dve.drain()
            dve.wait_ge(sem("log1p_ln"), n + 1)
            v.tensor_tensor(ln, ln, c, ALU.add)
            dve.drain()

        def flat2(buf):
            return buf.rearrange("p k t -> p (k t)")

        def tok(buf):
            return flat2(buf).rearrange("p (a d) -> p a d", a=TT)

        def act_head_norm(act, n, o, r):
            act.wait_ge(sem("head_out"), n + 1)
            nc.scalar.activation(sq, o, ACT.Square).then_inc(sem("head_squares"), 1)
            act.wait_ge(sem("head_sums"), n + 1)
            nc.scalar.activation(r.rearrange("p (b k) t -> p b (k t)", b=4), pm[:, :, :], ACT.Ln, bias=eps[:, 0:1], scale=1.0 / P)
            act.drain()
            nc.scalar.activation(r, r, ACT.Exp, scale=-0.5).then_inc(sem("head_rstd"), 1)

        def pe_head_norm(pe, n):
            pe.wait_ge(sem("head_squares"), n + 1)
            for b in range(4):
                e = nc.tensor.matmul(pm[:, b, :], ones[:, :], flat2(sq)[:, b * 2 * T:(b + 1) * 2 * T], start=True, stop=True)
            e.then_inc(sem("head_sums"), 1)

        att_s = mix[:, 8].rearrange("p (w j g) t -> p w j g t", w=2, j=2)
        att_w = mix[:, 9, 0:2, :]
        att_wT = mix[:, 9, 2:4, :]
        att_small = mix[:, 9, 4, :].rearrange("p (j c) -> p j c", j=2)

        def pe_attention(pe, s, groups, Q, K, Vt, row_term=None):
            n0, dg = s["att0"], P // groups
            mm = nc.tensor.matmul

            def scores(it):
                hd, qt = it // 2, it % 2
                nk = (qt + 1) * P
                if it >= 2:
                    pe.wait_ge(sem("att_scores_read"), n0 + it - 1)
                for g in range(groups):
                    bank = pm[:, 2 * (it % 2) + g, 0:nk]
                    e = mm(bank, Q[g * dg:(g + 1) * dg, hd, qt * P:(qt + 1) * P], K[g * dg:(g + 1) * dg, hd, 0:nk],
                           start=True, stop=row_term is None)
                if row_term is not None:
                    lhsT, rhs = row_term(hd)
                    e = mm(pm[:, 2 * (it % 2), 0:nk], lhsT, rhs[:, 0:nk], start=False, stop=True)
                e.then_inc(sem("att_scores"), 1)

            def turn(it):
                pe.wait_ge(sem("att_weights"), n0 + it + 1)
                for k in range(it % 2 + 1):
                    e = nc.tensor.transpose(pp[:, 2 + it % 2, k * P:(k + 1) * P], att_w[:, it % 2, k * P:(k + 1) * P], ident[:, :])
                e.then_inc(sem("att_turned"), 1)

            def values(it):
                hd, qt = it // 2, it % 2
                pe.wait_ge(sem("att_wT"), n0 + it + 1)
                if qt == 0 and hd >= 2:
                    pe.wait_ge(sem("att_out_read"), n0 // 2 + hd - 1)
                for k in range(qt + 1):
                    e = mm(pp[:, hd % 2, qt * P:(qt + 1) * P], Vt[:, k, hd * P:(hd + 1) * P], att_wT[:, it % 2, k * P:(k + 1) * P],
                           start=(k == 0), stop=(k == qt))
                e.then_inc(sem("att_out"), 1)

            scores(0)
            for it in range(16):
                if it < 15:
                    scores(it + 1)
                turn(it)
                values(it)

        def act_attention(act, s, groups, scale):
            n0 = s["att0"]
            for it in range(16):
                j, nk = it % 2, (it % 2 + 1) * P
                act.wait_ge(sem("att_max"), n0 + it + 1)
                for g in range(groups):
                    e = nc.scalar.activation(att_s[:, 1, j, g, 0:nk], att_s[:, 0, j, g, 0:nk], ACT.Exp, scale=scale,
                                             bias=att_small[:, j, g:g + 1], accum_out=att_small[:, j, 2 + g:3 + g])
                e.then_inc(sem("att_exp"), 1)
                act.wait_ge(sem("att_turned"), n0 + it + 1)
                nc.scalar.activation(att_wT[:, j, 0:nk], pp[:, 2 + j, 0:nk], ACT.Copy).then_inc(sem("att_wT"), 1)

        def dve_attention(dve, s, groups, scale, bias, factor, o, second=None):
            v, n0 = nc.vector, s["att0"]

            def maxima(it):
                hd, j, nk = it // 2, it % 2, (it % 2 + 1) * P
                dve.wait_ge(sem("att_scores"), n0 + it + 1)
                if groups == 2:
                    b = bias[:, j, 0:nk].rearrange("p (a k) -> p a k", a=1).to_broadcast([P, 2, nk])
                    v.scalar_tensor_tensor(att_s[:, 0, j, :, 0:nk], b, factor(hd), pm[:, 2 * j:2 * j + 2, 0:nk],
                                           ALU.mult, ALU.add).then_inc(sem("att_scores_read"), 1)
                else:
                    v.scalar_tensor_tensor(att_s[:, 0, j, 0, 0:nk], bias[:, j, 0:nk], factor(hd), pm[:, 2 * j, 0:nk],
                                           ALU.mult, ALU.add).then_inc(sem("att_scores_read"), 1)
                dve.drain()
                v.tensor_reduce(att_small[:, j, 4:4 + groups], att_s[:, 0, j, 0:groups, 0:nk], AX_X, ALU.max)
                dve.drain()
                v.tensor_scalar(att_small[:, j, 0:groups], att_small[:, j, 4:4 + groups], -scale, None, ALU.mult
                                ).then_inc(sem("att_max"), 1)

            def weights(it):
                j, nk = it % 2, (it % 2 + 1) * P
                dve.wait_ge(sem("att_exp"), n0 + it + 1)
                v.reciprocal(att_small[:, j, 4:4 + groups], att_small[:, j, 2:2 + groups])
                dve.drain()
                e = v.tensor_scalar(att_w[:, j, 0:nk], att_s[:, 1, j, 0, 0:nk], att_small[:, j, 4:5], None, ALU.mult)
                if groups == 2:
                    v.tensor_tensor(att_small[:, j, 6:7], att_small[:, j, 5:6], second, ALU.mult)
                    dve.drain()
                    e = v.scalar_tensor_tensor(att_w[:, j, 0:nk], att_s[:, 1, j, 1, 0:nk], att_small[:, j, 6:7],
                                               att_w[:, j, 0:nk], ALU.mult, ALU.add)
                e.then_inc(sem("att_weights"), 1)

            def take(hd):
                dve.wait_ge(sem("att_out"), n0 + 2 * hd + 2)
                v.tensor_copy(o[:, hd, :], pp[:, hd % 2, 0:T]).then_inc(sem("att_out_read"), 1)

            maxima(0)
            for it in range(16):
                if it < 15:
                    maxima(it + 1)
                weights(it)
                if it % 2 == 1 and it >= 3:
                    take(it // 2 - 1)
            take(7)
            dve.drain()

        def pe_token_major(pe, src, name, count0, ready):
            pe.wait_ge(*ready)
            for b in range(4):
                t, half = b // 2, b % 2
                for k in range(4):
                    e = nc.tensor.transpose(pp[:, b, k * P:(k + 1) * P], src[:, 4 * half + k, t * P:(t + 1) * P], ident[:, :])
                e.then_inc(sem(name), 1)

        R_GATE, R_X, R_CONV, R_CORR, R_R, R_I, R_A, R_TH = (mix[:, b] for b in range(8))

        def act_rec(act, s, read_out, split, rstd):
            seg = s["segs"][1]
            n_cols = seg.next.kt * seg.next.width
            act_log1p(act, s["ls0"], rec_col[:, 0, :], rec_col[:, 1, :], rec_col[:, 3, :])
            act.wait_ge(sem("rec_conv"), 1)
            fill_hi(act, s["fill"] + 1, R_CONV)
            for slot, (dst, bias_row) in enumerate(((R_R, VEC_REC_BA), (R_I, VEC_REC_BX))):
                act.wait_ge(sem("panel_done"), seg.g0 + slot + 1)
                nc.scalar.activation(R_CORR[:, 0:4, :], pp[:, :, T:2 * T], ACT.Copy)
                nc.scalar.activation(R_CORR[:, 4:8, :], pm[:, :, T:2 * T], ACT.Copy).then_inc(sem("corr_copied"), 1)
                split(slot, 16 * (seg.g0 // 2 + 2), n_cols)
                act.wait_ge(sem("panel_out"), seg.g0 + slot + 1)
                for k in range(KD):
                    e = nc.scalar.activation(dst[:, k, :], dst[:, k, :], ACT.Sigmoid, bias=vec[:, k, bias_row:bias_row + 1])
                e.then_inc(sem("rec_sigmoid"), 1)
            act.wait_ge(sem("rec_lambda"), 1)
            act.drain()
            for k in range(KD):
                nc.scalar.activation(R_TH[:, k, :], R_R[:, k, :], ACT.Tanh, scale=rec_col[:, 4, k:k + 1])
            for k in range(KD):
                e = nc.scalar.activation(R_A[:, k, :], R_R[:, k, :], ACT.Exp, scale=rec_col[:, 4, k:k + 1])
            e.then_inc(sem("rec_a"), 1)
            act.wait_ge(sem("rec_one_minus_a2"), 1)
            nc.scalar.activation(R_TH, R_TH, ACT.Sqrt, scale=-1.0).then_inc(sem("rec_sqrt"), 1)
            nc.scalar.activation(R_GATE, R_GATE, ACT.Gelu_apprx_tanh).then_inc(sem("rec_gelu"), 1)
            act.wait_ge(sem("rec_gated"), 1)
            fill_hi(act, s["fill"] + 2, R_A)
            read_out(s["segs"][2], s)

        def dve_rec(dve, s, read_out, split):
            v, seg = nc.vector, s["segs"][1]
            read_out(s["segs"][0], s, mix[:, 0:2].rearrange("p b k t -> p (b k) t"))
            dve_conv(dve, R_CONV, R_X, range(KD), VEC_REC_CONV_W, VEC_REC_CONV_B)
            v.tensor_copy(rec_col[:, 5, :], vec[:, :, VEC_REC_LAM]).then_inc(sem("rec_conv"), 1)
            dve.drain()
            dve_log1p(dve, s["ls0"], rec_col[:, 5, :], rec_col[:, 0, :], rec_col[:, 1, :], rec_col[:, 2, :], rec_col[:, 3, :])
            v.scalar_tensor_tensor(rec_col[:, 4, :], rec_col[:, 5, :], 0.0, rec_col[:, 3, :], ALU.min, ALU.subtract)
            dve.drain()
            v.tensor_scalar(rec_col[:, 4, :], rec_col[:, 4, :], 8.0, None, ALU.mult).then_inc(sem("rec_lambda"), 1)
            fill_lo(dve, s["fill"] + 1, R_CONV)
            for slot, dst in enumerate((R_R, R_I)):
                dve.wait_ge(sem("corr_copied"), seg.g0 + slot + 1)
                v.tensor_tensor(dst[:, 0:4, :], pp[:, :, 0:T], R_CORR[:, 0:4, :], ALU.add)
                v.tensor_tensor(dst[:, 4:8, :], pm[:, :, 0:T], R_CORR[:, 4:8, :], ALU.add).then_inc(sem("panel_out"), 1)
                split(slot, seg.g0 + slot + 3, seg.next.kt * seg.next.width)
            dve.wait_ge(sem("rec_sigmoid"), 2)
            v.tensor_tensor(R_I, R_I, R_CONV, ALU.mult)
            dve.wait_ge(sem("rec_a"), 1)
            v.tensor_tensor(R_R, R_A, R_A, ALU.mult)
            dve.drain()
            v.scalar_tensor_tensor(R_TH, R_R, 1.0, R_TH, ALU.add, ALU.mult).then_inc(sem("rec_one_minus_a2"), 1)
            v.memset(R_A[:, :, 0:1], 0.0)
            dve.wait_ge(sem("rec_sqrt"), 1)
            v.tensor_tensor(R_I, R_I, R_TH, ALU.mult)
            dve.drain()
            v.tensor_tensor_scan(flat2(R_R), flat2(R_A), flat2(R_I), 0.0, ALU.mult, ALU.add)
            dve.drain()
            dve.wait_ge(sem("rec_gelu"), 1)
            v.tensor_tensor(R_A, R_R, R_GATE, ALU.mult).then_inc(sem("rec_gated"), 1)
            fill_lo(dve, s["fill"] + 2, R_A)
            read_out(s["segs"][2], s)

        def pe_rec(pe, s, products, last_products, out_products):
            seg = s["segs"][1]
            pe.wait_ge(sem("x_lo"), 4 * s["fill"] + 8)
            for slot in range(2):
                pe.wait_ge(sem("weights_lo"), seg.g0 + slot + 1)
                pe.wait_ge(sem("panel_out"), seg.g0 + slot)
                for n in range(KD):
                    bank = pp[:, n, :] if n < 4 else pm[:, n - 4, :]
                    nc.tensor.matmul(bank, whi[:, slot, n * P:(n + 1) * P], xs[:, n, :], start=True, stop=False)
                    e = nc.tensor.matmul(bank[:, 0:T], wlo[:, slot, n * P:(n + 1) * P], xs[:, n, 0:T], start=False, stop=True)
                e.then_inc(sem("panel_done"), 1)
            out_products(s, s["fill"] + 2)

        def dve_conv(dve, dst, src, tiles, w_row, b_row, vec_tile=lambda k: k):
            v = nc.vector
            for k in tiles:
                q = vec_tile(k)
                v.tensor_scalar(dst[:, k, :], src[:, k, :], vec[:, q, w_row + 3:w_row + 4], vec[:, q, b_row:b_row + 1],
                                ALU.mult, ALU.add)
            for j in (2, 1, 0):
                d = 3 - j
                dve.drain()
                for k in tiles:
                    q = vec_tile(k)
                    v.scalar_tensor_tensor(dst[:, k, d:T], src[:, k, 0:T - d], vec[:, q, w_row + j:w_row + j + 1],
                                           dst[:, k, d:T], ALU.mult, ALU.add)
            dve.drain()

        def act_pool(act, s, read_out, split, rstd):
            seg = s["segs"][1]
            act.wait_ge(sem("pool_means"), 1)
            fill_hi(act, s["fill"] + 1, mix[:, 4])
            for slot in range(2):
                act.wait_ge(sem("panel_done"), seg.g0 + slot + 1)
                nc.scalar.activation(mix[:, 5, 4 * slot:4 * slot + 4, :], (pp, pm)[slot][:, :, T:2 * T], ACT.Copy
                                     ).then_inc(sem("corr_copied"), 1)
                split(slot, 16 * (seg.g0 // 2 + 2), seg.next.kt * seg.next.width)
            act.wait_ge(sem("panel_out"), seg.g0 + 2)
            fill_hi(act, s["fill"] + 2, mix[:, 4], VEC_POOL_SCALE)
            read_out(s["segs"][2], s)

        def dve_pool(dve, s, read_out, split):
            v, seg = nc.vector, s["segs"][1]
            U, W1, W2, RC, PO = (mix[:, b] for b in range(5))
            read_out(s["segs"][0], s, U)
            for g in range(4):
                v.memset(RC[:, g, :], 1.0 / 2 ** (g + 1))
                v.tensor_scalar(RC[:, 4 + g, 0:16], steps[:, :], float(2 ** (g + 1)), None, ALU.min)
            dve.drain()
            v.reciprocal(RC[:, 0:4, 0:16], RC[:, 4:8, 0:16])
            for dst, src, k0, d in ((W1, U, 0, 1), (W2, W1, 2, 2), (W1, W2, 4, 4), (W2, W1, 6, 8)):
                v.tensor_copy(dst[:, k0:, 0:d], src[:, k0:, 0:d])
                v.tensor_tensor(dst[:, k0:, d:T], src[:, k0:, d:T], src[:, k0:, 0:T - d], ALU.add)
                dve.drain()
            for g, W in enumerate((W1, W2, W1, W2)):
                v.tensor_tensor(PO[:, 2 * g:2 * g + 2, :], W[:, 2 * g:2 * g + 2, :], RC[:, g:g + 1, :].to_broadcast([P, 2, T]),
                                ALU.mult)
            dve.drain()
            v.tensor_tensor(PO, PO, U, ALU.subtract).then_inc(sem("pool_means"), 1)
            fill_lo(dve, s["fill"] + 1, PO)
            for slot in range(2):
                dve.wait_ge(sem("corr_copied"), seg.g0 + slot + 1)
                q = slice(4 * slot, 4 * slot + 4)
                v.tensor_tensor(PO[:, q, :], (pp, pm)[slot][:, :, 0:T], mix[:, 5, q, :], ALU.add).then_inc(sem("panel_out"), 1)
                split(slot, seg.g0 + slot + 3, seg.next.kt * seg.next.width)
            fill_lo(dve, s["fill"] + 2, PO, VEC_POOL_SCALE)
            read_out(s["segs"][2], s)

        def pe_pool(pe, s, products, last_products, out_products):
            seg = s["segs"][1]
            pe.wait_ge(sem("x_lo"), 4 * s["fill"] + 8)
            for slot in range(2):
                pe.wait_ge(sem("weights_lo"), seg.g0 + slot + 1)
                pe.wait_ge(sem("panel_out"), seg.g0 + slot)
                for n in range(4):
                    bank = (pp, pm)[slot][:, n, :]
                    for t in range(2):
                        c = (2 * (n // 2) + t) * PC + (n % 2) * P
                        k = 2 * (2 * slot + n // 2) + t
                        nc.tensor.matmul(bank, whi[:, slot, c:c + P], xs[:, k, :], start=(t == 0), stop=False)
                        e = nc.tensor.matmul(bank[:, 0:T], wlo[:, slot, c:c + P], xs[:, k, 0:T], start=False, stop=(t == 1))
                e.then_inc(sem("panel_done"), 1)
            out_products(s, s["fill"] + 2)

        DA_SCALE = 64 ** -0.5

        def act_diff(act, s, read_out, split, rstd):
            act.wait_ge(sem("diff_lambda_sums"), 1)
            nc.scalar.activation(small[:, 2:4], small[:, 0:2], ACT.Exp).then_inc(sem("diff_lambda_exp"), 1)
            for b in range(4):
                act.wait_ge(sem("turned"), s["turn0"] + b + 1)
                nc.scalar.activation(tok(mix[:, 3])[:, b // 2, 512 * (b % 2):512 * (b % 2) + 512], pp[:, b, :], ACT.Copy
                                     ).then_inc(sem("turned_read"), 1)
            act_attention(act, s, 2, DA_SCALE)
            act_head_norm(act, s["hn0"], mix[:, 4], mix[:, 5])
            act.wait_ge(sem("heads_done"), s["hn0"] + 1)
            fill_hi(act, s["fill"] + 1, mix[:, 4])
            read_out(s["segs"][1], s)

        def dve_diff(dve, s, read_out, split):
            v = nc.vector
            lam_init = 0.8 - 0.6 * math.exp(-0.3 * s["layer"])
            read_out(s["segs"][0], s, mix[:, 0:3].rearrange("p b k t -> p (b k) t"))
            dve.wait_ge(sem("rows_loaded"), 32)
            lam = lamrow[:, :].rearrange("p (a b d) -> p a b d", a=2, b=2)
            v.tensor_tensor(tsum[:, 0, 0:128].rearrange("p (a d) -> p a d", a=2), lam[:, :, 0, :], lam[:, :, 1, :], ALU.mult
                            ).then_inc(sem("diff_projected"), 1)
            dve.drain()
            v.tensor_reduce(small[:, 0:2], tsum[:, 0, 0:128].rearrange("p (a d) -> p a d", a=2), AX_X, ALU.add
                            ).then_inc(sem("diff_lambda_sums"), 1)
            dve.wait_ge(sem("diff_lambda_exp"), 1)
            v.tensor_tensor(small[:, 4:5], small[:, 3:4], small[:, 2:3], ALU.subtract)
            dve.drain()
            v.tensor_scalar(small[:, 5:6], small[:, 4:5], -lam_init, None, ALU.add)
            dve.drain()
            slope = [2.0 ** (-8.0 * (hd + 1) / 8) for hd in range(8)]
            dve_attention(dve, s, 2, DA_SCALE, dist, lambda hd: -slope[hd] / DA_SCALE, mix[:, 4], small[:, 5:6])
            v.tensor_scalar(small[:, 6:7], vec[:, 0, VEC_SUBLN:VEC_SUBLN + 1], 1.0 - lam_init, None, ALU.mult
                            ).then_inc(sem("head_out"), 1)
            dve.drain()
            dve.wait_ge(sem("head_rstd"), s["hn0"] + 1)
            v.scalar_tensor_tensor(mix[:, 4], mix[:, 4], small[:, 6:7], mix[:, 5], ALU.mult, ALU.mult
                                   ).then_inc(sem("heads_done"), 1)
            fill_lo(dve, s["fill"] + 1, mix[:, 4])
            read_out(s["segs"][1], s)

        def pe_diff(pe, s, products, last_products, out_products):
            pe_token_major(pe, mix[:, 2], "turned", s["turn0"], (sem("diff_projected"), 1))
            pe.wait_ge(sem("turned_read"), s["turn0"] + 4)
            pe_attention(pe, s, 2, mix[:, 0], mix[:, 1], tok(mix[:, 3]))
            pe_head_norm(pe, s["hn0"])
            out_products(s, s["fill"] + 1)

        def act_hgrn(act, s, read_out, split, rstd):
            Q, F, V, G, K, D1, B, QR, VT, KO = (mix[:, b] for b in range(10))
            it = s["it"] + 1
            if s["layer"] > 0:
                act.wait_ge(sem("lower_bound_shifted"), 1)
                nc.scalar.activation(lbw[:, :, 0:4], lbw[:, :, 0:4], ACT.Exp).then_inc(sem("lower_bound_exp"), 1)
            act.wait_ge(sem("hgrn_projected"), it)
            nc.scalar.activation(F, F, ACT.Sigmoid).then_inc(sem("hgrn_sigmoid"), 1)
            act.wait_ge(sem("turned"), s["turn0"] + 4)
            for b in range(4):
                e = nc.scalar.activation(tok(VT)[:, b // 2, 512 * (b % 2):512 * (b % 2) + 512], pp[:, b, :], ACT.Copy)
                e.then_inc(sem("turned_read"), 1)
            act.wait_ge(sem("hgrn_forget"), it)
            nc.scalar.activation(D1, F, ACT.Ln).then_inc(sem("hgrn_log"), 1)
            act.wait_ge(sem("hgrn_differences"), it)
            nc.scalar.activation(QR, D1, ACT.Exp).then_inc(sem("hgrn_exp"), 1)
            act.drain()
            nc.scalar.activation(D1, D1, ACT.Exp, scale=-1.0).then_inc(sem("hgrn_exp"), 1)
            nc.scalar.activation(B, B, ACT.Exp).then_inc(sem("hgrn_exp"), 1)
            nc.scalar.activation(F, F, ACT.Exp).then_inc(sem("hgrn_exp"), 1)
            nc.scalar.activation(G, G, ACT.Silu).then_inc(sem("hgrn_silu"), 1)
            act_head_norm(act, s["hn0"], D1, QR)
            act.wait_ge(sem("heads_done"), s["hn0"] + 1)
            fill_hi(act, s["fill"] + 1, D1)
            read_out(s["segs"][1], s)

        def dve_hgrn(dve, s, read_out, split):
            v = nc.vector
            Q, F, V, G, K, D1, B, QR, VT, KO = (mix[:, b] for b in range(10))
            it = s["it"] + 1
            read_out(s["segs"][0], s, mix[:, 0:4].rearrange("p b k t -> p (b k) t"))
            v.memset(small[:, 0:1], 0.0).then_inc(sem("hgrn_projected"), 1)
            if s["layer"] == 0:
                v.memset(lbw[:, :, 4:5], 0.0)
            else:
                rows = vec[:, :, VEC_LB:VEC_LB + 4]
                v.tensor_reduce(lbw[:, :, 4:5], rows, AX_X, ALU.max)
                dve.drain()
                v.tensor_tensor(lbw[:, :, 0:4], rows, lbw[:, :, 4:5].to_broadcast([P, KD, 4]), ALU.subtract
                                ).then_inc(sem("lower_bound_shifted"), 1)
                dve.wait_ge(sem("lower_bound_exp"), 1)
                v.tensor_reduce(lbw[:, :, 4:5], lbw[:, :, 0:4], AX_X, ALU.add)
                v.tensor_reduce(lbw[:, :, 5:6], lbw[:, :, 1:s["layer"] + 1], AX_X, ALU.add)
                dve.drain()
                v.reciprocal(lbw[:, :, 4:5], lbw[:, :, 4:5])
                dve.drain()
                v.tensor_tensor(lbw[:, :, 4:5], lbw[:, :, 4:5], lbw[:, :, 5:6], ALU.mult)
            dve.drain()
            v.tensor_scalar(lbw[:, :, 5:6], lbw[:, :, 4:5], -1.0, 1.0, ALU.mult, ALU.add)
            dve.drain()
            dve.wait_ge(sem("hgrn_sigmoid"), it)
            for k in range(KD):
                e = v.tensor_scalar(F[:, k, :], F[:, k, :], lbw[:, k, 5:6], lbw[:, k, 4:5], ALU.mult, ALU.add)
            e.then_inc(sem("hgrn_forget"), 1)
            dve.drain()
            v.tensor_scalar(K, F, -1.0, 1.0, ALU.mult, ALU.add)
            dve.wait_ge(sem("hgrn_log"), it)
            for k in range(KD):
                v.tensor_tensor_scan(B[:, k, :], keep[:, :], D1[:, k, :], 0.0, ALU.mult, ALU.add)
            dve.drain()
            blk = lambda buf: flat2(buf).rearrange("p (n t) -> p n t", t=HGB)
            n_blk = KD * NB
            v.tensor_tensor(blk(D1), blk(B), blk(B)[:, :, HGB // 2:HGB // 2 + 1].to_broadcast([P, n_blk, HGB]), ALU.subtract)
            v.tensor_tensor(blk(F), blk(B)[:, :, HGB - 1:HGB].to_broadcast([P, n_blk, HGB]), blk(B), ALU.subtract
                            ).then_inc(sem("hgrn_differences"), 1)
            for n, (dst, src, e) in enumerate(((QR, Q, QR), (D1, K, D1), (Q, Q, B), (K, K, F))):
                dve.wait_ge(sem("hgrn_exp"), 4 * (it - 1) + n + 1)
                v.tensor_tensor(dst, src, e, ALU.mult).then_inc(sem("hgrn_operand"), 1)
            for b in range(4):
                dve.wait_ge(sem("turned"), s["turn0"] + 4 + b + 1)
                o = slice(512 * (b % 2), 512 * (b % 2) + 512)
                v.tensor_scalar(tok(F)[:, b // 2, o], pp[:, b, :], even_odd[:, 0:1], None, ALU.mult)
                v.tensor_scalar(tok(KO)[:, b // 2, o], pp[:, b, :], even_odd[:, 1:2], None, ALU.mult
                                ).then_inc(sem("turned_read"), 1)
            AT = flat2(V).rearrange("p (n c) -> p n c", c=P)
            v.memset(V, 0.0)
            dve.drain()
            for b in range(4):
                dve.wait_ge(sem("hgrn_scores"), 4 * (it - 1) + b + 1)
                for j in range(4):
                    e = v.copy_predicated(AT[:, 4 * b + j, :], block_causal[:, :].bitcast(I32), pm[:, b, j * P:(j + 1) * P])
                e.then_inc(sem("hgrn_masked"), 1)
            S = flat2(K).rearrange("p (j c) -> p j c", j=2)
            for n in range(NB - 1):
                dve.wait_ge(sem("hgrn_update"), (NB - 1) * (it - 1) + n + 1)
                for hd in range(8):
                    u = pm[:, 2 * (n % 2) + hd // 4, (hd % 4) * P:(hd % 4) * P + P]
                    o = slice(hd * P, hd * P + P)
                    if n == 0:
                        e = v.tensor_copy(S[:, 1, o], u)
                    else:
                        c = HGB * n + HGB - 1
                        e = v.scalar_tensor_tensor(S[:, (n + 1) % 2, o], S[:, n % 2, o], B[:, hd, c:c + 1], u, ALU.mult, ALU.add)
                e.then_inc(sem("hgrn_state"), 1)
                dve.drain()
            dve.wait_ge(sem("hgrn_out"), it)
            v.tensor_copy(D1.rearrange("p (b k) t -> p b (k t)", b=4), pp[:, :, :]).then_inc(sem("head_out"), 1)
            dve.drain()
            dve.wait_ge(sem("hgrn_silu"), it)
            dve.wait_ge(sem("head_rstd"), s["hn0"] + 1)
            j = VEC_GNORM + s["j"]
            v.scalar_tensor_tensor(D1, D1, vec[:, 0, j:j + 1], QR, ALU.mult, ALU.mult)
            dve.drain()
            v.tensor_tensor(D1, D1, G, ALU.mult).then_inc(sem("heads_done"), 1)
            fill_lo(dve, s["fill"] + 1, D1)
            read_out(s["segs"][1], s)

        def pe_hgrn(pe, s, products, last_products, out_products):
            mm = nc.tensor.matmul
            Q, F, V, G, K, D1, B, QR, VT, KO = (mix[:, b] for b in range(10))
            i0 = s["it"]
            pe_token_major(pe, V, "turned", s["turn0"], (sem("hgrn_projected"), i0 + 1))
            pe.wait_ge(sem("hgrn_operand"), 4 * i0 + 4)
            pe.wait_ge(sem("turned_read"), s["turn0"] + 4)
            pe_token_major(pe, K, "turned", s["turn0"] + 4, (sem("hgrn_operand"), 4 * i0 + 4))
            for b in range(4):
                for j in range(4):
                    hd, t = (4 * b + j) // 2, j % 2
                    o = slice(t * P, t * P + P)
                    e = mm(pm[:, b, j * P:(j + 1) * P], D1[:, hd, o], QR[:, hd, o], start=True, stop=True)
                e.then_inc(sem("hgrn_scores"), 1)
            AT = flat2(V).rearrange("p (n c) -> p n c", c=P)
            out_cols = lambda hd, a, b: pp[:, hd // 2, (hd % 2) * T + a:(hd % 2) * T + b]
            pe.wait_ge(sem("turned_read"), s["turn0"] + 8)
            for hd in range(8):
                if hd % 2 == 0:
                    pe.wait_ge(sem("hgrn_masked"), 4 * i0 + hd // 2 + 1)
                for t in range(TT):
                    mm(out_cols(hd, t * P, t * P + P), tok(VT)[:, t, hd * P:hd * P + P], AT[:, 2 * hd + t, :],
                       start=(hd % 2 == 0 and t == 0), stop=False, skip_group_check=True)
            S = flat2(K).rearrange("p (j c) -> p j c", j=2)
            for n in range(NB):
                t, nb = n // 8, n % 8
                rows = slice(32 * (nb // 2), 32 * (nb // 2) + 32)
                kt = tok((F, KO)[nb % 2])
                if n < NB - 1:
                    if n >= 2:
                        pe.wait_ge(sem("hgrn_state"), (NB - 1) * i0 + n - 1)
                    for hd in range(8):
                        e = mm(pm[:, 2 * (n % 2) + hd // 4, (hd % 4) * P:(hd % 4) * P + P],
                               kt[rows, t, hd * P:hd * P + P], tok(VT)[rows, t, hd * P:hd * P + P], start=True, stop=True)
                    e.then_inc(sem("hgrn_update"), 1)
                if n >= 1:
                    pe.wait_ge(sem("hgrn_state"), (NB - 1) * i0 + n)
                    for hd in range(8):
                        e = mm(out_cols(hd, HGB * n, HGB * n + HGB), S[:, n % 2, hd * P:hd * P + P],
                               Q[:, hd, HGB * n:HGB * n + HGB], start=False, stop=(n == NB - 1), skip_group_check=True)
            e.then_inc(sem("hgrn_out"), 1)
            pe_head_norm(pe, s["hn0"])
            out_products(s, s["fill"] + 1)
        FOX_SCALE = P ** -0.5
        SSM_HD = D // SSM_H
        H_DT, H_F = mix[:, 2, 4, :], mix[:, 2, 5, :]
        H_ACS, H_CUM = mix[:, 7, 4, :], mix[:, 7, 5, :]
        H_COLS = mix[:, 7, 6, 0:64].rearrange("p (a h) -> p a h", a=4)
        H_LAST, H_DECAY = mix[:, 7, 6, 64:80], mix[:, 7, 6, 80:96]
        H_CB = flat2(mix[:, 8])[:, 0:512].rearrange("p (g t) -> p g t", g=2)
        H_BT = flat2(mix[:, 8])[:, 512:768]
        H_XD = flat2(mix[:, 2])[:, 0:D]
        H_ST = flat2(mix[:, 9])[:, 0:D]
        H_YO = flat2(mix[:, 9])[:, D:2 * D]

        def seg_decay(hd):
            return mix[:, 8, 3 + hd % 2, :]

        def seg_weight(hd):
            return mix[:, 8, 5 + hd % 2, :]

        def act_hyb(act, s, read_out, split, rstd):
            read_out(s["segs"][1], s)
            read_out(s["segs"][2], s)
            act.wait_ge(sem("hyb_conv"), 1)
            nc.scalar.activation(mix[:, 6], mix[:, 6], ACT.Silu)
            nc.scalar.activation(mix[:, 7, 0:4, :], mix[:, 7, 0:4, :], ACT.Silu)
            nc.scalar.activation(mix[:, 0], mix[:, 0], ACT.Silu).then_inc(sem("hyb_silu"), 1)
            nc.scalar.activation(small[:, 0:1], vec[:, 0, VEC_A_LOG:VEC_A_LOG + 1], ACT.Exp).then_inc(sem("hyb_a"), 1)
            for n in range(2):
                act_log1p(act, s["ls0"] + n, mix[:, 9, 4 * n, :], mix[:, 9, 4 * n + 1, :], mix[:, 9, 4 * n + 3, :])
            act.wait_ge(sem("hyb_decay_log"), 1)
            nc.scalar.activation(H_DECAY, H_DECAY, ACT.Exp).then_inc(sem("hyb_decay"), 1)
            act.wait_ge(sem("hyb_states"), 1)
            nc.scalar.activation(H_ST.rearrange("p (g c) -> p g c", g=2), pm[:, 2:4, :], ACT.Copy).then_inc(sem("hyb_states_read"), 1)
            for hd in range(SSM_H):
                act.wait_ge(sem("seg_log"), hd + 1)
                nc.scalar.activation(seg_decay(hd), seg_decay(hd), ACT.Exp).then_inc(sem("seg_exp"), 1)
            act.wait_ge(sem("hyb_off"), 1)
            act.wait_ge(sem("seg_weights"), SSM_H)
            nc.scalar.activation(flat2(mix[:, 8])[:, 0:D].rearrange("p (g c) -> p g c", g=2), pm[:, 0:2, :], ACT.Exp
                                 ).then_inc(sem("hyb_decay_out"), 1)
            act.wait_ge(sem("hyb_gated"), 1)
            nc.scalar.activation(mix[:, 9], mix[:, 6], ACT.Square).then_inc(sem("hyb_squares"), 1)
            act.wait_ge(sem("hyb_sums"), 1)
            nc.scalar.activation(corr[:, 0, :], pm[:, 0, :], ACT.Ln, bias=eps[:, 0:1], scale=1.0 / 512)
            act.drain()
            nc.scalar.activation(corr[:, 0, :], corr[:, 0, :], ACT.Exp, scale=-0.5).then_inc(sem("hyb_rstd"), 1)
            for b in range(4):
                act.wait_ge(sem("turned"), s["turn0"] + 4 + b + 1)
                nc.scalar.activation(tok(mix[:, 1])[:, b // 2, 512 * (b % 2):512 * (b % 2) + 512], pp[:, b, :], ACT.Copy
                                     ).then_inc(sem("turned_read"), 1)
            act_attention(act, s, 1, FOX_SCALE)
            act.wait_ge(sem("att_out_read"), (s["att0"] + 16) // 2)
            for k in range(KD):
                e = nc.scalar.activation(hs[:, k, 0:T], mix[:, 6, k, :], ACT.Copy, scale=vec[:, k, VEC_SSM_NORM:VEC_SSM_NORM + 1])
            e.then_inc(sem("cat_hi"), 1)
            nc.scalar.activation(hs[:, KD:2 * KD, 0:T], y[:, :, :], ACT.Copy).then_inc(sem("cat_hi"), 1)
            read_out(s["segs"][3], s)

        def dve_hyb(dve, s, read_out, split):
            v = nc.vector
            read_out(s["segs"][0], s, mix[:, 0:3].rearrange("p b k t -> p (b k) t"))
            read_out(s["segs"][1], s, (H_DT, H_F))
            read_out(s["segs"][2], s, mix[:, 3:6].rearrange("p b k t -> p (b k) t"))
            dve_conv(dve, mix[:, 6], mix[:, 1], range(KD), VEC_SSM_CONV_X, VEC_SSM_CONV_BX)
            dve_conv(dve, mix[:, 7], mix[:, 2], range(4), VEC_SSM_CONV_BC, VEC_SSM_CONV_BBC)
            v.tensor_scalar(H_DT, H_DT, vec[:, 0, VEC_DT_BIAS:VEC_DT_BIAS + 1], None, ALU.add)
            v.tensor_scalar(H_F, H_F, vec[:, 0, VEC_FOX_B:VEC_FOX_B + 1], None, ALU.add).then_inc(sem("hyb_conv"), 1)
            dve.drain()
            for n, x in enumerate((H_DT, H_F)):
                dve_log1p(dve, s["ls0"] + n, x, *(mix[:, 9, 4 * n + j, :] for j in range(4)))
            v.scalar_tensor_tensor(H_DT, H_DT, 0.0, mix[:, 9, 3, :], ALU.max, ALU.add)
            v.scalar_tensor_tensor(H_F, H_F, 0.0, mix[:, 9, 7, :], ALU.min, ALU.subtract)
            dve.drain()
            dve.wait_ge(sem("hyb_a"), 1)
            v.tensor_scalar(mix[:, 9, 0, :], H_DT, small[:, 0:1], -1.0, ALU.mult, ALU.mult)
            dve.drain()
            for c in range(TT):
                o = slice(c * P, c * P + P)
                v.tensor_tensor_scan(H_ACS[:, o], ones[:, :], mix[:, 9, 0, o], 0.0, ALU.mult, ALU.add)
                v.tensor_tensor_scan(mix[:, 9, 1, o], ones[:, :], H_F[:, o], mix[:, 9, 1, P - 1:P] if c else 0.0,
                                     ALU.mult, ALU.add)
                dve.drain()
            v.tensor_scalar(H_CUM, mix[:, 9, 1, :], -1.0 / FOX_SCALE, None, ALU.mult).then_inc(sem("hyb_scans"), 1)
            dve.wait_ge(sem("hyb_cols"), 1)
            v.tensor_copy(H_COLS, pm[:, 0, :].rearrange("p (a r) -> p a r", a=4)[:, :, 0:SSM_H])
            v.tensor_copy(H_LAST, pm[:, 1, 0:SSM_H])
            dve.drain()
            v.tensor_tensor(H_DECAY, H_LAST, H_COLS[:, 2, :], ALU.subtract).then_inc(sem("hyb_decay_log"), 1)
            dve.wait_ge(sem("hyb_cb"), 1)
            v.tensor_tensor(flat2(mix[:, 8])[:, 0:512].rearrange("p (n t) -> p n t", n=4),
                            pm[:, 3, :].rearrange("p (n t) -> p n t", n=4),
                            tri[:, :].rearrange("p (a t) -> p a t", a=1).to_broadcast([P, 4, P]), ALU.mult)
            v.tensor_copy(H_BT, pm[:, 2, 0:256]).then_inc(sem("hyb_cb_read"), 1)
            for b in range(4):
                t, half = b // 2, b % 2
                dve.wait_ge(sem("turned"), s["turn0"] + b + 1)
                v.tensor_tensor(tok(mix[:, 1])[:, t, 512 * half:512 * half + 512].rearrange("p (h d) -> p h d", h=8),
                                pp[:, b, :].rearrange("p (h d) -> p h d", h=8),
                                H_COLS[:, t, 8 * half:8 * half + 8].rearrange("p (h a) -> p h a", a=1).to_broadcast([P, 8, SSM_HD]),
                                ALU.mult).then_inc(sem("turned_read"), 1)
            dve.drain()
            dve.wait_ge(sem("hyb_decay"), 1)
            v.tensor_tensor(H_XD.rearrange("p (h d) -> p h d", h=SSM_H),
                            tok(mix[:, 1])[:, 0, :].rearrange("p (h d) -> p h d", h=SSM_H),
                            H_DECAY.rearrange("p (h a) -> p h a", a=1).to_broadcast([P, SSM_H, SSM_HD]),
                            ALU.mult).then_inc(sem("hyb_x"), 1)

            def difference(hd):
                dve.wait_ge(sem("seg_sums"), hd + 1)
                for c in range(TT):
                    o = slice(c * P, c * P + P)
                    e = v.tensor_scalar(seg_decay(hd)[:, o], pm[:, hd % 2, o], H_COLS[:, 2 + c, hd:hd + 1], 0.0,
                                        ALU.subtract, ALU.min)
                e.then_inc(sem("seg_log"), 1)

            difference(0)
            for hd in range(SSM_H):
                if hd < SSM_H - 1:
                    difference(hd + 1)
                dve.wait_ge(sem("seg_exp"), hd + 1)
                if hd >= 2:
                    dve.wait_ge(sem("seg_out"), hd - 1)
                v.tensor_tensor(seg_weight(hd), seg_decay(hd), H_CB[:, hd // 8, :], ALU.mult).then_inc(sem("seg_weights"), 1)
            dve.wait_ge(sem("rows_loaded"), 32)
            v.tensor_copy(rec_col[0:64, 5, :], skiprow[0:64, 0::2])
            v.tensor_copy(rec_col[64:P, 5, :], skiprow[64:P, 1::2])
            dve.drain()
            dve.wait_ge(sem("seg_out"), SSM_H)
            for k in range(KD):
                v.scalar_tensor_tensor(mix[:, 6, k, :], mix[:, 6, k, :], rec_col[:, 5, k:k + 1],
                                       pp[:, k // 2, (k % 2) * T:(k % 2) * T + T], ALU.mult, ALU.add)
            dve.wait_ge(sem("hyb_decay_out"), 1)
            v.tensor_tensor(H_YO.rearrange("p (g c) -> p g c", g=2), pm[:, 2:4, :],
                            flat2(mix[:, 8])[:, 0:D].rearrange("p (g c) -> p g c", g=2), ALU.mult)
            dve.drain()
            v.tensor_tensor(mix[:, 6, :, P:T], mix[:, 6, :, P:T], H_YO.rearrange("p (k t) -> p k t", k=KD), ALU.add)
            dve.drain()
            v.tensor_tensor(mix[:, 6], mix[:, 6], mix[:, 0], ALU.mult).then_inc(sem("hyb_gated"), 1)
            dve.drain()
            dve.wait_ge(sem("hyb_rstd"), 1)
            for g in range(2):
                v.tensor_tensor(mix[:, 6, 4 * g:4 * g + 4, :], mix[:, 6, 4 * g:4 * g + 4, :],
                                corr[:, 0, g * T:g * T + T].rearrange("p (a t) -> p a t", a=1).to_broadcast([P, 4, T]), ALU.mult)
            dve.drain()
            dve_attention(dve, s, 1, FOX_SCALE, causal, lambda hd: -1.0, y)
            for k in range(KD):
                if k == 0:
                    dve.wait_ge(sem("cat_hi"), 1)
                e = v.scalar_tensor_tensor(hs[:, k, T:2 * T], mix[:, 6, k, :], vec[:, k, VEC_SSM_NORM:VEC_SSM_NORM + 1],
                                           hs[:, k, 0:T].bitcast(F32), ALU.mult, ALU.subtract)
            e.then_inc(sem("cat_lo"), 1)
            dve.wait_ge(sem("cat_hi"), 2)
            v.tensor_tensor(hs[:, KD:2 * KD, T:2 * T], y[:, :, :], hs[:, KD:2 * KD, 0:T].bitcast(F32), ALU.subtract
                            ).then_inc(sem("cat_lo"), 1)
            dve.drain()
            read_out(s["segs"][3], s)

        def pe_hyb(pe, s, products, last_products, out_products):
            mm = nc.tensor.matmul
            products(s["segs"][1], xs)
            products(s["segs"][2], xs)
            B = [mix[:, 7, g, :] for g in range(2)]
            C = [mix[:, 7, 2 + g, :] for g in range(2)]
            chunk = [slice(0, P), slice(P, T)]
            pe.wait_ge(sem("hyb_scans"), 1)
            for n, src in enumerate((H_DT, H_DT, H_ACS, H_ACS)):
                nc.tensor.transpose(pm[:, 0, n * P:(n + 1) * P], src[:, chunk[n % 2]], ident[:, :])
            mm(pm[:, 1, 0:SSM_H], H_ACS[:, P - 1:P].to_broadcast([P, P]), ident[:, 0:SSM_H], start=True, stop=True
               ).then_inc(sem("hyb_cols"), 1)
            pe.wait_ge(sem("hyb_silu"), 1)
            for g in range(2):
                nc.tensor.transpose(pm[:, 2, g * P:(g + 1) * P], B[g][:, chunk[0]], ident[:, :])
                for c in range(TT):
                    e = mm(pm[:, 3, (2 * g + c) * P:(2 * g + c + 1) * P], B[g][:, chunk[c]], C[g][:, chunk[c]],
                           start=True, stop=True)
            e.then_inc(sem("hyb_cb"), 1)
            pe_token_major(pe, mix[:, 6], "turned", s["turn0"], (sem("hyb_silu"), 1))
            pe.wait_ge(sem("hyb_cb_read"), 1)
            pe.wait_ge(sem("hyb_x"), 1)
            for g in range(2):
                e = mm(pm[:, 2 + g, :], H_BT[:, g * P:(g + 1) * P], H_XD[:, g * 512:(g + 1) * 512], start=True, stop=True)
            e.then_inc(sem("hyb_states"), 1)

            def sums_on_all(hd):
                if hd >= 2:
                    pe.wait_ge(sem("seg_log"), hd - 1)
                mm(pm[:, hd % 2, 0:T], ident[:, hd:hd + 1].to_broadcast([P, P]), H_ACS, start=True, stop=True
                   ).then_inc(sem("seg_sums"), 1)

            sums_on_all(0)
            for hd in range(SSM_H):
                if hd < SSM_H - 1:
                    sums_on_all(hd + 1)
                pe.wait_ge(sem("seg_weights"), hd + 1)
                k, r = hd // 2, SSM_HD * (hd % 2)
                for c in range(TT):
                    e = mm(pp[r:r + SSM_HD, k // 2, (k % 2) * T + c * P:(k % 2) * T + (c + 1) * P],
                           tok(mix[:, 1])[:, c, hd * SSM_HD:(hd + 1) * SSM_HD], seg_weight(hd)[:, chunk[c]], start=True, stop=True)
                e.then_inc(sem("seg_out"), 1)
            pe.wait_ge(sem("hyb_states_read"), 1)
            pe.wait_ge(sem("seg_log"), SSM_H)
            for k in range(KD):
                o = slice((k % 4) * P, (k % 4) * P + P)
                mm(pm[:, 2 + k // 4, o], H_ST[:, k * P:(k + 1) * P], C[k // 4][:, chunk[1]], start=True, stop=True)
                for hd in (2 * k, 2 * k + 1):
                    r = SSM_HD * (hd % 2)
                    e = mm(pm[r:r + SSM_HD, k // 4, o], ident[:, hd:hd + 1].to_broadcast([P, SSM_HD]), H_ACS[:, chunk[1]],
                           start=True, stop=True)
            e.then_inc(sem("hyb_off"), 1)
            pe.wait_ge(sem("hyb_squares"), 1)
            for g in range(2):
                for k in range(4):
                    e = mm(pm[:, 0, g * T:(g + 1) * T], ones[:, :], mix[:, 9, 4 * g + k, :], start=(k == 0), stop=(k == 3))
            e.then_inc(sem("hyb_sums"), 1)
            pe_token_major(pe, mix[:, 5], "turned", s["turn0"] + 4, (sem("hyb_gated"), 1))
            pe.wait_ge(sem("turned_read"), s["turn0"] + 8)
            pe.wait_ge(sem("hyb_rstd"), 1)
            pe_attention(pe, s, 1, mix[:, 3], mix[:, 4], tok(mix[:, 1]),
                         lambda hd: (ident[:, FOX_ROW + hd:FOX_ROW + hd + 1].to_broadcast([P, P]), H_CUM))
            last_products(s, hs, x_wait=(sem("cat_lo"), 1), second_half=KD, b_wait=(sem("cat_lo"), 2))

        ACT_MIX = {HGRN: act_hgrn, DIFF: act_diff, POOL: act_pool, HYB: act_hyb, REC: act_rec}
        DVE_MIX = {HGRN: dve_hgrn, DIFF: dve_diff, POOL: dve_pool, HYB: dve_hyb, REC: dve_rec}
        PE_MIX = {HGRN: pe_hgrn, DIFF: pe_diff, POOL: pe_pool, HYB: pe_hyb, REC: pe_rec}

        block = ctx.enter_context(nc.Block())

        @block.sync
        def _(sp):
            rows = mix[:, 0].rearrange("p k t -> p (k t)")
            sp.wait_ge(sem("table_cleared"), 1)

            def row(r, src, n=1, c0=0, c=D):
                sp.dma_start(rows[r:r + n, c0:c0 + c], src).then_inc(sem("table_loaded"), 16)
            row(VEC_GAIN1, a["norm_gains"].rearrange("l s d -> (l s) d"), 24)
            row(VEC_GAIN2, a["norm_g_2"].rearrange("l s d -> (l s) d"), 12)
            row(VEC_LB, a["hgrn_lb_raw"], 4)
            row(VEC_POOL_SCALE, a["pool_scale"])
            row(VEC_SSM_NORM, a["ssm_norm_g_2"])
            row(VEC_REC_CONV_W, a["rec_conv_w_2"][0], 4)
            row(VEC_REC_CONV_B, a["rec_conv_b_2"])
            row(VEC_REC_BA, a["rec_b_a_2"])
            row(VEC_REC_BX, a["rec_b_x_2"])
            row(VEC_REC_LAM, a["rec_lambda_2"])
            row(VEC_SSM_CONV_X, a["ssm_conv_w_2"][0][:, 0:D], 4)
            row(VEC_SSM_CONV_BX, a["ssm_conv_b_2"][:, 0:D])
            row(VEC_SSM_CONV_BC, a["ssm_conv_w_2"][0][:, D:D + 512], 4, 0, 512)
            row(VEC_SSM_CONV_BBC, a["ssm_conv_b_2"][:, D:D + 512], 1, 0, 512)
            row(VEC_GNORM, a["hgrn_gnorm"], 2, 0, P)
            row(VEC_SUBLN, a["diff_subln"], 1, 0, P)
            row(VEC_DT_BIAS, a["ssm_dt_bias_2"], 1, 0, 16)
            row(VEC_A_LOG, a["ssm_a_log_2"], 1, 0, 16)
            row(VEC_FOX_B, a["fox_b_f_2"], 1, FOX_ROW, 8)
            sp.dma_start(mix[:, 1].rearrange("p k t -> p (k t)").rearrange("p (a d) -> p a d", a=TT),
                         a["x"][0].rearrange("(a p) d -> p a d", p=P)).then_inc(sem("x_loaded"), 16)
            sp.dma_start(lamrow[:, :], a["diff_lambda"].rearrange("o f d -> o (f d)").to_broadcast([P, 4 * 64])
                         ).then_inc(sem("rows_loaded"), 16)
            sp.dma_start(skiprow[:, :], a["ssm_d_2"].to_broadcast([P, SSM_H])).then_inc(sem("rows_loaded"), 16)

            for seg in flat:
                def load(i, slot, g, seg=seg):
                    if g is not None:
                        sp.wait_ge(sem("weights_hi"), g - 1)
                        sp.wait_ge(sem("weights_lo"), g - 1)
                    sp.dma_start(raw[:, slot, 0:seg.kt * seg.width].rearrange("p (k c) -> p k c", c=seg.width),
                                 seg.source(i, slot)).then_inc(sem("raw_landed_" + "AB"[slot]), 16)
                start = 0
                if seg.g0 == 0:
                    load(0, 0, None)
                    load(0, 1, None)
                    start = 1
                if seg.bodies - start == 1:
                    load(start, 0, seg.g0 + 2 * start)
                    load(start, 1, seg.g0 + 2 * start + 1)
                elif seg.bodies > start:
                    with sp.Fori(start, seg.bodies) as i:
                        load(i, 0, 2 * i + seg.g0)
                        load(i, 1, 2 * i + (seg.g0 + 1))
            for t in range(TT):
                sp.wait_ge(sem("result_ready"), t + 1)
                sp.dma_start(out[0, t * P:(t + 1) * P, :], mix[:, 0].rearrange("p k t -> p (k t)")[:, t * D:(t + 1) * D]
                             ).then_inc(sem("result_stored"), 16)
            sp.wait_ge(sem("result_stored"), 16 * TT)

        @block.gpsimd
        def _(pool):
            pool.memset(mix[:, 0], 0.0).then_inc(sem("table_cleared"), 1)
            pool.memset(ones[:, :], 1.0)
            pool.memset(tri[:, :], 1.0)
            pool.memset(keep[:, :], 1.0)
            pool.memset(causal[:, :, :], 0.0)
            pool.memset(even_tmp, 1.0)
            pool.iota(mix[:, 2, 0:2, :].bitcast(I32), pattern=[[P, TT], [-1, T]], base=0, channel_multiplier=1)
            pool.iota(mix[:, 2, 2, 0:16].bitcast(I32), pattern=[[1, 16]], base=1, channel_multiplier=0)
            pool.memset(eps[:, :], EPS)
            pool.memset(ident[:, :], 0.0)
            pool.drain()
            pool.affine_select(out=ident[:, :], in_=ident[:, :], compare_op=ALU.not_equal, fill=1.0, base=0,
                               pattern=[[-1, P]], channel_multiplier=1)
            pool.affine_select(out=tri[:, :], in_=tri[:, :], compare_op=ALU.is_ge, fill=0.0, base=0,
                               pattern=[[1, P]], channel_multiplier=-1)
            pool.affine_select(out=causal[:, :, :], in_=causal[:, :, :], compare_op=ALU.is_ge, fill=BIG, base=0,
                               pattern=[[P, TT], [-1, T]], channel_multiplier=1)
            pool.memset(keep[:, :].rearrange("p (n t) -> p n t", t=HGB)[:, :, 0:1], 0.0)
            pool.affine_select(out=even_tmp, in_=even_tmp, compare_op=ALU.is_ge, fill=0.0, base=0,
                               pattern=[[-32, 4]], channel_multiplier=1)
            pool.drain()
            pool.affine_select(out=even_tmp, in_=even_tmp, compare_op=ALU.is_ge, fill=0.0, base=HGB - 1,
                               pattern=[[32, 4]], channel_multiplier=-1)
            pool.affine_select(out=block_causal[:, :].rearrange("p (n t) -> p n t", t=HGB),
                               in_=tri[:, :].rearrange("p (n t) -> p n t", t=HGB), compare_op=ALU.is_ge, fill=0.0, base=0,
                               pattern=[[-HGB, P // HGB], [0, HGB]], channel_multiplier=1
                               ).then_inc(sem("constants_ready"), 1)

        @block.scalar
        def _(act):
            def split(slot, landed, cols):
                act.wait_ge(sem("raw_landed_" + "AB"[slot]), landed)
                nc.scalar.activation(whi[:, slot, 0:cols], raw[:, slot, 0:cols], ACT.Copy).then_inc(sem("weights_hi"), 1)

            def rstd(dst, n, width=D):
                act.wait_ge(sem("squares_summed"), n + 1)
                nc.scalar.activation(rln[:, :], psum_stat, ACT.Ln, bias=eps[:, 0:1], scale=1.0 / width)
                act.drain()
                nc.scalar.activation(dst, rln[:, :], ACT.Exp, scale=-0.5).then_inc(sem("rstd_ready"), 1)

            def split_pair(n, pair):
                if pair == 0:
                    act.wait_ge(sem("raw_landed_B"), 16 * (subs[n + 1]["segs"][0].g0 // 2 + 1))
                o = slice(2 * pair * PC, (2 * pair + 2) * PC)
                nc.scalar.activation(whi[:, 1, o], raw[:, 1, o], ACT.Copy
                                     ).then_inc(sem("weights_hi" if pair == 3 else "first_b_hi"), 1)

            def open_sublayer(s):
                for pair in range(4):
                    act.wait_ge(sem("h_ready"), 4 * s["n"] + pair + 1)
                    for k in (2 * pair, 2 * pair + 1):
                        e = nc.scalar.activation(xs[:, k, 0:T], h[:, k, :], ACT.Copy, scale=vec[:, k, s["gain"]:s["gain"] + 1])
                    e.then_inc(sem("x_hi"), 1)
                nc.scalar.activation(sq, h[:, :, :], ACT.Square).then_inc(sem("squares_ready"), 1)

            def square_output(s, pair):
                out_seg = s["segs"][-1]
                act.wait_ge(sem("panel_out"), out_seg.g0 + (pair + 1) * out_seg.bodies // 2)
                nc.scalar.activation(sq[:, 2 * pair:2 * pair + 2, :], y[:, 2 * pair:2 * pair + 2, :], ACT.Square
                                     ).then_inc(sem("squares_ready"), 1)

            def scale_output(s, pair):
                g = s["gain"] + 1
                for k in (2 * pair, 2 * pair + 1):
                    e = nc.scalar.activation(upd[:, k, :], y[:, k, :], ACT.Copy, scale=vec[:, k, g:g + 1])
                e.then_inc(sem("output_scaled"), 1)

            def close_sublayer(s):
                more = s["n"] + 1 < len(subs)
                if more:
                    split_pair(s["n"], 0)
                square_output(s, 3)
                if more:
                    split_pair(s["n"], 1)
                    split_pair(s["n"], 2)
                rstd(rpost[:, :], 2 * s["n"] + 1)
                if more:
                    split_pair(s["n"], 3)
                scale_output(s, 3)

            def read_out(seg, s, after_first=None):
                closing = seg is s["segs"][-1]
                if closing:
                    nc.scalar.preload_act_table_set("natural_log_exp_and_others")

                def body(i, nxt):
                    g = 2 * i + seg.g0
                    for slot in range(2):
                        act.wait_ge(sem("panel_done"), g + (slot + 1))
                        nc.scalar.activation(two(corr[:, slot, :]), corr_half(slot), ACT.Copy).then_inc(sem("corr_copied"), 1)
                        if closing and i == seg.bodies - 1 and slot == 1:
                            break
                        if nxt:
                            split(slot, 16 * i + 16 * (seg.g0 // 2 + 2), nxt)
                        if closing and (seg.bodies == 2 or slot == 1):
                            pair = 2 * i + slot if seg.bodies == 2 else i
                            square_output(s, pair)
                            scale_output(s, pair)
                        if slot == 0 and after_first is not None and isinstance(i, int) and i == 0:
                            after_first()
                        if seg.role == "ffn":
                            f = s["ffn"] * seg.bodies
                            if slot == 0:
                                act.wait_ge(sem("gate_ready"), i + (f + 1))
                                nc.scalar.activation(silu[:, :], gate[:, :], ACT.Silu).then_inc(sem("silu_ready"), 1)
                            else:
                                act.wait_ge(sem("hidden_ready"), i + (f + 1))
                                nc.scalar.activation(hs[:, bass.ds(2 * i, 2), 0:T], two(hid[:, :]), ACT.Copy
                                                     ).then_inc(sem("hidden_hi"), 1)
                seg_loop(act, seg, body, peel_first=after_first is not None, unroll=closing)

            for slot in range(2):
                split(slot, 16, flat[0].kt * flat[0].width)
            nc.scalar.preload_act_table_set("natural_log_exp_and_others")
            for s in subs:
                open_sublayer(s)
                segs = s["segs"]
                read_out(segs[0], s, after_first=lambda: rstd(rpre[:, :], 2 * s["n"]))
                if s["kind"] == FFN:
                    read_out(segs[1], s)
                else:
                    ACT_MIX[s["kind"]](act, s, read_out, split, rstd)
                close_sublayer(s)

        @block.vector
        def _(dve):
            v = nc.vector

            def split(slot, count, cols):
                dve.wait_ge(sem("weights_hi"), count)
                v.tensor_tensor(wlo[:, slot, 0:cols], raw[:, slot, 0:cols], whi[:, slot, 0:cols].bitcast(F32),
                                ALU.subtract).then_inc(sem("weights_lo"), 1)

            def lo_pair(s, pair):
                dve.wait_ge(sem("x_hi"), 4 * s["fill"] + pair + 1)
                for k in (2 * pair, 2 * pair + 1):
                    e = v.scalar_tensor_tensor(xs[:, k, T:2 * T], h[:, k, :], vec[:, k, s["gain"]:s["gain"] + 1],
                                               xs[:, k, 0:T].bitcast(F32), ALU.mult, ALU.subtract)
                e.then_inc(sem("x_lo"), 1)

            def split_pair(n, pair):
                if pair == 3:
                    dve.wait_ge(sem("weights_hi"), subs[n + 1]["segs"][0].g0 + 2)
                else:
                    dve.wait_ge(sem("first_b_hi"), 3 * n + pair + 1)
                o = slice(2 * pair * PC, (2 * pair + 2) * PC)
                v.tensor_tensor(wlo[:, 1, o], raw[:, 1, o], whi[:, 1, o].bitcast(F32), ALU.subtract
                                ).then_inc(sem("weights_lo" if pair == 3 else "first_b_lo"), 1)

            def close_sublayer(s, nxt):
                n = s["n"]
                if nxt is not None:
                    for pair in range(3):
                        split_pair(n, pair)
                r2 = rpost[:, :].rearrange("p (a t) -> p a t", a=1).to_broadcast([P, 2, T])
                dve.wait_ge(sem("rstd_ready"), 2 * n + 2)
                for pair in range(4):
                    q = slice(2 * pair, 2 * pair + 2)
                    dve.wait_ge(sem("output_scaled"), 4 * n + pair + 1)
                    v.tensor_tensor(upd[:, q, :], upd[:, q, :], r2, ALU.mult)
                    dve.drain()
                    v.tensor_tensor(h[:, q, :], h[:, q, :], upd[:, q, :], ALU.add).then_inc(sem("h_ready"), 1)
                    if nxt is not None and pair:
                        lo_pair(nxt, pair - 1)
                if nxt is not None:
                    split_pair(n, 3)
                    dve.drain()
                    lo_pair(nxt, 3)

            def read_out(seg, s, dst=None):
                opening, closing = seg is s["segs"][0], seg is s["segs"][-1]
                r2 = rpre[:, :].rearrange("p (a t) -> p a t", a=1).to_broadcast([P, 2, T])

                def body(i, nxt):
                    g = 2 * i + seg.g0
                    for slot in range(2):
                        t = two(tsum[:, slot, :])
                        y2 = y[:, 2 * i:2 * i + 2, :] if seg.role == "down" else None
                        if seg.role == "down" and slot == 1:
                            dve.drain()
                            dve.wait_ge(sem("corr_copied"), g + 2)
                            v.tensor_tensor(y2, y2, main_half(slot), ALU.add)
                            dve.drain()
                            v.tensor_tensor(y2, y2, two(corr[:, slot, :]), ALU.add).then_inc(sem("panel_out"), 1)
                        else:
                            to = y2 if y2 is not None else t
                            if seg.role == "out":
                                to = y[:, 4 * i + 2 * slot:4 * i + 2 * slot + 2, :]
                            dve.wait_ge(sem("corr_copied"), g + (slot + 1))
                            v.tensor_tensor(to, main_half(slot), two(corr[:, slot, :]), ALU.add).then_inc(sem("panel_out"), 1)
                        wait_rstd = opening and isinstance(i, int) and i == 0 and slot == 0
                        split_now = seg.role in ("down", "out") or wait_rstd
                        if nxt and split_now and not (closing and i == seg.bodies - 1 and slot == 1):
                            split(slot, g + (slot + 3), nxt)
                        if seg.role in ("down", "out"):
                            continue
                        dve.drain()
                        if wait_rstd:
                            dve.wait_ge(sem("rstd_ready"), 2 * s["n"] + 1)
                        if seg.role == "ffn":
                            f = s["ffn"] * seg.bodies
                            if slot == 0:
                                v.tensor_tensor(two(gate[:, :]), t, r2, ALU.mult).then_inc(sem("gate_ready"), 1)
                            else:
                                v.tensor_tensor(t, t, r2, ALU.mult)
                                dve.drain()
                                dve.wait_ge(sem("silu_ready"), i + (f + 1))
                                v.tensor_tensor(hid[:, :], tsum[:, slot, :], silu[:, :], ALU.mult
                                                ).then_inc(sem("hidden_ready"), 1)
                        elif seg.role == "small":
                            v.tensor_tensor(dst[slot], tsum[:, slot, slot * T:slot * T + T], rpre[:, :], ALU.mult)
                        else:
                            v.tensor_tensor(dst[:, bass.ds(4 * i + 2 * slot, 2), :], t, r2, ALU.mult)
                        if nxt and not split_now:
                            split(slot, g + (slot + 3), nxt)
                        if seg.role == "ffn" and slot == 1:
                            dve.wait_ge(sem("hidden_hi"), i + (f + 1))
                            v.tensor_tensor(hs[:, bass.ds(2 * i, 2), T:2 * T], two(hid[:, :]),
                                            hs[:, bass.ds(2 * i, 2), 0:T].bitcast(F32), ALU.subtract
                                            ).then_inc(sem("hidden_lo"), 1)
                seg_loop(dve, seg, body, peel_first=opening, unroll=closing)
                dve.drain()

            for slot in range(2):
                split(slot, slot + 1, flat[0].kt * flat[0].width)
            dve.wait_ge(sem("constants_ready"), 1)
            v.tensor_copy(dist[:, :, :], mix[:, 2, 0:2, :].bitcast(I32))
            v.tensor_copy(steps[:, :], mix[:, 2, 2, 0:16].bitcast(I32))
            v.tensor_reduce(even_odd[:, 0:1], even_tmp, AX_X, ALU.add)
            dve.drain()
            v.tensor_scalar(even_odd[:, 1:2], even_odd[:, 0:1], -1.0, 1.0, ALU.mult, ALU.add)
            v.scalar_tensor_tensor(dist[:, :, :], dist[:, :, :], -1.0, dist[:, :, :], ALU.mult, ALU.max)
            dve.drain()
            for t in range(TT):
                v.memset(dist[0:64, t, t * P + 64:(t + 1) * P], BIG)
            for b in range(2):
                dve.wait_ge(sem("vectors_turned"), b + 1)
                v.tensor_copy(vec[:, 4 * b:4 * b + 4, :],
                              pm[:, b, :].rearrange("p (k r) -> p k r", r=P)[:, :, 0:NVEC])
            dve.drain()
            for g in (1, 5):
                half = vec[:, :, 0:36].rearrange("p k (l s) -> p k l s", s=6)[:, :, :, g]
                e = v.tensor_scalar(half, half, 0.5, None, ALU.mult)
            e.then_inc(sem("vectors_ready"), 1)
            for b in range(4):
                dve.wait_ge(sem("x_turned"), b + 1)
                v.tensor_copy(h[:, 2 * b:2 * b + 2, :], two(pp[:, b, :])).then_inc(sem("h_ready"), 1)
            dve.drain()
            for pair in range(4):
                lo_pair(subs[0], pair)
            for s, following in zip(subs, subs[1:] + [None]):
                segs = s["segs"]
                if s["kind"] == FFN:
                    read_out(segs[0], s)
                    read_out(segs[1], s)
                else:
                    DVE_MIX[s["kind"]](dve, s, read_out, split)
                close_sublayer(s, following)
            for t in range(TT):
                for half in range(2):
                    dve.wait_ge(sem("result_turned"), 2 * t + half + 1)
                    e = v.tensor_copy(mix[:, 0].rearrange("p k t -> p (k t)")[:, t * D + half * 512:t * D + half * 512 + 512],
                                      pp[:, half, :])
                e.then_inc(sem("result_ready"), 1)

        @block.tensor
        def _(pe):
            mm = nc.tensor.matmul

            def tile_product(seg, slot, ft, x, k, x_k):
                bank, c = pp[:, 2 * slot + ft, :], k * PC + ft * P
                mm(bank, whi[:, slot, c:c + P], x[:, x_k, :], start=(k == 0), stop=False)
                return mm(bank[:, 0:T], wlo[:, slot, c:c + P], x[:, x_k, 0:T], start=False, stop=(k == seg.kt - 1))

            def first_pair(seg, fill, after_x, b_in_pairs=None):
                pe.wait_ge(sem("weights_lo"), seg.g0 + (1 if b_in_pairs is not None else 2))
                if seg.g0:
                    pe.wait_ge(sem("panel_out"), seg.g0)
                for k in range(KD):
                    if k % 2 == 0:
                        pe.wait_ge(sem("x_lo"), 4 * fill + k // 2 + 1)
                        if b_in_pairs is not None and k < 6:
                            pe.wait_ge(sem("first_b_lo"), 3 * b_in_pairs + k // 2 + 1)
                        elif b_in_pairs is not None:
                            pe.wait_ge(sem("weights_lo"), seg.g0 + 2)
                    tile_product(seg, 0, 0, xs, k, k)
                    e = tile_product(seg, 0, 1, xs, k, k)
                    if k == KD - 1:
                        e.then_inc(sem("panel_done"), 1)
                    tile_product(seg, 1, 0, xs, k, k)
                if after_x is not None:
                    after_x()
                for k in range(KD):
                    e = tile_product(seg, 1, 1, xs, k, k)
                e.then_inc(sem("panel_done"), 1)

            def products(seg, x, first=None, x_wait=None, second_half=0, b_wait=None, sums=None):
                def body(i, nxt):
                    g = 2 * i + seg.g0
                    for slot in range(2):
                        pe.wait_ge(sem("weights_lo"), g + (slot + 1))
                        pe.wait_ge(sem("panel_out"), g + (slot - 1))
                        if x_wait is not None and slot == 0 and i == 0:
                            pe.wait_ge(*x_wait)
                        if b_wait is not None and slot == 1 and i == 0:
                            pe.wait_ge(*b_wait)
                        for ft in range(2):
                            for k in range(seg.kt):
                                e = tile_product(seg, slot, ft, x, k, second_half * slot + k)
                                if sums is not None and ft == 1 and k == seg.kt // 2:
                                    sums(2 * i + slot)
                        e.then_inc(sem("panel_done"), 1)
                start = 0
                if first is not None:
                    first()
                    start = 1
                if sums is not None or seg.bodies - start <= 1:
                    for i in range(start, seg.bodies):
                        body(i, 0)
                else:
                    with pe.Fori(start, seg.bodies) as i:
                        body(i, 0)

            def column_sums(s):
                pe.wait_ge(sem("squares_ready"), 5 * s["n"] + 1)
                for k in range(KD):
                    e = mm(psum_stat, ones[:, :], sq[:, k, :], start=(k == 0), stop=(k == KD - 1))
                e.then_inc(sem("squares_summed"), 1)

            def output_sums(s, pair):
                pe.wait_ge(sem("squares_ready"), 5 * s["n"] + 2 + pair)
                for k in (2 * pair, 2 * pair + 1):
                    e = mm(psum_stat, ones[:, :], sq[:, k, :], start=(k == 0), stop=(k == KD - 1))
                if pair == 3:
                    e.then_inc(sem("squares_summed"), 1)

            def last_products(s, x, **how):
                seg = s["segs"][-1]

                def sums(panel):
                    if seg.bodies == 2:
                        for pair in ((0, 1), (2,))[panel - 2]:
                            output_sums(s, pair)
                    elif seg.bodies == 4 and panel and panel % 2 == 0:
                        output_sums(s, panel // 2 - 1)
                products(seg, x, sums=sums, **how)
                output_sums(s, 3)

            def out_products(s, fill):
                last_products(s, xs, first=lambda: first_pair(s["segs"][-1], fill, None))

            pe.wait_ge(sem("constants_ready"), 1)
            pe.wait_ge(sem("table_loaded"), 16 * N_TABLE_LOADS)
            for b in range(2):
                for k in range(4):
                    f = 4 * b + k
                    e = nc.tensor.transpose(pm[:, b, k * P:k * P + NVEC],
                                            mix[:, 0].rearrange("p k t -> p (k t)")[0:NVEC, f * P:f * P + P],
                                            ident[0:NVEC, 0:NVEC])
                e.then_inc(sem("vectors_turned"), 1)
            pe.wait_ge(sem("x_loaded"), 16)
            xin = mix[:, 1].rearrange("p k t -> p (k t)").rearrange("p (a d) -> p a d", a=TT)
            for b in range(4):
                for k in range(2):
                    for t in range(TT):
                        f = 2 * b + k
                        e = nc.tensor.transpose(pp[:, b, k * T + t * P:k * T + t * P + P], xin[:, t, f * P:f * P + P],
                                                ident[:, :])
                e.then_inc(sem("x_turned"), 1)
            pe.wait_ge(sem("h_ready"), 4)
            for s in subs:
                n, segs = s["n"], s["segs"]
                products(segs[0], xs, first=lambda: first_pair(segs[0], s["fill"], lambda: column_sums(s),
                                                               n - 1 if n else None))
                if s["kind"] == FFN:
                    f = s["ffn"] * segs[0].bodies
                    last_products(s, hs, x_wait=(sem("hidden_lo"), f + 6), second_half=KH,
                                  b_wait=(sem("hidden_lo"), f + segs[0].bodies))
                else:
                    PE_MIX[s["kind"]](pe, s, products, last_products, out_products)
            pe.wait_ge(sem("h_ready"), 4 * len(subs) + 4)
            for t in range(TT):
                for half in range(2):
                    if t:
                        pe.wait_ge(sem("result_ready"), t)
                    for k in range(4):
                        e = nc.tensor.transpose(pp[:, half, k * P:k * P + P], h[:, 4 * half + k, t * P:t * P + P], ident[:, :])
                    e.then_inc(sem("result_turned"), 1)


INS = ["x", "norm_gains", "ffn1_w_in", "ffn1_w_out", "ffn2_w_in", "ffn2_w_out", "hgrn_w_in", "hgrn_gnorm",
       "hgrn_w_out", "hgrn_lb_raw", "diff_w_in", "diff_lambda", "diff_subln", "diff_w_out", "pool_w_in",
       "pool_w_group", "pool_scale", "pool_w_out", "norm_g_2", "ffn_w_in_2", "ffn_w_out_2", "hyb_w_in_2",
       "ssm_conv_w_2", "ssm_conv_b_2", "ssm_dt_bias_2", "ssm_a_log_2", "ssm_d_2", "ssm_norm_g_2", "fox_b_f_2",
       "hyb_w_out_2", "rec_w_in_2", "rec_conv_w_2", "rec_conv_b_2", "rec_w_a_2", "rec_b_a_2", "rec_w_x_2",
       "rec_b_x_2", "rec_lambda_2", "rec_w_out_2"]


def kernel(**inputs):
    import concourse.bacc as bacc
    from concourse.bass_utils import run_bass_kernel_spmd

    nc = bacc.Bacc("TRN2", target_bir_lowering=False, num_devices=1)
    arrays, aps = {}, {}
    for name in INS:
        arrays[name] = np.ascontiguousarray(inputs[name])
        aps[name] = nc.dram_tensor(name, arrays[name].shape, mybir.dt.from_np(arrays[name].dtype),
                                   kind="ExternalInput").ap()
    out = nc.dram_tensor("out", (1, T, D), F32, kind="ExternalOutput").ap()
    build(nc, aps, out)
    return run_bass_kernel_spmd(nc, [arrays], core_ids=[0]).results[0]["out"]
```

```python
import math
from contextlib import ExitStack

import numpy as np

import concourse.bass as bass
import concourse.mybir as mybir
from concourse.alu_op_type import AluOpType as ALU

F32 = mybir.dt.float32
F32R = mybir.dt.float32r
I32 = mybir.dt.int32
ACT = mybir.ActivationFunctionType
AX_X = mybir.AxisListType.X

P = 128
T = 256
TT = T // P
D = 1024
KD = D // P
FF = 2816
KF = FF // P
PC = 256
KH = KF // 2
EPS = 1e-6
SSM_H = 16
HGB = 16
NB = T // HGB
BIG = 1e30

VEC_GAIN1, VEC_GAIN2 = 0, 24
VEC_LB = 36
VEC_POOL_SCALE, VEC_SSM_NORM = 40, 41
VEC_REC_CONV_W, VEC_REC_CONV_B, VEC_REC_BA, VEC_REC_BX, VEC_REC_LAM = 42, 46, 47, 48, 49
VEC_SSM_CONV_X, VEC_SSM_CONV_BX = 50, 54
VEC_SSM_CONV_BC, VEC_SSM_CONV_BBC = 55, 59
VEC_GNORM, VEC_SUBLN, VEC_DT_BIAS, VEC_A_LOG, VEC_FOX_B = 60, 62, 63, 64, 65
NVEC = 66
N_TABLE_LOADS = 19
FOX_ROW = 120

FFN, HGRN, DIFF, POOL, HYB, REC = "ffn", "hgrn", "diff", "pool", "hyb", "rec"


class Segment:

    def __init__(self, role, kt, bodies, source, width=PC):
        self.role, self.kt, self.bodies, self.source, self.width = role, kt, bodies, source, width


def columns(w, first=0):
    def source(i, slot):
        return w[:, bass.ds(first + (2 * i + slot) * PC, PC)].rearrange("(k p) c -> p k c", p=P)
    return source


def gate_and_up(w):
    def source(i, slot):
        return w[:, bass.ds(slot * FF + i * PC, PC)].rearrange("(k p) c -> p k c", p=P)
    return source


def row_halves(w, rows):
    def source(i, slot):
        return w[slot * rows:(slot + 1) * rows, bass.ds(i * PC, PC)].rearrange("(k p) c -> p k c", p=P)
    return source


def hgrn_panels(w):
    def source(i, slot):
        p = 2 * i + slot
        kind, j = ((1, 0, 2)[p % 3], p // 3) if p < 12 else (3, p - 12)
        return w[:, kind * D + j * PC:kind * D + (j + 1) * PC].rearrange("(k p) c -> p k c", p=P)
    return source


def listed(w, firsts):
    def source(i, slot):
        first = firsts[2 * i + slot]
        return w[:, first:first + PC].rearrange("(k p) c -> p k c", p=P)
    return source


def qkv_panels(w):
    def source(i, slot):
        p = 2 * i + slot
        return w[:, (p % 3) * D + (p // 3) * PC:][:, 0:PC].rearrange("(k p) c -> p k c", p=P)
    return source


def build(nc, a, out):
    def ffn(w_in, w_out, gain):
        return dict(kind=FFN, gain=gain, segs=[
            Segment("ffn", KD, FF // PC, gate_and_up(w_in)),
            Segment("down", KH, D // PC, row_halves(w_out, FF // 2))])

    def out_proj(w):
        return Segment("out", KD, D // PC // 2, columns(w))

    subs = []
    for l in range(4):
        g = VEC_GAIN1 + 6 * l
        subs.append(ffn(a["ffn1_w_in"][l], a["ffn1_w_out"][l], g))
        if l % 3 == 0:
            j = l // 3
            subs.append(dict(kind=HGRN, gain=g + 2, layer=l, j=j, segs=[
                Segment("heads", KD, 4 * D // (2 * PC), hgrn_panels(a["hgrn_w_in"][j])), out_proj(a["hgrn_w_out"][j])]))
        elif l == 1:
            subs.append(dict(kind=DIFF, gain=g + 2, layer=l, segs=[
                Segment("heads", KD, 3 * D // (2 * PC), qkv_panels(a["diff_w_in"][0])), out_proj(a["diff_w_out"][0])]))
        else:
            wg = a["pool_w_group"][0]
            subs.append(dict(kind=POOL, gain=g + 2, segs=[
                Segment("heads", KD, D // (2 * PC), listed(a["pool_w_in"][0], [3 * PC, 2 * PC, PC, 0])),
                Segment("group", 4, 1, lambda i, slot: wg[2 * slot:2 * slot + 2].rearrange("g (t p) c -> p (g t) c", p=P)),
                out_proj(a["pool_w_out"][0])]))
        subs.append(ffn(a["ffn2_w_in"][l], a["ffn2_w_out"][l], g + 4))
    for l in range(2):
        g = VEC_GAIN2 + 6 * l
        subs.append(ffn(a["ffn_w_in_2"][l, 0], a["ffn_w_out_2"][l, 0], g))
        if l == 0:
            w = a["hyb_w_in_2"][0]
            n_zx, n_qkv = 1024 + 1536, 3 * D
            subs.append(dict(kind=HYB, gain=g + 2, segs=[
                Segment("small", KD, 1, lambda i, slot: w[:, (n_zx, n_zx + 16 + n_qkv + 8 - PC)[slot]:][:, 0:PC].rearrange(
                    "(k p) c -> p k c", p=P)),
                Segment("heads", KD, n_zx // (2 * PC), listed(w, [2 * D, 2 * D + PC] + [D + PC * k for k in range(4)] + [PC * k for k in range(4)])),
                Segment("heads", KD, n_qkv // (2 * PC), lambda i, slot: columns(w, n_zx + 16)(i, slot)),
                Segment("down", KD, D // PC, row_halves(a["hyb_w_out_2"][0], D))]))
        else:
            wa, wx = a["rec_w_a_2"][0], a["rec_w_x_2"][0]
            subs.append(dict(kind=REC, gain=g + 2, segs=[
                Segment("heads", KD, 3, listed(a["rec_w_in_2"][0], [D, D + PC, D + 2 * PC, D + 3 * PC, 0, PC])),
                Segment("block", KD, 1, lambda i, slot: (wa, wx)[slot].rearrange("n p c -> p n c"), width=P),
                Segment("heads", KD, 1, listed(a["rec_w_in_2"][0], [2 * PC, 3 * PC])),
                out_proj(a["rec_w_out_2"][0])]))
        subs.append(ffn(a["ffn_w_in_2"][l, 1], a["ffn_w_out_2"][l, 1], g + 4))
    panels = fills = ffns = downs = 0
    log1ps = hgrns = seconds = 0
    flat = []
    for n, s in enumerate(subs):
        s["n"], s["fill"] = n, fills
        fills += {FFN: 1, HYB: 1, HGRN: 2, DIFF: 2, POOL: 2, REC: 2}[s["kind"]]
        s["ls0"], s["it"], s["seconds"] = log1ps, hgrns, seconds
        seconds += s["kind"] in (POOL, REC)
        log1ps += s["kind"] in (HYB, REC)
        hgrns += s["kind"] == HGRN
        if s["kind"] == FFN:
            s["ffn"] = ffns
            ffns += 1
        for seg in s["segs"]:
            seg.g0 = panels
            panels += 2 * seg.bodies
            flat.append(seg)
            if seg.role == "down":
                seg.d0 = downs
                downs += seg.bodies
    for seg, nxt in zip(flat, flat[1:] + [None]):
        seg.next = nxt

    ctx = ExitStack()
    with ctx:
        def sb(name, shape, dt=F32):
            return ctx.enter_context(nc.sbuf_tensor(name, shape, dt))

        sems = {}

        def sem(name):
            if name not in sems:
                sems[name] = ctx.enter_context(nc.semaphore(name))
            return sems[name]

        raw = sb("raw", [P, 2, KH * PC])
        whi = sb("whi", [P, 2, KH * PC], F32R)
        wlo = sb("wlo", [P, 2, KH * PC], F32R)
        xs = sb("xs", [P, KD, 2 * T], F32R)
        h = sb("h", [P, KD, T])
        y = sb("y", [P, KD, T])
        corr = sb("corr", [P, 2, 2 * T])
        tsum = sb("tsum", [P, 2, 2 * T])
        gate = sb("gate", [P, 2 * T])
        silu = sb("silu", [P, 2 * T])
        hid = sb("hid", [P, 2 * T])
        rpre = sb("rpre", [P, T])
        rpost = sb("rpost", [P, T])
        rln = sb("rln", [P, T])
        vec = sb("vec", [P, KD, NVEC])
        ones = sb("ones", [P, P])
        ident = sb("ident", [P, P])
        eps = sb("eps", [P, 1])
        MB = 10
        pool_done = sb("pool_done", [P, 1])
        small = sb("small", [P, 8])
        lbw = sb("lbw", [P, KD, 6])
        rec_col = sb("rec_col", [P, 6, KD])
        dist = sb("dist", [P, TT, T])
        causal = sb("causal", [P, TT, T])
        tri = sb("tri", [P, P])
        block_causal = sb("block_causal", [P, P])
        keep = sb("keep", [P, T])
        sibling = sb("sibling", [P, P])
        steps = sb("steps", [P, 16])
        lamrow = sb("lamrow", [P, 4 * 64])
        skiprow = sb("skiprow", [P, SSM_H])
        mix_offset = nc.sbuf_base
        mix = sb("mix", [P, MB, KD, T])
        hs = nc.alloc_sbuf_tensor_at("hs", [P, KF, 2 * T], F32R, offset=mix_offset)
        xs2 = nc.alloc_sbuf_tensor_at("xs2", [P, KD, 2 * T], F32R, offset=mix_offset + (MB - 2) * KD * T * 4)
        sq = mix[:, MB - 1]
        upd = mix[:, MB - 2]

        pp = ctx.enter_context(nc.psum_tensor("pp", [P, 4, 2 * T], F32))
        pm = ctx.enter_context(nc.psum_tensor("pm", [P, 4, 2 * T], F32))
        psum_stat = pm[:, 3, 0:T]

        def main_half(slot):
            return pp[:, 2 * slot:2 * slot + 2, 0:T]

        def corr_half(slot):
            return pp[:, 2 * slot:2 * slot + 2, T:2 * T]

        def two(buf):
            return buf.rearrange("p (a t) -> p a t", a=2)

        def seg_loop(eng, seg, body, peel_first=False, unroll=False):
            nxt = 0 if seg.next is None else seg.next.kt * seg.next.width
            mine = seg.kt * seg.width
            if unroll:
                for i in range(seg.bodies):
                    body(i, nxt if i == seg.bodies - 1 else mine)
                return
            first = 1 if peel_first else 0
            last = seg.bodies - (nxt != mine)
            if last <= first:
                for i in range(seg.bodies):
                    body(i, nxt if i == seg.bodies - 1 else mine)
                return
            if peel_first:
                body(0, mine)
            if last - first == 1:
                body(first, mine)
            else:
                with eng.Fori(first, last) as i:
                    body(i, mine)
            if nxt != mine:
                body(seg.bodies - 1, nxt)

        def fill_hi(act, fill, src, gain=None):
            for pair in range(4):
                if gain is None:
                    q = slice(2 * pair, 2 * pair + 2)
                    e = nc.scalar.activation(xs[:, q, 0:T], src[:, q, :], ACT.Copy)
                else:
                    for k in (2 * pair, 2 * pair + 1):
                        e = nc.scalar.activation(xs[:, k, 0:T], src[:, k, :], ACT.Copy, scale=vec[:, k, gain:gain + 1])
                e.then_inc(sem("x_hi"), 1)

        def fill_lo(dve, fill, src, gain=None):
            for pair in range(4):
                dve.wait_ge(sem("x_hi"), 4 * fill + pair + 1)
                if gain is None:
                    q = slice(2 * pair, 2 * pair + 2)
                    e = nc.vector.tensor_tensor(xs[:, q, T:2 * T], src[:, q, :], xs[:, q, 0:T].bitcast(F32), ALU.subtract)
                else:
                    for k in (2 * pair, 2 * pair + 1):
                        e = nc.vector.scalar_tensor_tensor(xs[:, k, T:2 * T], src[:, k, :], vec[:, k, gain:gain + 1],
                                                           xs[:, k, 0:T].bitcast(F32), ALU.mult, ALU.subtract)
                e.then_inc(sem("x_lo"), 1)

        def log1p_quotient(dve, e, w, c):
            v = nc.vector
            v.tensor_scalar(w, e, 1.0, None, ALU.add).then_inc(sem("log1p_w"), 1)
            dve.drain()
            v.tensor_scalar(c, w, -1.0, None, ALU.add)
            dve.drain()
            v.tensor_tensor(c, e, c, ALU.subtract)
            dve.drain()
            v.reciprocal(e, w)
            dve.drain()
            v.tensor_tensor(c, c, e, ALU.mult)
            dve.drain()

        def flat2(buf):
            return buf.rearrange("p k t -> p (k t)")

        def tok(buf):
            return flat2(buf).rearrange("p (a d) -> p a d", a=TT)

        def hi_of_second(act, s, pair, src):
            q = slice(2 * pair, 2 * pair + 2)
            act.wait_ge(sem("second_ready"), 4 * s["seconds"] + SECOND_ORDER[s["kind"]].index(pair) + 1)
            nc.scalar.activation(xs2[:, q, 0:T], src[:, q, :], ACT.Copy).then_inc(sem("second_hi"), 1)

        def lo_of_second(dve, s, pair, src):
            q = slice(2 * pair, 2 * pair + 2)
            dve.wait_ge(sem("second_hi"), 4 * s["seconds"] + SECOND_ORDER[s["kind"]].index(pair) + 1)
            nc.vector.tensor_tensor(xs2[:, q, T:2 * T], src[:, q, :], xs2[:, q, 0:T].bitcast(F32), ALU.subtract
                                    ).then_inc(sem("second_lo"), 1)

        SECOND_ORDER = {POOL: (3, 2, 1, 0), REC: (0, 1, 2, 3)}

        R_GATE, R_X, R_CONV, R_CORR, R_R, R_I, R_A, R_TH = (mix[:, b] for b in range(8))

        def rec_dst(p):
            return R_X[:, 2 * p:2 * p + 2, :] if p < 4 else R_GATE[:, 2 * p - 8:2 * p - 6, :]

        REC_QUARTERS = ((0, 0, R_R), (1, 0, R_I), (0, 4, R_R), (1, 4, R_I))

        def act_rec(act, s, read_out, split, rstd):
            seg = s["segs"][1]
            n_cols = seg.next.kt * seg.next.width

            def hook(p):
                if p == 1:
                    act.wait_ge(sem("log1p_negabs"), s["ls0"] + 1)
                    nc.scalar.activation(rec_col[:, 0, :], rec_col[:, 0, :], ACT.Exp).then_inc(sem("log1p_exp"), 1)
                elif p == 3:
                    act.wait_ge(sem("log1p_w"), s["ls0"] + 1)
                    nc.scalar.activation(rec_col[:, 3, :], rec_col[:, 1, :], ACT.Ln).then_inc(sem("log1p_ln"), 1)
                if 1 <= p <= 4:
                    hi_of_second(act, s, p - 1, R_CONV)

            read_out(s["segs"][0], s, after_first=lambda: rstd(rpre[:, :], 2 * s["n"]), hook=hook)
            for n, (slot, k0, dst) in enumerate(REC_QUARTERS):
                if n < 2:
                    act.wait_ge(sem("rec_quarter"), n + 1)
                else:
                    act.wait_ge(sem("panel_done"), seg.g0 + slot + 1)
                half = slice(4 * slot, 4 * slot + 4)
                e = nc.scalar.activation(R_CORR[:, half, :], (pp, pm)[slot][:, :, T:2 * T], ACT.Copy)
                e.then_inc(sem("rec_corr" if n < 2 else "corr_copied"), 1)
                if n >= 2:
                    split(slot, 16 * (seg.g0 // 2 + 2), n_cols)

            def sigmoids(slot):
                dst, bias_row = ((R_R, VEC_REC_BA), (R_I, VEC_REC_BX))[slot]
                act.wait_ge(sem("panel_out"), seg.g0 + slot + 1)
                for k in range(KD):
                    e = nc.scalar.activation(dst[:, k, :], dst[:, k, :], ACT.Sigmoid, bias=vec[:, k, bias_row:bias_row + 1])
                e.then_inc(sem("rec_sigmoid"), 1)

            def gates(p):
                if p == 0:
                    nc.scalar.activation(R_A, R_R, ACT.Exp).then_inc(sem("rec_a"), 1)

            sigmoids(0)
            sigmoids(1)
            act.wait_ge(sem("rec_log_a"), 1)
            nc.scalar.activation(R_TH, R_R, ACT.Tanh)
            read_out(s["segs"][2], s, hook=gates)
            for half in range(2):
                act.wait_ge(sem("rec_one_minus_a2"), half + 1)
                q = slice(4 * half, 4 * half + 4)
                nc.scalar.activation(R_TH[:, q, :], R_TH[:, q, :], ACT.Sqrt, scale=-1.0).then_inc(sem("rec_sqrt"), 1)
            act.wait_ge(sem("rec_gates"), 1)
            nc.scalar.activation(R_GATE, R_GATE, ACT.Gelu_apprx_tanh).then_inc(sem("rec_gelu"), 1)
            for half in range(2):
                act.wait_ge(sem("rec_gated"), half + 1)
                for pair in (2 * half, 2 * half + 1):
                    q = slice(2 * pair, 2 * pair + 2)
                    nc.scalar.activation(xs[:, q, 0:T], R_A[:, q, :], ACT.Copy).then_inc(sem("x_hi"), 1)
            read_out(s["segs"][3], s)

        def dve_rec(dve, s, read_out, split):
            v, seg = nc.vector, s["segs"][1]

            def hook(p):
                dve.drain()
                if 1 <= p <= 4:
                    lo_of_second(dve, s, p - 1, R_CONV)
                if p < 4:
                    dve_conv(dve, R_CONV, R_X, (2 * p, 2 * p + 1), VEC_REC_CONV_W, VEC_REC_CONV_B)
                    v.memset(small[:, 1:2], 0.0).then_inc(sem("second_ready"), 1)
                if p == 0:
                    v.tensor_copy(rec_col[:, 5, :], vec[:, :, VEC_REC_LAM])
                    dve.drain()
                    v.scalar_tensor_tensor(rec_col[:, 0, :], rec_col[:, 5, :], -1.0, rec_col[:, 5, :], ALU.mult, ALU.min
                                           ).then_inc(sem("log1p_negabs"), 1)
                elif p == 2:
                    dve.wait_ge(sem("log1p_exp"), s["ls0"] + 1)
                    log1p_quotient(dve, *(rec_col[:, r, :] for r in range(3)))
                elif p == 4:
                    dve.wait_ge(sem("log1p_ln"), s["ls0"] + 1)
                    v.tensor_tensor(rec_col[:, 3, :], rec_col[:, 3, :], rec_col[:, 2, :], ALU.add)
                    dve.drain()
                    v.scalar_tensor_tensor(rec_col[:, 4, :], rec_col[:, 5, :], 0.0, rec_col[:, 3, :], ALU.min, ALU.subtract)
                    dve.drain()
                    v.tensor_scalar(rec_col[:, 4, :], rec_col[:, 4, :], 8.0, None, ALU.mult)
                    dve.drain()

            read_out(s["segs"][0], s, rec_dst, hook=hook)
            for n, (slot, k0, dst) in enumerate(REC_QUARTERS):
                if n < 2:
                    dve.wait_ge(sem("rec_corr"), n + 1)
                else:
                    dve.wait_ge(sem("corr_copied"), seg.g0 + slot + 1)
                half = slice(4 * slot, 4 * slot + 4)
                v.tensor_tensor(dst[:, k0:k0 + 4, :], (pp, pm)[slot][:, :, 0:T], R_CORR[:, half, :], ALU.add
                                ).then_inc(sem("rec_read" if n < 2 else "panel_out"), 1)
            for slot in range(2):
                split(slot, seg.g0 + slot + 3, seg.next.kt * seg.next.width)
            dve.wait_ge(sem("rec_sigmoid"), 1)
            for k in range(KD):
                e = v.tensor_scalar(R_R[:, k, :], R_R[:, k, :], rec_col[:, 4, k:k + 1], None, ALU.mult)
            e.then_inc(sem("rec_log_a"), 1)

            dve.wait_ge(sem("rec_sigmoid"), 2)
            v.tensor_tensor(R_I, R_I, R_CONV, ALU.mult)
            halves = (slice(0, 4), slice(4, 8))

            def gates(p):
                if p == 0:
                    dve.wait_ge(sem("rec_a"), 1)
                    for q in halves:
                        v.tensor_tensor(R_R[:, q, :], R_A[:, q, :], R_A[:, q, :], ALU.mult)
                        dve.drain()
                        v.scalar_tensor_tensor(R_TH[:, q, :], R_R[:, q, :], 1.0, R_TH[:, q, :], ALU.add, ALU.mult
                                               ).then_inc(sem("rec_one_minus_a2"), 1)
                if p == 1:
                    v.memset(small[:, 2:3], 0.0).then_inc(sem("rec_gates"), 1)

            read_out(s["segs"][2], s, lambda p: R_GATE[:, 4 + 2 * p:6 + 2 * p, :], hook=gates)
            v.memset(R_A[:, :, 0:1], 0.0)
            for half, q in enumerate(halves):
                dve.wait_ge(sem("rec_sqrt"), half + 1)
                v.tensor_tensor(R_I[:, q, :], R_I[:, q, :], R_TH[:, q, :], ALU.mult)
                dve.drain()
                v.tensor_tensor_scan(flat2(R_R[:, q, :]), flat2(R_A[:, q, :]), flat2(R_I[:, q, :]), 0.0, ALU.mult, ALU.add)
                dve.drain()
            dve.wait_ge(sem("rec_gelu"), 1)
            for q in halves:
                v.tensor_tensor(R_A[:, q, :], R_R[:, q, :], R_GATE[:, q, :], ALU.mult).then_inc(sem("rec_gated"), 1)
            fill_lo(dve, s["fill"] + 1, R_A)
            read_out(s["segs"][3], s)

        def pe_rec(pe, s, products, last_products, out_products, first_of, keep_clock):
            seg = s["segs"][1]
            products(s["segs"][0], xs, first=lambda: first_of(s), hook=lambda p: None)
            pe.wait_ge(sem("second_lo"), 4 * s["seconds"] + 4)
            pe.wait_ge(sem("panel_out"), seg.g0)
            for n, (slot, k0, _) in enumerate(REC_QUARTERS):
                if n < 2:
                    pe.wait_ge(sem("weights_lo"), seg.g0 + slot + 1)
                else:
                    pe.wait_ge(sem("rec_read"), n - 1)
                for k in range(k0, k0 + 4):
                    bank = (pp, pm)[slot][:, k - k0, :]
                    nc.tensor.matmul(bank, whi[:, slot, k * P:(k + 1) * P], xs2[:, k, :], start=True, stop=False)
                    e = nc.tensor.matmul(bank[:, 0:T], wlo[:, slot, k * P:(k + 1) * P], xs2[:, k, 0:T], start=False, stop=True)
                e.then_inc(sem("rec_quarter" if n < 2 else "panel_done"), 1)
            products(s["segs"][2], xs)
            out_products(s, s["fill"] + 1)

        def dve_conv(dve, dst, src, tiles, w_row, b_row, vec_tile=lambda k: k):
            v = nc.vector
            for k in tiles:
                q = vec_tile(k)
                v.tensor_scalar(dst[:, k, :], src[:, k, :], vec[:, q, w_row + 3:w_row + 4], vec[:, q, b_row:b_row + 1],
                                ALU.mult, ALU.add)
            for j in (2, 1, 0):
                d = 3 - j
                dve.drain()
                for k in tiles:
                    q = vec_tile(k)
                    v.scalar_tensor_tensor(dst[:, k, d:T], src[:, k, 0:T - d], vec[:, q, w_row + j:w_row + j + 1],
                                           dst[:, k, d:T], ALU.mult, ALU.add)
            dve.drain()

        P_U, P_W1, P_W2, P_RC, P_OUT, P_CORR = (mix[:, b] for b in range(6))

        def pool_tiles(p):
            return slice(6 - 2 * p, 8 - 2 * p)

        def act_pool(act, s, read_out, split, rstd):
            seg = s["segs"][1]

            def hook(p):
                if p >= 2:
                    hi_of_second(act, s, 5 - p, P_OUT)

            read_out(s["segs"][0], s, after_first=lambda: rstd(rpre[:, :], 2 * s["n"]), hook=hook)
            for pair in (1, 0):
                hi_of_second(act, s, pair, P_OUT)
            for slot in range(2):
                act.wait_ge(sem("panel_done"), seg.g0 + slot + 1)
                nc.scalar.activation(P_CORR[:, 4 * slot:4 * slot + 4, :], (pp, pm)[slot][:, :, T:2 * T], ACT.Copy
                                     ).then_inc(sem("corr_copied"), 1)
                if slot == 0:
                    split(slot, 16 * (seg.g0 // 2 + 2), seg.next.kt * seg.next.width)
            act.wait_ge(sem("panel_out"), seg.g0 + 1)
            for pair in range(4):
                if pair == 2:
                    split(1, 16 * (seg.g0 // 2 + 2), seg.next.kt * seg.next.width)
                    act.wait_ge(sem("panel_out"), seg.g0 + 2)
                for k in (2 * pair, 2 * pair + 1):
                    e = nc.scalar.activation(xs[:, k, 0:T], P_OUT[:, k, :], ACT.Copy,
                                             scale=vec[:, k, VEC_POOL_SCALE:VEC_POOL_SCALE + 1])
                e.then_inc(sem("x_hi"), 1)
            read_out(s["segs"][2], s)

        def dve_pool(dve, s, read_out, split):
            v, seg = nc.vector, s["segs"][1]

            for g in range(4):
                v.memset(P_RC[:, g, :], 1.0 / 2 ** (g + 1))
                v.tensor_scalar(P_RC[:, 4 + g, 0:16], steps[:, :], float(2 ** (g + 1)), None, ALU.min)
            dve.drain()
            v.reciprocal(P_RC[:, 0:4, 0:16], P_RC[:, 4:8, 0:16])

            def hook(p):
                if p >= 2:
                    lo_of_second(dve, s, 5 - p, P_OUT)
                if p:
                    means(p - 1)

            def means(p):
                dve.drain()
                g, q, src = 3 - p, pool_tiles(p), P_U
                for n in range(g + 1):
                    d, dst = 2 ** n, (P_W1, P_W2)[n % 2]
                    v.tensor_copy(dst[:, q, 0:d], src[:, q, 0:d])
                    v.tensor_tensor(dst[:, q, d:T], src[:, q, d:T], src[:, q, 0:T - d], ALU.add)
                    dve.drain()
                    src = dst
                v.tensor_tensor(P_OUT[:, q, :], src[:, q, :], P_RC[:, g:g + 1, :].to_broadcast([P, 2, T]), ALU.mult)
                dve.drain()
                v.tensor_tensor(P_OUT[:, q, :], P_OUT[:, q, :], P_U[:, q, :], ALU.subtract).then_inc(sem("second_ready"), 1)

            read_out(s["segs"][0], s, lambda p: P_U[:, pool_tiles(p), :], hook=hook)
            means(3)
            for pair in (1, 0):
                lo_of_second(dve, s, pair, P_OUT)
            for slot in range(2):
                dve.wait_ge(sem("corr_copied"), seg.g0 + slot + 1)
                q = slice(4 * slot, 4 * slot + 4)
                v.tensor_tensor(P_OUT[:, q, :], (pp, pm)[slot][:, :, 0:T], P_CORR[:, q, :], ALU.add).then_inc(sem("panel_out"), 1)
                if slot == 0:
                    split(slot, seg.g0 + slot + 3, seg.next.kt * seg.next.width)
            dve.drain()
            for pair in range(4):
                if pair == 2:
                    split(1, seg.g0 + 4, seg.next.kt * seg.next.width)
                dve.wait_ge(sem("x_hi"), 4 * s["fill"] + 5 + pair)
                for k in (2 * pair, 2 * pair + 1):
                    e = v.scalar_tensor_tensor(xs[:, k, T:2 * T], P_OUT[:, k, :], vec[:, k, VEC_POOL_SCALE:VEC_POOL_SCALE + 1],
                                               xs[:, k, 0:T].bitcast(F32), ALU.mult, ALU.subtract)
                e.then_inc(sem("x_lo"), 1)
            read_out(s["segs"][2], s)

        def pe_pool(pe, s, products, last_products, out_products, first_of, keep_clock):
            seg = s["segs"][1]
            products(s["segs"][0], xs, first=lambda: first_of(s), hook=lambda p: None)
            pe.wait_ge(sem("second_lo"), 4 * s["seconds"] + 4)
            for slot in range(2):
                pe.wait_ge(sem("weights_lo"), seg.g0 + slot + 1)
                pe.wait_ge(sem("panel_out"), seg.g0 + slot)
                for n in range(4):
                    bank = (pp, pm)[slot][:, n, :]
                    for t in range(2):
                        c = (2 * (n // 2) + t) * PC + (n % 2) * P
                        k = 2 * (2 * slot + n // 2) + t
                        nc.tensor.matmul(bank, whi[:, slot, c:c + P], xs2[:, k, :], start=(t == 0), stop=False)
                        e = nc.tensor.matmul(bank[:, 0:T], wlo[:, slot, c:c + P], xs2[:, k, 0:T], start=False, stop=(t == 1))
                e.then_inc(sem("panel_done"), 1)
            out_products(s, s["fill"] + 1)

        AT_QT = (slice(0, P), slice(P, 3 * P))
        AT_SUM, AT_REC = 4, 8

        def at_slot(n):
            return mix[:, 2 + n // 4, 2 * (n % 4):2 * (n % 4) + 2, :]

        def at(name, j):
            names = ("q", "k", "vt", "w", "wT")
            return at_slot(2 * names.index(name) + j % 2 if name in names else 10 + ("v", "sq", "r").index(name))

        def at_scores(hd):
            return mix[:, 1, 4 * (hd % 2):4 * (hd % 2) + 4, :].rearrange("p (g k) t -> p g (k t)", g=2)

        def at_col(hd, c):
            return flat_pair(at("w", hd))[:, 3 * P + c:3 * P + c + 1]

        def flat_pair(buf):
            return buf.rearrange("p h t -> p (h t)")

        def at_panel(p):
            return "qkv"[p % 3], p // 3

        AT_DELAYS = dict(
            pe=(("scores0", 3), ("turn_values", 4), ("scores1", 4), ("turn0", 5), ("turn1", 6), ("values0", 6), ("values1", 7),
                ("sums", 8)),
            act=(("exp0", 3), ("values", 4), ("exp1", 4), ("wT0", 5), ("wT1", 6), ("square", 7), ("rstd", 8)),
            dve=(("max0", 3), ("weights0", 4), ("max1", 4), ("weights1", 5), ("out", 7), ("norm", 8)))

        def at_steps(engine, p, step):
            left = []
            for j in range(KD // 2):
                for name, d in AT_DELAYS[engine]:
                    if min(3 * j + d, 3 * KD // 2) == p:
                        left.append((3 * j + d, j, name))
            for _, j, name in sorted(left, key=lambda x: x[:2]):
                step(name, j)

        def pe_at_step(pe, s, groups):
            n0, dg, mm = 0, P // groups, nc.tensor.matmul

            def step(name, j):
                n = n0 + j + 1
                h = int(name[-1]) if name[-1] in "01" else 0
                m = 2 * (n - 1) + h + 1
                if name == "turn_values":
                    pe.wait_ge(sem("at_values_in"), n)
                    if j:
                        pe.wait_ge(sem("at_wT"), m - 1)
                    for c in range(4):
                        e = nc.tensor.transpose(pm[:, 2, c * P:(c + 1) * P], flat_pair(at("v", j))[:, c * P:(c + 1) * P], ident[:, :])
                    e.then_inc(sem("at_values_turned"), 1)
                elif name.startswith("scores"):
                    pe.wait_ge(sem("at_keys_in"), n)
                    if m > 1:
                        pe.wait_ge(sem("at_scores_read"), m - 1)
                    for g in range(groups):
                        rows = slice(g * dg, (g + 1) * dg)
                        for qt in range(TT):
                            e = mm(pm[:, g, AT_QT[qt]], at("q", j)[rows, h, qt * P:(qt + 1) * P], at("k", j)[rows, h, 0:(qt + 1) * P],
                                   start=True, stop=True)
                    e.then_inc(sem("at_scores"), 1)
                elif name.startswith("turn"):
                    pe.wait_ge(sem("at_weights"), m)
                    pe.wait_ge(sem("at_vt"), n if h == 0 else n)
                    if h:
                        pe.wait_ge(sem("at_wT"), m - 1)
                    for c in range(3):
                        e = nc.tensor.transpose(pm[:, 2, c * P:(c + 1) * P], flat_pair(at("w", h))[:, c * P:(c + 1) * P], ident[:, :])
                    e.then_inc(sem("at_turned"), 1)
                elif name.startswith("values"):
                    pe.wait_ge(sem("at_wT"), m)
                    if j and h == 0:
                        pe.wait_ge(sem("at_rstd"), n - 1)
                    vt, wT, o = flat_pair(at("vt", j)), flat_pair(at("wT", h)), h * T
                    v_tile = [vt[:, (2 * h + c) * P:(2 * h + c + 1) * P] for c in range(TT)]
                    mm(pm[:, 3, o:o + P], v_tile[0], wT[:, 0:P], start=True, stop=True)
                    mm(pm[:, 3, o + P:o + T], v_tile[0], wT[:, P:2 * P], start=True, stop=False)
                    mm(pm[:, 3, o + P:o + T], v_tile[1], wT[:, 2 * P:3 * P], start=False, stop=True).then_inc(sem("at_out"), 1)
                elif name == "sums":
                    pe.wait_ge(sem("at_squares"), n)
                    mm(pm[:, 3, :], ones[:, :], flat_pair(at("sq", j)), start=True, stop=True).then_inc(sem("at_sums"), 1)
            return step

        def act_at_step(act, s, groups, scale):
            n0 = 0

            def step(name, j):
                n = n0 + j + 1
                h = int(name[-1]) if name[-1] in "01" else 0
                m = 2 * (n - 1) + h + 1
                if name == "values":
                    act.wait_ge(sem("at_values_turned"), n)
                    nc.scalar.activation(flat_pair(at("vt", j)), pm[:, 2, :], ACT.Copy).then_inc(sem("at_vt"), 1)
                elif name.startswith("exp"):
                    act.wait_ge(sem("at_max"), m)
                    sc = at_scores(h)
                    for qt in range(TT):
                        for g in range(groups):
                            c = groups * qt + g
                            e = nc.scalar.activation(sc[:, g, AT_QT[qt]], sc[:, g, AT_QT[qt]], ACT.Exp, scale=scale,
                                                     bias=at_col(h, c), accum_out=at_col(h, AT_SUM + c))
                    e.then_inc(sem("at_exp"), 1)
                elif name.startswith("wT"):
                    act.wait_ge(sem("at_turned"), m)
                    nc.scalar.activation(flat_pair(at("wT", h))[:, 0:3 * P], pm[:, 2, 0:3 * P], ACT.Copy).then_inc(sem("at_wT"), 1)
                elif name == "square":
                    act.wait_ge(sem("at_out_read"), n)
                    nc.scalar.activation(at("sq", j), mix[:, 0, 2 * j:2 * j + 2, :], ACT.Square).then_inc(sem("at_squares"), 1)
                elif name == "rstd":
                    act.wait_ge(sem("at_sums"), n)
                    r = flat_pair(at("r", j))
                    nc.scalar.activation(r, pm[:, 3, :], ACT.Ln, bias=eps[:, 0:1], scale=1.0 / P)
                    act.drain()
                    nc.scalar.activation(r, r, ACT.Exp, scale=-0.5).then_inc(sem("at_rstd"), 1)
            return step

        def dve_at_step(dve, s, groups, scale, bias, factor, second, norm_gain):
            v, n0 = nc.vector, 0

            def step(name, j):
                n = n0 + j + 1
                h = int(name[-1]) if name[-1] in "01" else 0
                m = 2 * (n - 1) + h + 1
                sc, w = at_scores(h), flat_pair(at("w", h))
                cols = w[:, 3 * P:3 * P + 12]
                if name.startswith("max"):
                    dve.wait_ge(sem("at_scores"), m)
                    for qt in range(TT):
                        b = bias[:, qt, 0:(qt + 1) * P].rearrange("p (a k) -> p a k", a=1).to_broadcast([P, groups, (qt + 1) * P])
                        e = v.scalar_tensor_tensor(sc[:, 0:groups, AT_QT[qt]], b, factor(2 * j + h), pm[:, 0:groups, AT_QT[qt]],
                                                   ALU.mult, ALU.add)
                    e.then_inc(sem("at_scores_read"), 1)
                    dve.drain()
                    for qt in range(TT):
                        v.tensor_reduce(cols[:, AT_REC + groups * qt:AT_REC + groups * (qt + 1)], sc[:, 0:groups, AT_QT[qt]],
                                        AX_X, ALU.max)
                    dve.drain()
                    v.tensor_scalar(cols[:, 0:4], cols[:, AT_REC:AT_REC + 4], -scale, None, ALU.mult).then_inc(sem("at_max"), 1)
                elif name.startswith("weights"):
                    dve.wait_ge(sem("at_exp"), m)
                    if m > 2:
                        dve.wait_ge(sem("at_turned"), m - 2)
                    v.reciprocal(cols[:, AT_REC:AT_REC + 4], cols[:, AT_SUM:AT_SUM + 4])
                    dve.drain()
                    for qt in range(TT):
                        c = AT_REC + groups * qt
                        v.tensor_scalar(w[:, AT_QT[qt]], sc[:, 0, AT_QT[qt]], cols[:, c:c + 1], None, ALU.mult)
                        v.tensor_tensor(cols[:, c + 1:c + 2], cols[:, c + 1:c + 2], second, ALU.mult)
                    dve.drain()
                    for qt in range(TT):
                        c = AT_REC + groups * qt
                        e = v.scalar_tensor_tensor(w[:, AT_QT[qt]], sc[:, 1, AT_QT[qt]], cols[:, c + 1:c + 2], w[:, AT_QT[qt]],
                                                   ALU.mult, ALU.add)
                    e.then_inc(sem("at_weights"), 1)
                elif name == "out":
                    dve.wait_ge(sem("at_out"), 2 * n)
                    v.tensor_copy(mix[:, 0, 2 * j:2 * j + 2, :], pm[:, 3, :].rearrange("p (h t) -> p h t", h=2)
                                  ).then_inc(sem("at_out_read"), 1)
                elif name == "norm":
                    dve.wait_ge(sem("at_rstd"), n)
                    o = mix[:, 0, 2 * j:2 * j + 2, :]
                    v.scalar_tensor_tensor(o, o, norm_gain, at("r", j), ALU.mult, ALU.mult).then_inc(sem("at_normed"), 1)
            return step

        DA_SCALE = 64 ** -0.5

        def act_diff(act, s, read_out, split, rstd):
            step = act_at_step(act, s, 2, DA_SCALE)

            def hook(p):
                if p == 0:
                    act.wait_ge(sem("diff_lambda_sums"), 1)
                    nc.scalar.activation(small[:, 2:4], small[:, 0:2], ACT.Exp).then_inc(sem("diff_lambda_exp"), 1)
                at_steps("act", p, step)
            read_out(s["segs"][0], s, after_first=lambda: rstd(rpre[:, :], 2 * s["n"]), hook=hook)
            at_steps("act", 3 * KD // 2, step)
            for pair in range(4):
                q = slice(2 * pair, 2 * pair + 2)
                act.wait_ge(sem("at_normed"), pair + 1)
                nc.scalar.activation(xs[:, q, 0:T], mix[:, 0, q, :], ACT.Copy).then_inc(sem("x_hi"), 1)
            read_out(s["segs"][1], s)

        def dve_diff(dve, s, read_out, split):
            v = nc.vector
            lam_init = 0.8 - 0.6 * math.exp(-0.3 * s["layer"])
            slope = [2.0 ** (-8.0 * (hd + 1) / 8) for hd in range(8)]
            step = dve_at_step(dve, s, 2, DA_SCALE, dist, lambda hd: -slope[hd] / DA_SCALE, small[:, 5:6], small[:, 6:7])

            def hook(p):
                if p == 0:
                    dve.drain()
                    dve.wait_ge(sem("rows_loaded"), 32)
                    lam = lamrow[:, :].rearrange("p (a b d) -> p a b d", a=2, b=2)
                    product = flat_pair(at("sq", 0))[:, 0:128].rearrange("p (a d) -> p a d", a=2)
                    v.tensor_tensor(product, lam[:, :, 0, :], lam[:, :, 1, :], ALU.mult)
                    dve.drain()
                    v.tensor_reduce(small[:, 0:2], product, AX_X, ALU.add).then_inc(sem("diff_lambda_sums"), 1)
                elif p == 1:
                    dve.wait_ge(sem("diff_lambda_exp"), 1)
                    v.tensor_tensor(small[:, 4:5], small[:, 3:4], small[:, 2:3], ALU.subtract)
                    v.tensor_scalar(small[:, 6:7], vec[:, 0, VEC_SUBLN:VEC_SUBLN + 1], 1.0 - lam_init, None, ALU.mult)
                    dve.drain()
                    v.tensor_scalar(small[:, 5:6], small[:, 4:5], -lam_init, None, ALU.add)
                    dve.drain()
                at_steps("dve", p, step)
            read_out(s["segs"][0], s, lambda p: at(*at_panel(p)), hook=hook)
            at_steps("dve", 3 * KD // 2, step)
            dve.drain()
            fill_lo(dve, s["fill"] + 1, mix[:, 0])
            read_out(s["segs"][1], s)

        def pe_diff(pe, s, products, last_products, out_products, first_of, keep_clock):
            step = pe_at_step(pe, s, 2)
            products(s["segs"][0], xs, first=lambda: first_of(s), hook=lambda p: at_steps("pe", p, step))
            at_steps("pe", 3 * KD // 2, step)
            out_products(s, s["fill"] + 1)

        HG_LEVELS = (16, 32, 64, 128)
        HG_GROUPS = KD // 2
        HG_G, HG_O = mix[:, 0], mix[:, 1]

        def hg_slot(n):
            return mix[:, 2 + n // 4, 2 * (n % 4):2 * (n % 4) + 2, :]

        def hg(name, j):
            twice = ("q", "k", "b", "d", "qr", "kr", 16, 32, 64, 128, "vt", "at", "across")
            once = ("f", "v", "last", "sq", "r")
            return hg_slot(2 * twice.index(name) + j % 2 if name in twice else 2 * len(twice) + once.index(name))

        def hg_flat(buf):
            return buf.rearrange("p h t -> p (h t)")

        def blocks(buf, size):
            return hg_flat(buf).rearrange("p (n e l) -> p n e l", e=2, l=size)

        def tiles(buf):
            return hg_flat(buf).rearrange("p (c t) -> p c t", t=P)

        def hg_panel(p):
            return ("fqv"[p % 3], p // 3) if p < 3 * HG_GROUPS else ("g", p - 3 * HG_GROUPS)

        def hg_dst(p):
            kind, j = hg_panel(p)
            return HG_G[:, 2 * j:2 * j + 2, :] if kind == "g" else hg(kind, j)

        HG_DELAYS = [dict(
            act=dict(sigmoid=0, log=1, exp=2, values=3, exp32=3, exp64=4, exp128=5, rects=7, across=8, square=9, rstd=10),
            dve=dict(forget=1, sums=2, operands=3, level32=4, level64=5, mask=6, level128=6, out=9, norm=11),
            pe=dict(turn=3, scores=5, rects=7, across=8, out=9, sums=10))] * (HG_GROUPS - 2) + [dict(
            act=dict(sigmoid=0, log=1, exp=2, values=3, exp32=3, exp64=4, exp128=5, rects=7, across=7, square=8, rstd=9),
            dve=dict(forget=1, sums=2, operands=3, level32=4, level64=5, mask=6, level128=6, out=8, norm=10),
            pe=dict(turn=3, scores=5, rects=7, across=7, out=8, sums=9)), dict(
            act=dict(sigmoid=0, log=1, exp=2, values=3, exp32=3, exp64=4, exp128=4, rects=5, across=6, square=7, rstd=7),
            dve=dict(forget=1, sums=2, operands=3, level32=4, level64=4, mask=5, level128=5, out=7, norm=7),
            pe=dict(turn=3, scores=5, rects=5, across=6, out=7, sums=7))]

        def hg_steps(engine, p):
            for j in range(HG_GROUPS):
                for step, d in HG_DELAYS[j][engine].items():
                    at = min(3 * j + d, 4 * HG_GROUPS)
                    if at == p:
                        yield step, j

        def act_hgrn(act, s, read_out, split, rstd):
            it, n0 = s["it"], 4 * s["it"]

            def step(name, j):
                n = n0 + j + 1
                f, b, d = hg("f", j), hg("b", j), hg("d", j)

                def exp_level(k):
                    L = HG_LEVELS[k]
                    act.wait_ge(sem("hgrn_exponents"), 5 * (n - 1) + k + 2)
                    x, e = blocks(hg(L, j), L), blocks(b, L)
                    if L == P:
                        for h in range(2):
                            nc.scalar.activation(x[:, h, 0, :], e[:, h, 0, :], ACT.Exp, scale=-1.0, bias=e[:, h, 0, L - 1:L])
                    else:
                        nc.scalar.activation(x[:, :, 0, :], hg_flat(hg("last", j))[:, 0:T].rearrange("p (n l) -> p n l", l=L),
                                             ACT.Exp)
                    nc.scalar.activation(x[:, :, 1, :], e[:, :, 1, :], ACT.Exp).then_inc(sem("hgrn_exp"), 1)

                if name == "sigmoid":
                    if s["layer"] > 0 and j == 0:
                        act.wait_ge(sem("lower_bound_shifted"), 1)
                        nc.scalar.activation(lbw[:, :, 0:4], lbw[:, :, 0:4], ACT.Exp).then_inc(sem("lower_bound_exp"), 1)
                    act.wait_ge(sem("hgrn_projected"), n)
                    nc.scalar.activation(f, f, ACT.Sigmoid).then_inc(sem("hgrn_sigmoid"), 1)
                    nc.scalar.preload_act_table_set("natural_log_exp_and_others")
                elif name == "log":
                    act.wait_ge(sem("hgrn_forget"), n)
                    nc.scalar.activation(d, f, ACT.Ln).then_inc(sem("hgrn_log"), 1)
                elif name == "exp":
                    act.wait_ge(sem("hgrn_exponents"), 5 * (n - 1) + 1)
                    nc.scalar.activation(hg("qr", j), d, ACT.Exp)
                    nc.scalar.activation(hg("kr", j), d, ACT.Exp, scale=-1.0).then_inc(sem("hgrn_exp"), 1)
                    exp_level(0)
                elif name in ("exp32", "exp64", "exp128"):
                    exp_level(HG_LEVELS.index(int(name[3:])))
                elif name == "values":
                    act.wait_ge(sem("hgrn_turned"), n)
                    nc.scalar.activation(hg_flat(hg("vt", j)), pm[:, 2, :], ACT.Copy).then_inc(sem("hgrn_turned_read"), 1)
                elif name == "rects":
                    act.wait_ge(sem("hgrn_scores"), 3 * (n - 1) + 2)
                    act.wait_ge(sem("hgrn_masked"), n)
                    at, ps = tiles(hg("at", j)), pm[:, 2, :].rearrange("p (c t) -> p c t", t=P)
                    for rows, cols in ((slice(0, 32), slice(32, 64)), (slice(64, 96), slice(96, P)), (slice(0, 64), slice(64, P))):
                        e = nc.scalar.activation(at[rows, :, cols], ps[rows, :, cols], ACT.Copy)
                    e.then_inc(sem("hgrn_copied"), 1)
                elif name == "across":
                    act.wait_ge(sem("hgrn_scores"), 3 * (n - 1) + 3)
                    nc.scalar.activation(hg_flat(hg("across", j))[:, 0:T], pm[:, 3, 0:T], ACT.Copy).then_inc(sem("hgrn_copied"), 1)
                elif name == "square":
                    act.wait_ge(sem("hgrn_out_read"), n)
                    nc.scalar.activation(hg("sq", j), HG_O[:, 2 * j:2 * j + 2, :], ACT.Square).then_inc(sem("hgrn_squares"), 1)
                elif name == "rstd":
                    act.wait_ge(sem("hgrn_sums"), n)
                    r = hg_flat(hg("r", j))
                    nc.scalar.activation(r, pm[:, 1, :], ACT.Ln, bias=eps[:, 0:1], scale=1.0 / P)
                    act.drain()
                    nc.scalar.activation(r, r, ACT.Exp, scale=-0.5).then_inc(sem("hgrn_rstd"), 1)

            read_out(s["segs"][0], s, after_first=lambda: rstd(rpre[:, :], 2 * s["n"]), hook=hg_steps_of("act", step))
            act.wait_ge(sem("hgrn_gates"), it + 1)
            nc.scalar.activation(HG_G, HG_G, ACT.Silu).then_inc(sem("hgrn_silu"), 1)
            tail = list(hg_steps("act", 4 * HG_GROUPS))
            for name, j in tail:
                if name == "square":
                    step(name, j)
            nc.scalar.preload_act_table_set("natural_log_exp_and_others")
            for pair in range(4):
                if pair == 3:
                    step("rstd", 3)
                act.wait_ge(sem("hgrn_gated"), n0 + pair + 1)
                q = slice(2 * pair, 2 * pair + 2)
                nc.scalar.activation(xs[:, q, 0:T], HG_O[:, q, :], ACT.Copy).then_inc(sem("x_hi"), 1)
            read_out(s["segs"][1], s)

        def hg_steps_of(engine, step):
            def hook(p):
                for name, j in hg_steps(engine, p):
                    step(name, j)
            return hook

        def dve_hgrn(dve, s, read_out, split):
            v = nc.vector
            it, n0 = s["it"], 4 * s["it"]

            if s["layer"] > 0:
                rows = vec[:, :, VEC_LB:VEC_LB + 4]
                v.tensor_reduce(lbw[:, :, 4:5], rows, AX_X, ALU.max)
                dve.drain()
                v.tensor_tensor(lbw[:, :, 0:4], rows, lbw[:, :, 4:5].to_broadcast([P, KD, 4]), ALU.subtract
                                ).then_inc(sem("lower_bound_shifted"), 1)

            def lower_bound():
                dve.wait_ge(sem("lower_bound_exp"), 1)
                v.tensor_reduce(lbw[:, :, 4:5], lbw[:, :, 0:4], AX_X, ALU.add)
                v.tensor_reduce(lbw[:, :, 5:6], lbw[:, :, 1:s["layer"] + 1], AX_X, ALU.add)
                dve.drain()
                v.reciprocal(lbw[:, :, 4:5], lbw[:, :, 4:5])
                dve.drain()
                v.tensor_tensor(lbw[:, :, 4:5], lbw[:, :, 4:5], lbw[:, :, 5:6], ALU.mult)
                dve.drain()
                v.tensor_scalar(lbw[:, :, 5:6], lbw[:, :, 4:5], -1.0, 1.0, ALU.mult, ALU.add)

            def step(name, j):
                n = n0 + j + 1
                f, b, d, q, k = (hg(x, j) for x in ("f", "b", "d", "q", "k"))
                heads = slice(2 * j, 2 * j + 2)

                def exponents(level):
                    L = HG_LEVELS[level]
                    e = blocks(b, L)
                    if L < P:
                        v.tensor_tensor(hg_flat(hg("last", j))[:, 0:T].rearrange("p (n l) -> p n l", l=L),
                                        e[:, :, 0, L - 1:L].to_broadcast([P, T // L, L]), e[:, :, 0, :], ALU.subtract
                                        ).then_inc(sem("hgrn_exponents"), 1)

                def level(m):
                    L = HG_LEVELS[m]
                    x = blocks(hg(L, j), L)
                    dve.wait_ge(sem("hgrn_exp"), 5 * (n - 1) + m + 2)
                    e = blocks(b, L)
                    if L < P:
                        up = v.tensor_tensor(e[:, :, 1, :], e[:, :, 1, :], e[:, :, 0, L - 1:L].to_broadcast([P, T // L, L]), ALU.add)
                        if 2 * L == P:
                            up.then_inc(sem("hgrn_exponents"), 1)
                        else:
                            dve.drain()
                            exponents(m + 1)
                    v.tensor_tensor(x[:, :, 0, :], x[:, :, 0, :], blocks(k, L)[:, :, 0, :], ALU.mult)
                    v.tensor_tensor(x[:, :, 1, :], x[:, :, 1, :], blocks(q, L)[:, :, 1, :], ALU.mult
                                    ).then_inc(sem("hgrn_operand"), 1)

                if name == "forget":
                    dve.wait_ge(sem("hgrn_sigmoid"), n)
                    if s["layer"] > 0:
                        if j == 0:
                            lower_bound()
                            dve.drain()
                        for h in range(2):
                            v.tensor_scalar(f[:, h, :], f[:, h, :], lbw[:, 2 * j + h, 5:6], lbw[:, 2 * j + h, 4:5],
                                            ALU.mult, ALU.add)
                        dve.drain()
                    v.tensor_scalar(k, f, -1.0, 1.0, ALU.mult, ALU.add).then_inc(sem("hgrn_forget"), 1)
                elif name == "sums":
                    dve.wait_ge(sem("hgrn_log"), n)
                    for h in range(2):
                        v.tensor_tensor_scan(b[:, h, :], keep[:, :], d[:, h, :], 0.0, ALU.mult, ALU.add)
                    dve.drain()
                    blk = lambda buf: hg_flat(buf).rearrange("p (n t) -> p n t", t=HGB)
                    v.tensor_tensor(blk(d), blk(b), blk(b)[:, :, HGB // 2:HGB // 2 + 1].to_broadcast([P, 2 * NB, HGB]),
                                    ALU.subtract).then_inc(sem("hgrn_exponents"), 1)
                    exponents(0)
                elif name == "operands":
                    dve.wait_ge(sem("hgrn_exp"), 5 * (n - 1) + 1)
                    v.tensor_tensor(hg("qr", j), hg("qr", j), q, ALU.mult)
                    v.tensor_tensor(hg("kr", j), hg("kr", j), k, ALU.mult).then_inc(sem("hgrn_operand"), 1)
                    level(0)
                elif name in ("level32", "level64", "level128"):
                    level(HG_LEVELS.index(int(name[5:])))
                elif name == "mask":
                    dve.wait_ge(sem("hgrn_scores"), 3 * (n - 1) + 1)
                    for m, mask in enumerate((block_causal, sibling)):
                        e = v.copy_predicated(tiles(hg("at", j)),
                                              mask[:, :].rearrange("p (a t) -> p a t", a=1).to_broadcast([P, 4, P]).bitcast(I32),
                                              pm[:, m, :].rearrange("p (c t) -> p c t", t=P))
                        dve.drain()
                    v.memset(small[:, 0:1], 0.0).then_inc(sem("hgrn_masked"), 1)
                elif name == "out":
                    dve.wait_ge(sem("hgrn_out"), n)
                    v.tensor_copy(HG_O[:, heads, :], pm[:, 3, :].rearrange("p (h t) -> p h t", h=2)
                                  ).then_inc(sem("hgrn_out_read"), 1)
                elif name == "norm":
                    dve.wait_ge(sem("hgrn_rstd"), n)
                    gn = VEC_GNORM + s["j"]
                    v.scalar_tensor_tensor(HG_O[:, heads, :], HG_O[:, heads, :], vec[:, 0, gn:gn + 1], hg("r", j),
                                           ALU.mult, ALU.mult)
                    dve.drain()

            def gated(pair):
                q = slice(2 * pair, 2 * pair + 2)
                v.tensor_tensor(HG_O[:, q, :], HG_O[:, q, :], HG_G[:, q, :], ALU.mult).then_inc(sem("hgrn_gated"), 1)

            def lo(pair):
                q = slice(2 * pair, 2 * pair + 2)
                dve.wait_ge(sem("x_hi"), 4 * s["fill"] + 5 + pair)
                v.tensor_tensor(xs[:, q, T:2 * T], HG_O[:, q, :], xs[:, q, 0:T].bitcast(F32), ALU.subtract
                                ).then_inc(sem("x_lo"), 1)

            steps_of = hg_steps_of("dve", step)

            def hook(p):
                if p == 0:
                    for j in range(2):
                        v.memset(hg("at", j), 0.0)
                steps_of(p)
            read_out(s["segs"][0], s, hg_dst, hook=hook)
            v.memset(small[:, 1:2], 0.0).then_inc(sem("hgrn_gates"), 1)
            step("out", 3)
            step("norm", 2)
            dve.wait_ge(sem("hgrn_silu"), it + 1)
            for pair in range(3):
                gated(pair)
                if pair:
                    lo(pair - 1)
            lo(2)
            step("norm", 3)
            gated(3)
            dve.drain()
            lo(3)
            read_out(s["segs"][1], s)

        def pe_hgrn(pe, s, products, last_products, out_products, first_of, keep_clock):
            mm = nc.tensor.matmul
            n0 = 4 * s["it"]

            def step(name, j):
                n = n0 + j + 1
                if name == "turn":
                    pe.wait_ge(sem("hgrn_values"), n)
                    if j >= 2:
                        pe.wait_ge(sem("hgrn_copied"), 2 * (n - 2) - 1)
                    for c in range(4):
                        e = nc.tensor.transpose(pm[:, 2, c * P:(c + 1) * P], tiles(hg("v", j))[:, c, :], ident[:, :])
                    e.then_inc(sem("hgrn_turned"), 1)
                elif name == "scores":
                    if j >= 2:
                        pe.wait_ge(sem("hgrn_rstd"), n - 2)
                    pe.wait_ge(sem("hgrn_turned_read"), n)
                    pe.wait_ge(sem("hgrn_operand"), 5 * (n - 1) + 2)
                    for bank, kk, qq in ((0, "kr", "qr"), (1, HGB, HGB)):
                        for c in range(4):
                            e = mm(pm[:, bank, c * P:(c + 1) * P], tiles(hg(kk, j))[:, c, :], tiles(hg(qq, j))[:, c, :],
                                   start=True, stop=True)
                    e.then_inc(sem("hgrn_scores"), 1)
                elif name == "rects":
                    if j:
                        pe.wait_ge(sem("hgrn_copied"), 2 * (n - 1) - 1)
                    pe.wait_ge(sem("hgrn_turned_read"), min(n + 1, n0 + 4))
                    pe.wait_ge(sem("hgrn_operand"), 5 * (n - 1) + 4)
                    for c in range(4):
                        for L, first in ((32, 0), (32, 64), (64, 0)):
                            x = tiles(hg(L, j))[:, c, :]
                            o = c * P + first
                            e = mm(pm[first:first + L, 2, o + L:o + 2 * L], x[:, first:first + L], x[:, first + L:first + 2 * L],
                                   start=True, stop=True)
                    e.then_inc(sem("hgrn_scores"), 1)
                elif name == "across":
                    if j:
                        pe.wait_ge(sem("hgrn_out_read"), n - 1)
                    pe.wait_ge(sem("hgrn_operand"), 5 * n)
                    for h in range(2):
                        x = tiles(hg(P, j))
                        e = mm(pm[:, 3, h * P:(h + 1) * P], x[:, 2 * h, :], x[:, 2 * h + 1, :], start=True, stop=True)
                    e.then_inc(sem("hgrn_scores"), 1)
                elif name == "out":
                    pe.wait_ge(sem("hgrn_copied"), 2 * n)
                    pe.wait_ge(sem("hgrn_masked"), n)
                    vt, at, ax = tiles(hg("vt", j)), tiles(hg("at", j)), tiles(hg("across", j))
                    for h in range(2):
                        mm(pm[:, 3, h * T:h * T + P], vt[:, 2 * h, :], at[:, 2 * h, :], start=True, stop=True)
                        mm(pm[:, 3, h * T + P:h * T + T], vt[:, 2 * h + 1, :], at[:, 2 * h + 1, :], start=True, stop=False)
                        e = mm(pm[:, 3, h * T + P:h * T + T], vt[:, 2 * h, :], ax[:, h, :], start=False, stop=True)
                    e.then_inc(sem("hgrn_out"), 1)
                elif name == "sums":
                    pe.wait_ge(sem("hgrn_squares"), n)
                    pe.wait_ge(sem("hgrn_masked"), min(n + 1, n0 + 4))
                    mm(pm[:, 1, :], ones[:, :], hg_flat(hg("sq", j)), start=True, stop=True).then_inc(sem("hgrn_sums"), 1)

            products(s["segs"][0], xs, first=lambda: first_of(s), hook=hg_steps_of("pe", step))
            hg_steps_of("pe", step)(4 * HG_GROUPS)
            out_products(s, s["fill"] + 1)
        FOX_SCALE = P ** -0.5
        SSM_HD = D // SSM_H
        N_ZX = (D + 1536) // PC
        H_RAW = mix[:, 2, 4:6, :]
        H_DT, H_F = mix[:, 2, 4, :], mix[:, 2, 5, :]
        H_ACS, H_CUM = mix[:, 7, 4, :], mix[:, 7, 5, :]
        H_COLS = mix[:, 7, 6, 0:64].rearrange("p (a h) -> p a h", a=4)
        H_LAST, H_DECAY = mix[:, 7, 6, 64:80], mix[:, 7, 6, 80:96]
        H_CB = flat2(mix[:, 8])[:, 0:512].rearrange("p (g t) -> p g t", g=2)
        H_BT = mix[:, 8, 2, :]
        H_OUT_DECAY = flat2(mix[:, 8])[:, 4 * T:8 * T]
        H_XD = flat2(mix[:, 2])[:, 0:D]
        H_ST = flat2(mix[:, 9])[:, 0:D]
        H_YO = flat2(mix[:, 9])[:, D:2 * D]
        H_X, H_VT = mix[:, 1], mix[:, 5]

        def seg_decay(hd):
            return mix[:, 8, 3 + hd % 2, :]

        def seg_bank(k):
            return (pm, pp)[k % 2][:, 3, 0:T]

        def seg_weight(hd):
            return mix[:, 8, 5 + hd % 2, :]

        def fox_scores(it):
            return mix[:, 9, it % 2, :]

        def fox_exp(it):
            return mix[:, 9, 2 + it % 2, :]

        def fox_weights(it):
            return mix[:, 2, 4 + it % 2, :]

        def fox_turned(it):
            return mix[:, 2, 6 + it % 2, :]

        def fox_col(it, c):
            return mix[:, 8, 2, 4 * (it % 2) + c:4 * (it % 2) + c + 1]

        def hyb_square(k):
            return mix[:, 7, k, :] if k < 4 else (gate, silu)[k // 2 - 2][:, (k % 2) * T:(k % 2) * T + T]

        def hyb_dst(p):
            if p < 2:
                return mix[:, 2, 2 * p:2 * p + 2, :]
            k = 2 * ((p - 2) % 4)
            return mix[:, 1 if p < 6 else 0, k:k + 2, :]

        HYB_PLAN = dict(
            act={0: ["exp"], 1: ["ln"], 3: ["decay"], 6: ["silu_bc"], 10: ["silu_x"], 11: ["silu_z"], 15: ["states"],
                 17: ["out_decay"]},
            dve={0: ["abs"], 1: ["quotient"], 2: ["steps"], 3: ["columns"], 4: ["conv_bc0"], 5: ["conv_bc1"], 6: ["conv_x0"],
                 7: ["conv_x1"], 8: ["conv_x2"], 9: ["conv_x3"], 10: ["masked"], 12: ["x0"], 13: ["x1"], 14: ["decayed"],
                 18: ["off"]},
            pe={3: ["columns"], 8: ["cb"], 12: ["turn_x"], 15: ["states"], 17: ["off"]})
        H_LOG1P = (mix[:, 9, 0:2, :], mix[:, 9, 2:4, :], mix[:, 9, 4:6, :], mix[:, 9, 6:8, :])

        def hyb_hook(engine, first, step):
            def hook(p):
                for name in HYB_PLAN[engine].get(first + p, []):
                    step(name)
            return hook

        def act_hyb(act, s, read_out, split, rstd):
            e_buf, w_buf, _, ln_buf = H_LOG1P

            def step(name):
                if name == "exp":
                    act.wait_ge(sem("log1p_negabs"), s["ls0"] + 1)
                    nc.scalar.activation(e_buf, e_buf, ACT.Exp).then_inc(sem("log1p_exp"), 1)
                    nc.scalar.activation(small[:, 0:1], vec[:, 0, VEC_A_LOG:VEC_A_LOG + 1], ACT.Exp).then_inc(sem("hyb_a"), 1)
                elif name == "ln":
                    act.wait_ge(sem("log1p_w"), s["ls0"] + 1)
                    nc.scalar.activation(ln_buf, w_buf, ACT.Ln).then_inc(sem("log1p_ln"), 1)
                elif name == "decay":
                    act.wait_ge(sem("hyb_decay_log"), 1)
                    nc.scalar.activation(H_DECAY, H_DECAY, ACT.Exp).then_inc(sem("hyb_decay"), 1)
                elif name == "silu_bc":
                    act.wait_ge(sem("hyb_conv"), 2)
                    nc.scalar.activation(mix[:, 7, 0:4, :], mix[:, 7, 0:4, :], ACT.Silu).then_inc(sem("hyb_silu"), 1)
                elif name == "silu_x":
                    act.wait_ge(sem("hyb_conv"), 6)
                    nc.scalar.activation(mix[:, 6], mix[:, 6], ACT.Silu).then_inc(sem("hyb_silu"), 1)
                elif name == "silu_z":
                    nc.scalar.activation(mix[:, 0], mix[:, 0], ACT.Silu).then_inc(sem("hyb_silu"), 1)
                    nc.scalar.preload_act_table_set("natural_log_exp_and_others")
                elif name == "states":
                    act.wait_ge(sem("hyb_states"), 1)
                    nc.scalar.activation(H_ST.rearrange("p (g c) -> p g c", g=2), pm[:, 2:4, :], ACT.Copy
                                         ).then_inc(sem("hyb_states_read"), 1)
                elif name == "out_decay":
                    act.wait_ge(sem("hyb_off"), 1)
                    nc.scalar.activation(H_OUT_DECAY.rearrange("p (g c) -> p g c", g=2), pm[:, 0:2, :], ACT.Exp
                                         ).then_inc(sem("hyb_decay_out"), 1)

            read_out(s["segs"][0], s, after_first=lambda: rstd(rpre[:, :], 2 * s["n"]))
            read_out(s["segs"][1], s, hook=hyb_hook("act", 0, step))
            read_out(s["segs"][2], s, hook=hyb_hook("act", N_ZX, step))
            act.wait_ge(sem("values_turned"), 4)
            for b in range(4):
                nc.scalar.activation(tok(H_VT)[:, b // 2, 512 * (b % 2):512 * (b % 2) + 512], pp[:, b, :], ACT.Copy
                                     ).then_inc(sem("values_turned_read"), 1)

            def exps(it):
                nk = (it % 2 + 1) * P
                act.wait_ge(sem("fox_max"), it + 1)
                nc.scalar.activation(fox_exp(it)[:, 0:nk], fox_scores(it)[:, 0:nk], ACT.Exp, scale=FOX_SCALE,
                                     bias=fox_col(it, 0), accum_out=fox_col(it, 1)).then_inc(sem("fox_exp"), 1)
                act.wait_ge(sem("seg_log"), it + 1)
                nc.scalar.activation(seg_decay(it), seg_decay(it), ACT.Exp).then_inc(sem("seg_exp"), 1)

            exps(0)
            for it in range(SSM_H):
                if it < SSM_H - 1:
                    exps(it + 1)
                act.wait_ge(sem("fox_weights_turned"), it + 1)
                nk = (it % 2 + 1) * P
                nc.scalar.activation(fox_turned(it)[:, 0:nk], pp[:, 2, 0:nk], ACT.Copy).then_inc(sem("fox_wT"), 1)
                if it % 2 and it > 1:
                    square_tile(act, it // 2 - 1)
            square_tile(act, KD - 1)
            act.wait_ge(sem("fox_out_read"), KD)
            nc.scalar.activation(hs[:, KD:2 * KD, 0:T], y[:, :, :], ACT.Copy).then_inc(sem("cat_hi"), 1)
            act.wait_ge(sem("hyb_sums"), 1)
            nc.scalar.activation(corr[:, 0, :], pm[:, 0, :], ACT.Ln, bias=eps[:, 0:1], scale=1.0 / 512)
            act.drain()
            nc.scalar.activation(corr[:, 0, :], corr[:, 0, :], ACT.Exp, scale=-0.5).then_inc(sem("hyb_rstd"), 1)
            for k in range(KD):
                act.wait_ge(sem("hyb_normed"), k // 4 + 1)
                e = nc.scalar.activation(hs[:, k, 0:T], mix[:, 6, k, :], ACT.Copy, scale=vec[:, k, VEC_SSM_NORM:VEC_SSM_NORM + 1])
                if k % 4 == 3:
                    e.then_inc(sem("cat_hi"), 1)
            read_out(s["segs"][3], s)

        def square_tile(act, k):
            act.wait_ge(sem("hyb_gated"), k + 1)
            nc.scalar.activation(hyb_square(k), mix[:, 6, k, :], ACT.Square).then_inc(sem("hyb_squares"), 1)

        def dve_hyb(dve, s, read_out, split):
            v = nc.vector
            e_buf, w_buf, c_buf, ln_buf = H_LOG1P
            n_log = s["ls0"] + 1

            def step(name):
                if name == "abs":
                    v.tensor_scalar(H_DT, H_DT, vec[:, 0, VEC_DT_BIAS:VEC_DT_BIAS + 1], None, ALU.add)
                    v.tensor_scalar(H_F, H_F, vec[:, 0, VEC_FOX_B:VEC_FOX_B + 1], None, ALU.add)
                    dve.drain()
                    v.scalar_tensor_tensor(e_buf, H_RAW, -1.0, H_RAW, ALU.mult, ALU.min).then_inc(sem("log1p_negabs"), 1)
                elif name == "quotient":
                    dve.wait_ge(sem("log1p_exp"), n_log)
                    log1p_quotient(dve, e_buf, w_buf, c_buf)
                elif name == "steps":
                    dve.wait_ge(sem("log1p_ln"), n_log)
                    v.tensor_tensor(ln_buf, ln_buf, c_buf, ALU.add)
                    dve.drain()
                    v.scalar_tensor_tensor(H_DT, H_DT, 0.0, ln_buf[:, 0, :], ALU.max, ALU.add)
                    v.scalar_tensor_tensor(H_F, H_F, 0.0, ln_buf[:, 1, :], ALU.min, ALU.subtract)
                    dve.wait_ge(sem("hyb_a"), 1)
                    dve.drain()
                    v.tensor_scalar(e_buf[:, 0, :], H_DT, small[:, 0:1], -1.0, ALU.mult, ALU.mult)
                    dve.drain()
                    for c in range(TT):
                        o = slice(c * P, c * P + P)
                        v.tensor_tensor_scan(H_ACS[:, o], ones[:, :], e_buf[:, 0, o], 0.0, ALU.mult, ALU.add)
                        v.tensor_tensor_scan(e_buf[:, 1, o], ones[:, :], H_F[:, o], e_buf[:, 1, P - 1:P] if c else 0.0,
                                             ALU.mult, ALU.add)
                        dve.drain()
                    v.tensor_scalar(H_CUM, e_buf[:, 1, :], -1.0 / FOX_SCALE, None, ALU.mult).then_inc(sem("hyb_scans"), 1)
                elif name == "columns":
                    dve.wait_ge(sem("hyb_cols"), 1)
                    v.tensor_copy(H_COLS, pm[:, 0, :].rearrange("p (a r) -> p a r", a=4)[:, :, 0:SSM_H])
                    v.tensor_copy(H_LAST, pm[:, 1, 0:SSM_H])
                    dve.drain()
                    v.tensor_tensor(H_DECAY, H_LAST, H_COLS[:, 2, :], ALU.subtract).then_inc(sem("hyb_decay_log"), 1)
                elif name.startswith("conv"):
                    k = 2 * int(name[-1])
                    if name.startswith("conv_bc"):
                        dve_conv(dve, mix[:, 7], mix[:, 2], (k, k + 1), VEC_SSM_CONV_BC, VEC_SSM_CONV_BBC)
                    else:
                        dve_conv(dve, mix[:, 6], mix[:, 1], (k, k + 1), VEC_SSM_CONV_X, VEC_SSM_CONV_BX)
                    v.memset(small[:, 1:2], 0.0).then_inc(sem("hyb_conv"), 1)
                elif name == "masked":
                    dve.wait_ge(sem("hyb_cb"), 1)
                    v.tensor_tensor(flat2(mix[:, 8])[:, 0:512].rearrange("p (n t) -> p n t", n=4),
                                    pm[:, 3, :].rearrange("p (n t) -> p n t", n=4),
                                    tri[:, :].rearrange("p (a t) -> p a t", a=1).to_broadcast([P, 4, P]), ALU.mult)
                    v.tensor_copy(H_BT, pm[:, 2, 0:256]).then_inc(sem("hyb_cb_read"), 1)
                elif name in ("x0", "x1"):
                    t = int(name[-1])
                    for half in range(2):
                        dve.wait_ge(sem("x_tokens"), 2 * t + half + 1)
                        v.tensor_tensor(tok(H_X)[:, t, 512 * half:512 * half + 512].rearrange("p (h d) -> p h d", h=8),
                                        pm[:, 2 * t + half, :].rearrange("p (h d) -> p h d", h=8),
                                        H_COLS[:, t, 8 * half:8 * half + 8].rearrange("p (h a) -> p h a", a=1
                                                                                      ).to_broadcast([P, 8, SSM_HD]), ALU.mult)
                elif name == "decayed":
                    dve.wait_ge(sem("hyb_decay"), 1)
                    dve.drain()
                    v.tensor_tensor(H_XD.rearrange("p (h d) -> p h d", h=SSM_H),
                                    tok(H_X)[:, 0, :].rearrange("p (h d) -> p h d", h=SSM_H),
                                    H_DECAY.rearrange("p (h a) -> p h a", a=1).to_broadcast([P, SSM_H, SSM_HD]),
                                    ALU.mult).then_inc(sem("hyb_x"), 1)
                    dve.wait_ge(sem("rows_loaded"), 32)
                    v.tensor_copy(rec_col[0:64, 5, :], skiprow[0:64, 0::2])
                    v.tensor_copy(rec_col[64:P, 5, :], skiprow[64:P, 1::2])
                elif name == "off":
                    dve.wait_ge(sem("hyb_decay_out"), 1)
                    v.tensor_tensor(H_YO.rearrange("p (g c) -> p g c", g=2), pm[:, 2:4, :],
                                    H_OUT_DECAY.rearrange("p (g c) -> p g c", g=2), ALU.mult).then_inc(sem("hyb_off_read"), 1)

            read_out(s["segs"][0], s, (H_DT, H_F))
            read_out(s["segs"][1], s, hyb_dst, hook=hyb_hook("dve", 0, step))
            read_out(s["segs"][2], s, lambda p: mix[:, 3 + p // 4, 2 * (p % 4):2 * (p % 4) + 2, :],
                     hook=hyb_hook("dve", N_ZX, step))
            v.memset(small[:, 2:3], 0.0).then_inc(sem("hyb_values"), 1)

            def maxima(it):
                nk = (it % 2 + 1) * P
                dve.wait_ge(sem("fox_scores"), it + 1)
                v.tensor_tensor(fox_scores(it)[:, 0:nk], pm[:, it % 2, 0:nk], causal[:, it % 2, 0:nk], ALU.subtract
                                ).then_inc(sem("fox_scores_read"), 1)
                dve.drain()
                v.tensor_reduce(fox_col(it, 2), fox_scores(it)[:, 0:nk], AX_X, ALU.max)
                dve.drain()
                v.tensor_scalar(fox_col(it, 0), fox_col(it, 2), -FOX_SCALE, None, ALU.mult).then_inc(sem("fox_max"), 1)

            def difference(hd):
                dve.wait_ge(sem("seg_sums"), hd + 1)
                for c in range(TT):
                    o = slice(c * P, c * P + P)
                    e = v.tensor_scalar(seg_decay(hd)[:, o], pm[:, 2, o], H_COLS[:, 2 + c, hd:hd + 1], 0.0,
                                        ALU.subtract, ALU.min)
                e.then_inc(sem("seg_log"), 1)

            def tile_out(k):
                dve.wait_ge(sem("seg_out"), 2 * k + 2)
                v.scalar_tensor_tensor(mix[:, 6, k, :], mix[:, 6, k, :], rec_col[:, 5, k:k + 1], seg_bank(k), ALU.mult, ALU.add
                                       ).then_inc(sem("seg_out_read"), 1)
                dve.drain()
                v.tensor_tensor(mix[:, 6, k, P:T], mix[:, 6, k, P:T], H_YO[:, k * P:(k + 1) * P], ALU.add)
                dve.drain()
                v.tensor_tensor(mix[:, 6, k, :], mix[:, 6, k, :], mix[:, 0, k, :], ALU.mult).then_inc(sem("hyb_gated"), 1)

            def take(hd):
                dve.wait_ge(sem("fox_out"), 2 * hd + 2)
                v.tensor_copy(y[:, hd, :], pp[:, hd % 2, 0:T]).then_inc(sem("fox_out_read"), 1)

            maxima(0)
            difference(0)
            for it in range(SSM_H):
                nk = (it % 2 + 1) * P
                if it < SSM_H - 1:
                    maxima(it + 1)
                    difference(it + 1)
                dve.wait_ge(sem("fox_exp"), it + 1)
                v.reciprocal(fox_col(it, 2), fox_col(it, 1))
                dve.drain()
                v.tensor_scalar(fox_weights(it)[:, 0:nk], fox_exp(it)[:, 0:nk], fox_col(it, 2), None, ALU.mult
                                ).then_inc(sem("fox_weights"), 1)
                dve.wait_ge(sem("seg_exp"), it + 1)
                v.tensor_tensor(seg_weight(it), seg_decay(it), H_CB[:, it // 8, :], ALU.mult).then_inc(sem("seg_weights"), 1)
                if it % 2 == 1 and it >= 3:
                    take(it // 2 - 1)
                    tile_out(it // 2 - 1)
            tile_out(KD - 1)
            take(KD - 1)
            dve.wait_ge(sem("cat_hi"), 1)
            dve.drain()
            v.tensor_tensor(hs[:, KD:2 * KD, T:2 * T], y[:, :, :], hs[:, KD:2 * KD, 0:T].bitcast(F32), ALU.subtract
                            ).then_inc(sem("cat_lo"), 1)
            dve.wait_ge(sem("hyb_rstd"), 1)
            for g in range(2):
                v.tensor_tensor(mix[:, 6, 4 * g:4 * g + 4, :], mix[:, 6, 4 * g:4 * g + 4, :],
                                corr[:, 0, g * T:g * T + T].rearrange("p (a t) -> p a t", a=1).to_broadcast([P, 4, T]), ALU.mult
                                ).then_inc(sem("hyb_normed"), 1)
            dve.drain()
            for g in range(2):
                dve.wait_ge(sem("cat_hi"), 2 + g)
                for k in range(4 * g, 4 * g + 4):
                    e = v.scalar_tensor_tensor(hs[:, k, T:2 * T], mix[:, 6, k, :], vec[:, k, VEC_SSM_NORM:VEC_SSM_NORM + 1],
                                               hs[:, k, 0:T].bitcast(F32), ALU.mult, ALU.subtract)
                e.then_inc(sem("cat_lo"), 1)
            dve.drain()
            read_out(s["segs"][3], s)

        def pe_hyb(pe, s, products, last_products, out_products, first_of, keep_clock):
            mm = nc.tensor.matmul
            B = [mix[:, 7, g, :] for g in range(2)]
            C = [mix[:, 7, 2 + g, :] for g in range(2)]
            chunk = [slice(0, P), slice(P, T)]

            def turn(src, dst, signal):
                for b in range(4):
                    t, half = b // 2, b % 2
                    for k in range(4):
                        e = nc.tensor.transpose(dst[:, b, k * P:(k + 1) * P], src[:, 4 * half + k, t * P:(t + 1) * P], ident[:, :])
                    e.then_inc(sem(signal), 1)

            def step(name):
                if name == "columns":
                    pe.wait_ge(sem("hyb_scans"), 1)
                    for n, src in enumerate((H_DT, H_DT, H_ACS, H_ACS)):
                        nc.tensor.transpose(pm[:, 0, n * P:(n + 1) * P], src[:, chunk[n % 2]], ident[:, :])
                    mm(pm[:, 1, 0:SSM_H], H_ACS[:, P - 1:P].to_broadcast([P, P]), ident[:, 0:SSM_H], start=True, stop=True
                       ).then_inc(sem("hyb_cols"), 1)
                elif name == "cb":
                    pe.wait_ge(sem("hyb_silu"), 1)
                    for g in range(2):
                        nc.tensor.transpose(pm[:, 2, g * P:(g + 1) * P], B[g][:, chunk[0]], ident[:, :])
                        for c in range(TT):
                            e = mm(pm[:, 3, (2 * g + c) * P:(2 * g + c + 1) * P], B[g][:, chunk[c]], C[g][:, chunk[c]],
                                   start=True, stop=True)
                    e.then_inc(sem("hyb_cb"), 1)
                elif name == "turn_x":
                    pe.wait_ge(sem("hyb_silu"), 2)
                    pe.wait_ge(sem("hyb_cb_read"), 1)
                    turn(mix[:, 6], pm, "x_tokens")
                elif name == "states":
                    pe.wait_ge(sem("hyb_x"), 1)
                    for g in range(2):
                        e = mm(pm[:, 2 + g, :], H_BT[:, g * P:(g + 1) * P], H_XD[:, g * 512:(g + 1) * 512], start=True, stop=True)
                    e.then_inc(sem("hyb_states"), 1)
                elif name == "off":
                    pe.wait_ge(sem("hyb_states_read"), 1)
                    for k in range(KD):
                        o = slice((k % 4) * P, (k % 4) * P + P)
                        mm(pm[:, 2 + k // 4, o], H_ST[:, k * P:(k + 1) * P], C[k // 4][:, chunk[1]], start=True, stop=True)
                        for hd in (2 * k, 2 * k + 1):
                            r = SSM_HD * (hd % 2)
                            e = mm(pm[r:r + SSM_HD, k // 4, o], ident[:, hd:hd + 1].to_broadcast([P, SSM_HD]), H_ACS[:, chunk[1]],
                                   start=True, stop=True)
                    e.then_inc(sem("hyb_off"), 1)

            products(s["segs"][0], xs, first=lambda: first_of(s))
            products(s["segs"][1], xs, hook=hyb_hook("pe", 0, step))
            products(s["segs"][2], xs, hook=hyb_hook("pe", N_ZX, step))
            pe.wait_ge(sem("hyb_values"), 1)
            turn(mix[:, 5], pp, "values_turned")
            pe.wait_ge(sem("hyb_off_read"), 1)

            def scores(it):
                hd, qt = it // 2, it % 2
                nk = (qt + 1) * P
                if it >= 2:
                    pe.wait_ge(sem("fox_scores_read"), it - 1)
                mm(pm[:, it % 2, 0:nk], mix[:, 3, hd, qt * P:(qt + 1) * P], mix[:, 4, hd, 0:nk], start=True, stop=False)
                mm(pm[:, it % 2, 0:nk], ident[:, FOX_ROW + hd:FOX_ROW + hd + 1].to_broadcast([P, P]), H_CUM[:, 0:nk],
                   start=False, stop=True).then_inc(sem("fox_scores"), 1)

            def sums_on_all(hd):
                if hd:
                    pe.wait_ge(sem("seg_log"), hd)
                mm(pm[:, 2, 0:T], ident[:, hd:hd + 1].to_broadcast([P, P]), H_ACS, start=True, stop=True
                   ).then_inc(sem("seg_sums"), 1)

            scores(0)
            sums_on_all(0)
            pe.wait_ge(sem("values_turned_read"), 4)
            for it in range(SSM_H):
                if it < SSM_H - 1:
                    scores(it + 1)
                    sums_on_all(it + 1)
                pe.wait_ge(sem("fox_weights"), it + 1)
                for k in range(it % 2 + 1):
                    e = nc.tensor.transpose(pp[:, 2, k * P:(k + 1) * P], fox_weights(it)[:, k * P:(k + 1) * P], ident[:, :])
                e.then_inc(sem("fox_weights_turned"), 1)
                pe.wait_ge(sem("seg_weights"), it + 1)
                if it >= 4 and it % 2 == 0:
                    pe.wait_ge(sem("seg_out_read"), it // 2 - 1)
                r = SSM_HD * (it % 2)
                for c in range(TT):
                    e = mm(seg_bank(it // 2)[r:r + SSM_HD, c * P:(c + 1) * P], tok(H_X)[:, c, it * SSM_HD:(it + 1) * SSM_HD],
                           seg_weight(it)[:, chunk[c]], start=True, stop=True)
                e.then_inc(sem("seg_out"), 1)
                hd, qt = it // 2, it % 2
                pe.wait_ge(sem("fox_wT"), it + 1)
                if qt == 0 and hd >= 2:
                    pe.wait_ge(sem("fox_out_read"), hd - 1)
                for k in range(qt + 1):
                    e = mm(pp[:, hd % 2, qt * P:(qt + 1) * P], tok(H_VT)[:, k, hd * P:(hd + 1) * P],
                           fox_turned(it)[:, k * P:(k + 1) * P], start=(k == 0), stop=(k == qt))
                e.then_inc(sem("fox_out"), 1)
            pe.wait_ge(sem("fox_scores_read"), SSM_H)
            for g in range(2):
                pe.wait_ge(sem("hyb_squares"), 4 * g + 4)
                for k in range(4):
                    e = mm(pm[:, 0, g * T:(g + 1) * T], ones[:, :], hyb_square(4 * g + k), start=(k == 0), stop=(k == 3))
            e.then_inc(sem("hyb_sums"), 1)
            keep_clock(16, 1)
            last_products(s, hs, x_wait=(sem("cat_lo"), 3), second_half=KD)

        ACT_MIX = {HGRN: act_hgrn, DIFF: act_diff, POOL: act_pool, HYB: act_hyb, REC: act_rec}
        DVE_MIX = {HGRN: dve_hgrn, DIFF: dve_diff, POOL: dve_pool, HYB: dve_hyb, REC: dve_rec}
        PE_MIX = {HGRN: pe_hgrn, DIFF: pe_diff, POOL: pe_pool, HYB: pe_hyb, REC: pe_rec}

        block = ctx.enter_context(nc.Block())

        @block.sync
        def _(sp):
            sp.dma_start(tok(mix[:, 1]), a["x"][0].rearrange("(a p) d -> p a d", p=P)).then_inc(sem("x_loaded"), 16)

            def load(seg, i, slot, g):
                if g is not None:
                    sp.wait_ge(sem("weights_hi"), g - 1)
                    sp.wait_ge(sem("weights_lo"), g - 1)
                sp.dma_start(raw[:, slot, 0:seg.kt * seg.width].rearrange("p (k c) -> p k c", c=seg.width),
                             seg.source(i, slot)).then_inc(sem("raw_landed_" + "AB"[slot]), 16)

            for slot in range(2):
                load(flat[0], 0, slot, None)
            rows = flat2(mix[:, 0])
            sp.wait_ge(sem("table_cleared"), 1)

            def row(r, src, n=1, c0=0, c=D):
                sp.dma_start(rows[r:r + n, c0:c0 + c], src).then_inc(sem("table_loaded"), 16)
            row(VEC_GAIN1, a["norm_gains"].rearrange("l s d -> (l s) d"), 24)
            row(VEC_GAIN2, a["norm_g_2"].rearrange("l s d -> (l s) d"), 12)
            row(VEC_LB, a["hgrn_lb_raw"], 4)
            row(VEC_POOL_SCALE, a["pool_scale"])
            row(VEC_SSM_NORM, a["ssm_norm_g_2"])
            row(VEC_REC_CONV_W, a["rec_conv_w_2"][0], 4)
            row(VEC_REC_CONV_B, a["rec_conv_b_2"])
            row(VEC_REC_BA, a["rec_b_a_2"])
            row(VEC_REC_BX, a["rec_b_x_2"])
            row(VEC_REC_LAM, a["rec_lambda_2"])
            row(VEC_SSM_CONV_X, a["ssm_conv_w_2"][0][:, 0:D], 4)
            row(VEC_SSM_CONV_BX, a["ssm_conv_b_2"][:, 0:D])
            row(VEC_SSM_CONV_BC, a["ssm_conv_w_2"][0][:, D:D + 512], 4, 0, 512)
            row(VEC_SSM_CONV_BBC, a["ssm_conv_b_2"][:, D:D + 512], 1, 0, 512)
            row(VEC_GNORM, a["hgrn_gnorm"], 2, 0, P)
            row(VEC_SUBLN, a["diff_subln"], 1, 0, P)
            row(VEC_DT_BIAS, a["ssm_dt_bias_2"], 1, 0, 16)
            row(VEC_A_LOG, a["ssm_a_log_2"], 1, 0, 16)
            row(VEC_FOX_B, a["fox_b_f_2"], 1, FOX_ROW, 8)
            sp.dma_start(lamrow[:, :], a["diff_lambda"].rearrange("o f d -> o (f d)").to_broadcast([P, 4 * 64])
                         ).then_inc(sem("rows_loaded"), 16)
            sp.dma_start(skiprow[:, :], a["ssm_d_2"].to_broadcast([P, SSM_H])).then_inc(sem("rows_loaded"), 16)

            for seg in flat:
                start = int(seg.g0 == 0)
                if seg.bodies - start == 1:
                    load(seg, start, 0, seg.g0 + 2 * start)
                    load(seg, start, 1, seg.g0 + 2 * start + 1)
                elif seg.role == "heads":
                    for i in range(start, seg.bodies):
                        for slot in range(2):
                            load(seg, i, slot, 2 * i + slot + seg.g0)
                elif seg.bodies > start:
                    with sp.Fori(start, seg.bodies) as i:
                        load(seg, i, 0, 2 * i + seg.g0)
                        load(seg, i, 1, 2 * i + (seg.g0 + 1))
            for t in range(TT):
                sp.wait_ge(sem("result_ready"), t + 1)
                sp.dma_start(out[0, t * P:(t + 1) * P, :], mix[:, 0].rearrange("p k t -> p (k t)")[:, t * D:(t + 1) * D]
                             ).then_inc(sem("result_stored"), 16)
            sp.wait_ge(sem("result_stored"), 16 * TT)

        @block.gpsimd
        def _(pool):
            pool.memset(mix[:, 0], 0.0).then_inc(sem("table_cleared"), 1)
            pool.memset(ones[:, :], 1.0)
            pool.memset(tri[:, :], 1.0)
            pool.memset(keep[:, :], 1.0)
            pool.memset(causal[:, :, :], 0.0)
            odd = sibling[:, :].rearrange("p (m e t) -> p m e t", e=2, t=HGB)
            pool.memset(odd[:, :, 0, :], 0.0)
            pool.memset(odd[:, :, 1, :], 1.0)
            pool.iota(mix[:, 2, 0:2, :].bitcast(I32), pattern=[[P, TT], [-1, T]], base=0, channel_multiplier=1)
            pool.iota(mix[:, 2, 2, 0:16].bitcast(I32), pattern=[[1, 16]], base=1, channel_multiplier=0)
            pool.memset(eps[:, :], EPS)
            pool.memset(ident[:, :], 0.0)
            pool.drain()
            pool.affine_select(out=ident[:, :], in_=ident[:, :], compare_op=ALU.not_equal, fill=1.0, base=0,
                               pattern=[[-1, P]], channel_multiplier=1)
            pool.affine_select(out=tri[:, :], in_=tri[:, :], compare_op=ALU.is_ge, fill=0.0, base=0,
                               pattern=[[1, P]], channel_multiplier=-1)
            pool.affine_select(out=causal[:, :, :], in_=causal[:, :, :], compare_op=ALU.is_ge, fill=BIG, base=0,
                               pattern=[[P, TT], [-1, T]], channel_multiplier=1)
            pool.memset(keep[:, :].rearrange("p (n t) -> p n t", t=HGB)[:, :, 0:1], 0.0)
            pool.affine_select(out=odd[:, :, 1, :], in_=odd[:, :, 1, :], compare_op=ALU.is_ge, fill=0.0, base=0,
                               pattern=[[-2 * HGB, 4], [0, HGB]], channel_multiplier=1)
            pool.drain()
            pool.affine_select(out=odd[:, :, 1, :], in_=odd[:, :, 1, :], compare_op=ALU.is_ge, fill=0.0, base=HGB - 1,
                               pattern=[[2 * HGB, 4], [0, HGB]], channel_multiplier=-1)
            pool.affine_select(out=block_causal[:, :].rearrange("p (n t) -> p n t", t=HGB),
                               in_=tri[:, :].rearrange("p (n t) -> p n t", t=HGB), compare_op=ALU.is_ge, fill=0.0, base=0,
                               pattern=[[-HGB, P // HGB], [0, HGB]], channel_multiplier=1
                               ).then_inc(sem("constants_ready"), 1)
            def add(dst, src):
                return nc.gpsimd.tensor_tensor(dst, dst, src, ALU.add)

            with pool.Fori(0, len(subs)) as n:
                pool.wait_ge(sem("squares_ready"), 5 * n + 1)
                for half in (4, 2):
                    add(sq[:, 0:half, :], sq[:, half:2 * half, :])
                    pool.drain()
                add(sq[:, 0, :], sq[:, 1, :]).then_inc(sem("squares_added"), 1)
                for pair in range(3):
                    pool.wait_ge(sem("squares_ready"), 5 * n + (2 + pair))
                    k = 2 * pair
                    e = add(sq[:, k, :], sq[:, k + 1, :])
                    if pair:
                        pool.drain()
                        e = add(sq[:, 0, :], sq[:, k, :])
                    pool.drain()
                pool.memset(pool_done[:, :], 0.0).then_inc(sem("squares_added"), 1)

        @block.scalar
        def _(act):
            def split(slot, landed, cols):
                act.wait_ge(sem("raw_landed_" + "AB"[slot]), landed)
                nc.scalar.activation(whi[:, slot, 0:cols], raw[:, slot, 0:cols], ACT.Copy).then_inc(sem("weights_hi"), 1)

            def rstd(dst, n, width=D):
                act.wait_ge(sem("squares_summed"), n + 1)
                nc.scalar.activation(rln[:, :], psum_stat, ACT.Ln, bias=eps[:, 0:1], scale=1.0 / width)
                act.drain()
                nc.scalar.activation(dst, rln[:, :], ACT.Exp, scale=-0.5).then_inc(sem("rstd_ready"), 1)

            def split_pair(n, pair):
                if pair == 0:
                    act.wait_ge(sem("raw_landed_B"), 16 * (subs[n + 1]["segs"][0].g0 // 2 + 1))
                o = slice(2 * pair * PC, (2 * pair + 2) * PC)
                nc.scalar.activation(whi[:, 1, o], raw[:, 1, o], ACT.Copy
                                     ).then_inc(sem("weights_hi" if pair == 3 else "first_b_hi"), 1)

            def open_sublayer(s):
                for pair in range(4):
                    act.wait_ge(sem("h_ready"), 4 * s["n"] + pair + 1)
                    for k in (2 * pair, 2 * pair + 1):
                        e = nc.scalar.activation(xs[:, k, 0:T], h[:, k, :], ACT.Copy, scale=vec[:, k, s["gain"]:s["gain"] + 1])
                    e.then_inc(sem("x_hi"), 1)
                nc.scalar.activation(sq, h[:, :, :], ACT.Square).then_inc(sem("squares_ready"), 1)

            def square_output(s, pair):
                out_seg = s["segs"][-1]
                act.wait_ge(sem("panel_out"), out_seg.g0 + (pair + 1) * out_seg.bodies // 2)
                nc.scalar.activation(sq[:, 2 * pair:2 * pair + 2, :], y[:, 2 * pair:2 * pair + 2, :], ACT.Square
                                     ).then_inc(sem("squares_ready"), 1)

            def scale_output(s, pair):
                g = s["gain"] + 1
                for k in (2 * pair, 2 * pair + 1):
                    e = nc.scalar.activation(upd[:, k, :], y[:, k, :], ACT.Copy, scale=vec[:, k, g:g + 1])
                e.then_inc(sem("output_scaled"), 1)

            def close_sublayer(s):
                more = s["n"] + 1 < len(subs)
                if more:
                    split_pair(s["n"], 0)
                square_output(s, 3)
                if more:
                    split_pair(s["n"], 1)
                    split_pair(s["n"], 2)
                rstd(rpost[:, :], 2 * s["n"] + 1)
                if more:
                    split_pair(s["n"], 3)
                scale_output(s, 3)

            def read_out(seg, s, after_first=None, hook=None):
                closing = seg is s["segs"][-1]
                if closing:
                    nc.scalar.preload_act_table_set("natural_log_exp_and_others")

                def body(i, nxt):
                    g = 2 * i + seg.g0
                    for slot in range(2):
                        act.wait_ge(sem("panel_done"), g + (slot + 1))
                        nc.scalar.activation(two(corr[:, slot, :]), corr_half(slot), ACT.Copy).then_inc(sem("corr_copied"), 1)
                        if closing and i == seg.bodies - 1 and slot == 1:
                            break
                        if nxt:
                            split(slot, 16 * i + 16 * (seg.g0 // 2 + 2), nxt)
                        if closing and (seg.bodies == 2 or slot == 1):
                            pair = 2 * i + slot if seg.bodies == 2 else i
                            square_output(s, pair)
                            scale_output(s, pair)
                        if slot == 0 and after_first is not None and isinstance(i, int) and i == 0:
                            after_first()
                        if seg.role == "ffn":
                            f = s["ffn"] * seg.bodies
                            if slot == 0:
                                act.wait_ge(sem("gate_ready"), i + (f + 1))
                                nc.scalar.activation(silu[:, :], gate[:, :], ACT.Silu).then_inc(sem("silu_ready"), 1)
                            else:
                                act.wait_ge(sem("hidden_ready"), i + (f + 1))
                                nc.scalar.activation(hs[:, bass.ds(2 * i, 2), 0:T], two(hid[:, :]), ACT.Copy
                                                     ).then_inc(sem("hidden_hi"), 1)
                        if hook is not None:
                            hook(2 * i + slot)
                seg_loop(act, seg, body, peel_first=after_first is not None, unroll=closing or hook is not None)

            for slot in range(2):
                split(slot, 16, flat[0].kt * flat[0].width)
            nc.scalar.preload_act_table_set("natural_log_exp_and_others")
            act.wait_ge(sem("vectors_ready"), 1)
            for s in subs:
                open_sublayer(s)
                segs = s["segs"]
                if s["kind"] == FFN:
                    read_out(segs[0], s, after_first=lambda: rstd(rpre[:, :], 2 * s["n"]))
                    read_out(segs[1], s)
                else:
                    ACT_MIX[s["kind"]](act, s, read_out, split, rstd)
                close_sublayer(s)

        @block.vector
        def _(dve):
            v = nc.vector

            def split(slot, count, cols):
                dve.wait_ge(sem("weights_hi"), count)
                v.tensor_tensor(wlo[:, slot, 0:cols], raw[:, slot, 0:cols], whi[:, slot, 0:cols].bitcast(F32),
                                ALU.subtract).then_inc(sem("weights_lo"), 1)

            def lo_pair(s, pair):
                dve.wait_ge(sem("x_hi"), 4 * s["fill"] + pair + 1)
                for k in (2 * pair, 2 * pair + 1):
                    e = v.scalar_tensor_tensor(xs[:, k, T:2 * T], h[:, k, :], vec[:, k, s["gain"]:s["gain"] + 1],
                                               xs[:, k, 0:T].bitcast(F32), ALU.mult, ALU.subtract)
                e.then_inc(sem("x_lo"), 1)

            def split_pair(n, pair):
                if pair == 3:
                    dve.wait_ge(sem("weights_hi"), subs[n + 1]["segs"][0].g0 + 2)
                else:
                    dve.wait_ge(sem("first_b_hi"), 3 * n + pair + 1)
                o = slice(2 * pair * PC, (2 * pair + 2) * PC)
                v.tensor_tensor(wlo[:, 1, o], raw[:, 1, o], whi[:, 1, o].bitcast(F32), ALU.subtract
                                ).then_inc(sem("weights_lo" if pair == 3 else "first_b_lo"), 1)

            def close_sublayer(s, nxt):
                n = s["n"]
                if nxt is not None:
                    for pair in range(3):
                        split_pair(n, pair)
                r2 = rpost[:, :].rearrange("p (a t) -> p a t", a=1).to_broadcast([P, 2, T])
                dve.wait_ge(sem("rstd_ready"), 2 * n + 2)
                for pair in range(4):
                    q = slice(2 * pair, 2 * pair + 2)
                    dve.wait_ge(sem("output_scaled"), 4 * n + pair + 1)
                    v.tensor_tensor(upd[:, q, :], upd[:, q, :], r2, ALU.mult)
                    dve.drain()
                    v.tensor_tensor(h[:, q, :], h[:, q, :], upd[:, q, :], ALU.add).then_inc(sem("h_ready"), 1)
                    if nxt is not None and pair:
                        lo_pair(nxt, pair - 1)
                if nxt is not None:
                    split_pair(n, 3)
                    dve.drain()
                    lo_pair(nxt, 3)

            def read_out(seg, s, dst=None, hook=None):
                opening, closing = seg is s["segs"][0], seg is s["segs"][-1]
                r2 = rpre[:, :].rearrange("p (a t) -> p a t", a=1).to_broadcast([P, 2, T])

                def body(i, nxt):
                    g = 2 * i + seg.g0
                    for slot in range(2):
                        t = two(tsum[:, slot, :])
                        y2 = y[:, 2 * i:2 * i + 2, :] if seg.role == "down" else None
                        if seg.role == "down" and slot == 1:
                            dve.drain()
                            dve.wait_ge(sem("corr_copied"), g + 2)
                            v.tensor_tensor(y2, y2, main_half(slot), ALU.add)
                            dve.drain()
                            v.tensor_tensor(y2, y2, two(corr[:, slot, :]), ALU.add).then_inc(sem("panel_out"), 1)
                        else:
                            to = y2 if y2 is not None else t
                            if seg.role == "out":
                                to = y[:, 4 * i + 2 * slot:4 * i + 2 * slot + 2, :]
                            dve.wait_ge(sem("corr_copied"), g + (slot + 1))
                            v.tensor_tensor(to, main_half(slot), two(corr[:, slot, :]), ALU.add).then_inc(sem("panel_out"), 1)
                        wait_rstd = opening and isinstance(i, int) and i == 0 and slot == 0
                        split_now = seg.role in ("down", "out") or wait_rstd
                        if nxt and split_now and not (closing and i == seg.bodies - 1 and slot == 1):
                            split(slot, g + (slot + 3), nxt)
                        if seg.role in ("down", "out"):
                            continue
                        dve.drain()
                        if wait_rstd:
                            dve.wait_ge(sem("rstd_ready"), 2 * s["n"] + 1)
                        if seg.role == "ffn":
                            f = s["ffn"] * seg.bodies
                            if slot == 0:
                                v.tensor_tensor(two(gate[:, :]), t, r2, ALU.mult).then_inc(sem("gate_ready"), 1)
                            else:
                                v.tensor_tensor(t, t, r2, ALU.mult)
                                dve.drain()
                                dve.wait_ge(sem("silu_ready"), i + (f + 1))
                                v.tensor_tensor(hid[:, :], tsum[:, slot, :], silu[:, :], ALU.mult
                                                ).then_inc(sem("hidden_ready"), 1)
                        elif seg.role == "small":
                            v.tensor_tensor(dst[slot], tsum[:, slot, slot * T:slot * T + T], rpre[:, :], ALU.mult)
                        elif seg.role == "heads":
                            if s["kind"] not in (HGRN, DIFF):
                                kind, pair, signal = None, 0, None
                            elif s["kind"] == HGRN:
                                (kind, pair), pairs0, turned = hg_panel(2 * i + slot), 4 * s["it"], "hgrn_turned"
                                signal = {"f": "hgrn_projected", "v": "hgrn_values"}.get(kind)
                            else:
                                (kind, pair), pairs0, turned = at_panel(2 * i + slot), 0, "at_values_turned"
                                signal = {"k": "at_keys_in", "v": "at_values_in"}.get(kind)
                            if kind == "v" and pair:
                                dve.wait_ge(sem(turned), pairs0 + pair)
                            e = v.tensor_tensor(dst(2 * i + slot), t, r2, ALU.mult)
                            if signal is not None:
                                e.then_inc(sem(signal), 1)
                        else:
                            v.tensor_tensor(dst[:, bass.ds(4 * i + 2 * slot, 2), :], t, r2, ALU.mult)
                        if nxt and not split_now:
                            split(slot, g + (slot + 3), nxt)
                        if seg.role == "ffn" and slot == 1:
                            dve.wait_ge(sem("hidden_hi"), i + (f + 1))
                            v.tensor_tensor(hs[:, bass.ds(2 * i, 2), T:2 * T], two(hid[:, :]),
                                            hs[:, bass.ds(2 * i, 2), 0:T].bitcast(F32), ALU.subtract
                                            ).then_inc(sem("hidden_lo"), 1)
                        if hook is not None:
                            hook(2 * i + slot)
                seg_loop(dve, seg, body, peel_first=opening, unroll=closing or hook is not None)
                dve.drain()

            for b in range(4):
                dve.wait_ge(sem("x_turned"), b + 1)
                v.tensor_copy(h[:, 2 * b:2 * b + 2, :], two(pp[:, b, :])).then_inc(sem("h_ready"), 1)
            for slot in range(2):
                split(slot, slot + 1, flat[0].kt * flat[0].width)
            dve.wait_ge(sem("constants_ready"), 1)
            v.tensor_copy(dist[:, :, :], mix[:, 2, 0:2, :].bitcast(I32))
            v.tensor_copy(steps[:, :], mix[:, 2, 2, 0:16].bitcast(I32))
            dve.drain()
            v.scalar_tensor_tensor(dist[:, :, :], dist[:, :, :], -1.0, dist[:, :, :], ALU.mult, ALU.max)
            dve.drain()
            for t in range(TT):
                v.memset(dist[0:64, t, t * P + 64:(t + 1) * P], BIG)
            for b in range(2):
                dve.wait_ge(sem("vectors_turned"), b + 1)
                v.tensor_copy(vec[:, 4 * b:4 * b + 4, :],
                              pm[:, b, :].rearrange("p (k r) -> p k r", r=P)[:, :, 0:NVEC])
            dve.drain()
            for g in (1, 5):
                half = vec[:, :, 0:36].rearrange("p k (l s) -> p k l s", s=6)[:, :, :, g]
                e = v.tensor_scalar(half, half, 0.5, None, ALU.mult)
            e.then_inc(sem("vectors_ready"), 1)
            dve.drain()
            for pair in range(4):
                lo_pair(subs[0], pair)
            for s, following in zip(subs, subs[1:] + [None]):
                segs = s["segs"]
                if s["kind"] == FFN:
                    read_out(segs[0], s)
                    read_out(segs[1], s)
                else:
                    DVE_MIX[s["kind"]](dve, s, read_out, split)
                close_sublayer(s, following)
            for t in range(TT):
                for half in range(2):
                    dve.wait_ge(sem("result_turned"), 2 * t + half + 1)
                    e = v.tensor_copy(mix[:, 0].rearrange("p k t -> p (k t)")[:, t * D + half * 512:t * D + half * 512 + 512],
                                      pp[:, half, :])
                e.then_inc(sem("result_ready"), 1)

        @block.tensor
        def _(pe):
            mm = nc.tensor.matmul

            def tile_product(seg, slot, ft, x, k, x_k):
                bank, c = pp[:, 2 * slot + ft, :], k * PC + ft * P
                mm(bank, whi[:, slot, c:c + P], x[:, x_k, :], start=(k == 0), stop=False)
                return mm(bank[:, 0:T], wlo[:, slot, c:c + P], x[:, x_k, 0:T], start=False, stop=(k == seg.kt - 1))

            def first_pair(seg, fill, after_x, b_in_pairs=None):
                pe.wait_ge(sem("weights_lo"), seg.g0 + (1 if b_in_pairs is not None else 2))
                if seg.g0:
                    pe.wait_ge(sem("panel_out"), seg.g0)
                for k in range(KD):
                    if k % 2 == 0:
                        pe.wait_ge(sem("x_lo"), 4 * fill + k // 2 + 1)
                        if b_in_pairs is not None and k < 6:
                            pe.wait_ge(sem("first_b_lo"), 3 * b_in_pairs + k // 2 + 1)
                        elif b_in_pairs is not None:
                            pe.wait_ge(sem("weights_lo"), seg.g0 + 2)
                    tile_product(seg, 0, 0, xs, k, k)
                    e = tile_product(seg, 0, 1, xs, k, k)
                    if k == KD - 1:
                        e.then_inc(sem("panel_done"), 1)
                    tile_product(seg, 1, 0, xs, k, k)
                for k in range(KD):
                    e = tile_product(seg, 1, 1, xs, k, k)
                e.then_inc(sem("panel_done"), 1)
                if after_x is not None:
                    after_x()

            def products(seg, x, first=None, x_wait=None, second_half=0, b_wait=None, hook=None):
                def body(i, nxt):
                    g = 2 * i + seg.g0
                    for slot in range(2):
                        pe.wait_ge(sem("weights_lo"), g + (slot + 1))
                        pe.wait_ge(sem("panel_out"), g + (slot - 1))
                        if x_wait is not None and slot == 0 and i == 0:
                            pe.wait_ge(*x_wait)
                        if b_wait is not None and slot == 1 and i == 0:
                            pe.wait_ge(*b_wait)
                        for ft in range(2):
                            for k in range(seg.kt):
                                e = tile_product(seg, slot, ft, x, k, second_half * slot + k)
                        e.then_inc(sem("panel_done"), 1)
                        if hook is not None:
                            hook(2 * i + slot)
                start = 0
                if first is not None:
                    first()
                    start = 1
                if hook is not None or x_wait is not None or seg.bodies - start <= 1:
                    for i in range(start, seg.bodies):
                        body(i, 0)
                else:
                    with pe.Fori(start, seg.bodies) as i:
                        body(i, 0)

            def column_sums(s):
                pe.wait_ge(sem("squares_added"), 2 * s["n"] + 1)
                mm(psum_stat, ones[:, :], sq[:, 0, :], start=True, stop=True).then_inc(sem("squares_summed"), 1)

            def keep_clock(n, bank=2):
                for _ in range(n):
                    mm(pm[:, bank, 0:T], ones[:, :], keep[:, :], start=True, stop=True)

            def first_of(s):
                keep_clock(11 if s["n"] else 7)
                first_pair(s["segs"][0], s["fill"], lambda: column_sums(s), s["n"] - 1 if s["n"] else None)

            def last_products(s, x, **how):
                products(s["segs"][-1], x, **how)
                pe.wait_ge(sem("squares_added"), 2 * s["n"] + 2)
                mm(psum_stat, ones[:, :], sq[:, 0, :], start=True, stop=False)
                pe.wait_ge(sem("squares_ready"), 5 * s["n"] + 5)
                mm(psum_stat, ones[:, :], sq[:, 6, :], start=False, stop=False)
                mm(psum_stat, ones[:, :], sq[:, 7, :], start=False, stop=True).then_inc(sem("squares_summed"), 1)

            def out_products(s, fill):
                last_products(s, xs, first=lambda: first_pair(s["segs"][-1], fill, None))

            pe.wait_ge(sem("constants_ready"), 1)
            pe.wait_ge(sem("x_loaded"), 16)
            xin = mix[:, 1].rearrange("p k t -> p (k t)").rearrange("p (a d) -> p a d", a=TT)
            for b in range(4):
                for k in range(2):
                    for t in range(TT):
                        f = 2 * b + k
                        e = nc.tensor.transpose(pp[:, b, k * T + t * P:k * T + t * P + P], xin[:, t, f * P:f * P + P],
                                                ident[:, :])
                e.then_inc(sem("x_turned"), 1)
            pe.wait_ge(sem("table_loaded"), 16 * N_TABLE_LOADS)
            for b in range(2):
                for k in range(4):
                    f = 4 * b + k
                    e = nc.tensor.transpose(pm[:, b, k * P:k * P + NVEC],
                                            mix[:, 0].rearrange("p k t -> p (k t)")[0:NVEC, f * P:f * P + P],
                                            ident[0:NVEC, 0:NVEC])
                e.then_inc(sem("vectors_turned"), 1)
            pe.wait_ge(sem("h_ready"), 4)
            for s in subs:
                segs = s["segs"]
                if s["kind"] == FFN:
                    products(segs[0], xs, first=lambda: first_of(s))
                    f = s["ffn"] * segs[0].bodies
                    last_products(s, hs, x_wait=(sem("hidden_lo"), f + 6), second_half=KH,
                                  b_wait=(sem("hidden_lo"), f + segs[0].bodies))
                else:
                    PE_MIX[s["kind"]](pe, s, products, last_products, out_products, first_of, keep_clock)
            pe.wait_ge(sem("h_ready"), 4 * len(subs) + 4)
            for t in range(TT):
                for half in range(2):
                    if t:
                        pe.wait_ge(sem("result_ready"), t)
                    for k in range(4):
                        e = nc.tensor.transpose(pp[:, half, k * P:k * P + P], h[:, 4 * half + k, t * P:t * P + P], ident[:, :])
                    e.then_inc(sem("result_turned"), 1)


INS = ["x", "norm_gains", "ffn1_w_in", "ffn1_w_out", "ffn2_w_in", "ffn2_w_out", "hgrn_w_in", "hgrn_gnorm",
       "hgrn_w_out", "hgrn_lb_raw", "diff_w_in", "diff_lambda", "diff_subln", "diff_w_out", "pool_w_in",
       "pool_w_group", "pool_scale", "pool_w_out", "norm_g_2", "ffn_w_in_2", "ffn_w_out_2", "hyb_w_in_2",
       "ssm_conv_w_2", "ssm_conv_b_2", "ssm_dt_bias_2", "ssm_a_log_2", "ssm_d_2", "ssm_norm_g_2", "fox_b_f_2",
       "hyb_w_out_2", "rec_w_in_2", "rec_conv_w_2", "rec_conv_b_2", "rec_w_a_2", "rec_b_a_2", "rec_w_x_2",
       "rec_b_x_2", "rec_lambda_2", "rec_w_out_2"]


def kernel(**inputs):
    import concourse.bacc as bacc
    from concourse.bass_utils import run_bass_kernel_spmd

    nc = bacc.Bacc("TRN2", target_bir_lowering=False, num_devices=1)
    arrays, aps = {}, {}
    for name in INS:
        arrays[name] = np.ascontiguousarray(inputs[name])
        aps[name] = nc.dram_tensor(name, arrays[name].shape, mybir.dt.from_np(arrays[name].dtype),
                                   kind="ExternalInput").ap()
    out = nc.dram_tensor("out", (1, T, D), F32, kind="ExternalOutput").ap()
    build(nc, aps, out)
    return run_bass_kernel_spmd(nc, [arrays], core_ids=[0]).results[0]["out"]
```
